# Optimizing a Trainium2 kernel written in Bass

```python
import jax
import jax.numpy as jnp
from jax import lax
import numpy as np
import math
import jax, jax.numpy as jnp

D_MODEL = 1024
BATCH = 1
SEQ = 256
DEPTH = 1

N_META = 16
CHUNK = 128
PAD_FRONT = CHUNK - N_META
D_MIX = D_MODEL
RET_HEADS = 4
RET_DK = D_MIX // 2 // RET_HEADS
RET_DV = D_MIX // 2 // RET_HEADS
MLSTM_HEADS = 4
MLSTM_DH = D_MIX // 2 // MLSTM_HEADS
CONV_K = 5
N_EXPERTS = 16
EC_CAPACITY = 2
D_FF = 128 * ((8 * D_MODEL // 3 + 127) // 128)
ROPE_BASE = 10000.0
EPS = 1e-6
NEG = -1e30
RET_QK = RET_HEADS * RET_DK
RET_V = RET_HEADS * RET_DV
ML_W = MLSTM_HEADS * MLSTM_DH
N_GATES = 4 * MLSTM_HEADS
PROJ_SIZES = (RET_QK, RET_QK, RET_V, RET_V, ML_W, ML_W, ML_W, ML_W, N_GATES)
PROJ_COLS = sum(PROJ_SIZES)
SPLIT_AT = tuple(int(s) for s in np.cumsum(PROJ_SIZES)[:-1])


def _rmsnorm(x, g):
    xf = x.astype(jnp.float32)
    y = xf * lax.rsqrt(jnp.mean(xf * xf, axis=-1, keepdims=True) + EPS)
    return (y * g.astype(jnp.float32)).astype(x.dtype)

def _head_norm(y, g):
    mu = jnp.mean(y, axis=-1, keepdims=True)
    yc = y - mu
    var = jnp.mean(yc * yc, axis=-1, keepdims=True)
    out = (yc * lax.rsqrt(var + EPS)).reshape(y.shape[:2] + (-1,))
    return out * g.astype(jnp.float32)

def _rotary(x, pos):
    half = x.shape[-1] // 2
    inv = ROPE_BASE ** (-jnp.arange(half, dtype=jnp.float32) / half)
    ang = pos[:, None] * inv[None, :]
    cos = jnp.cos(ang)[None, :, None, :]
    sin = jnp.sin(ang)[None, :, None, :]
    x1, x2 = x[..., :half], x[..., half:]
    return jnp.concatenate([x1 * cos - x2 * sin, x2 * cos + x1 * sin], axis=-1)

def _pad_front(t, value=0.0):
    widths = [(0, 0)] * t.ndim
    widths[1] = (PAD_FRONT, 0)
    return jnp.pad(t, widths, constant_values=value)

def _flip(t):
    return jnp.flip(t, axis=1)

def _centred_conv(u, w, b):
    c = u.shape[-1]
    out = lax.conv_general_dilated(
        u, w.astype(u.dtype)[:, None, :], window_strides=(1,),
        padding=((CONV_K // 2, CONV_K // 2),),
        dimension_numbers=('NWC', 'WIO', 'NWC'), feature_group_count=c)
    return out + b.astype(u.dtype)

def _retention_dir(q, k, v, log_gamma):
    b_, t_, h_, dk = q.shape
    dv = v.shape[-1]
    nc = t_ // CHUNK
    q = q.reshape(b_, nc, CHUNK, h_, dk)
    k = k.reshape(b_, nc, CHUNK, h_, dk)
    v = v.reshape(b_, nc, CHUNK, h_, dv)
    idx = jnp.arange(CHUNK, dtype=jnp.float32)
    diff = idx[:, None] - idx[None, :]
    decay = jnp.where(diff >= 0, jnp.exp(log_gamma[:, None, None] * jnp.maximum(diff, 0.0)), 0.0)
    scores = jnp.einsum('bclhd,bcmhd->bchlm', q, k) * decay
    intra = jnp.einsum('bchlm,bcmhe->bclhe', scores, v)
    zeta = jnp.exp(log_gamma[:, None] * (CHUNK - 1.0 - idx)[None, :])
    upd = jnp.einsum('bclhd,bclhe,hl->bchde', k, v, zeta)
    g_chunk = jnp.exp(log_gamma * CHUNK)[:, None, None]

    def step(state, u_c):
        return g_chunk * state + u_c, state

    r0 = jnp.zeros((b_, h_, dk, dv), jnp.float32)
    _, r_prev = lax.scan(step, r0, jnp.moveaxis(upd, 1, 0))
    r_prev = jnp.moveaxis(r_prev, 0, 1)
    xi = jnp.exp(log_gamma[:, None] * (idx + 1.0)[None, :])
    cross = jnp.einsum('bclhd,bchde,hl->bclhe', q, r_prev, xi)
    return (intra + cross).reshape(b_, t_, h_, dv)

def _mlstm_dir(q, k, v, log_i, log_f):
    b_, t_, h_, d = q.shape
    nc = t_ // CHUNK
    q = q.reshape(b_, nc, CHUNK, h_, d)
    k = k.reshape(b_, nc, CHUNK, h_, d)
    v = v.reshape(b_, nc, CHUNK, h_, d)
    li = jnp.moveaxis(log_i.reshape(b_, nc, CHUNK, h_), 3, 2)
    lf = jnp.moveaxis(log_f.reshape(b_, nc, CHUNK, h_), 3, 2)
    bcum = jnp.cumsum(lf, axis=-1)
    b_last = bcum[..., -1]
    causal = jnp.tril(jnp.ones((CHUNK, CHUNK), dtype=bool))
    log_d = jnp.where(causal, bcum[..., :, None] - bcum[..., None, :] + li[..., None, :], NEG)
    log_u = b_last[..., None] - bcum + li
    a = jnp.max(log_u, axis=-1)
    w_u = jnp.exp(log_u - a[..., None])
    upd_c = jnp.einsum('bchl,bclhe,bclhd->bched', w_u, v, k)
    upd_n = jnp.einsum('bchl,bclhd->bchd', w_u, k)

    def step(carry, inp):
        c_st, n_st, m_st = carry
        uc, un, bl, ac = inp
        m_new = jnp.maximum(bl + m_st, ac)
        f = jnp.exp(bl + m_st - m_new)
        g = jnp.exp(ac - m_new)
        c_new = f[..., None, None] * c_st + g[..., None, None] * uc
        n_new = f[..., None] * n_st + g[..., None] * un
        return (c_new, n_new, m_new), (c_st, n_st, m_st)

    init = (jnp.zeros((b_, h_, d, d), jnp.float32),
            jnp.zeros((b_, h_, d), jnp.float32),
            jnp.zeros((b_, h_), jnp.float32))
    xs = (jnp.moveaxis(upd_c, 1, 0), jnp.moveaxis(upd_n, 1, 0),
          jnp.moveaxis(b_last, 1, 0), jnp.moveaxis(a, 1, 0))
    _, (c_prev, n_prev, m_prev) = lax.scan(step, init, xs)
    c_prev = jnp.moveaxis(c_prev, 0, 1)
    n_prev = jnp.moveaxis(n_prev, 0, 1)
    m_prev = jnp.moveaxis(m_prev, 0, 1)
    log_inter = bcum + m_prev[..., None]
    m_row = jnp.maximum(log_inter, jnp.max(log_d, axis=-1))
    s = jnp.einsum('bclhd,bcmhd->bchlm', q, k) * jnp.exp(log_d - m_row[..., None])
    w_inter = jnp.exp(log_inter - m_row)
    num = (jnp.einsum('bchlm,bcmhe->bclhe', s, v)
           + jnp.einsum('bclhd,bched,bchl->bclhe', q, c_prev, w_inter))
    den = jnp.sum(s, axis=-1) + jnp.einsum('bclhd,bchd,bchl->bchl', q, n_prev, w_inter)
    denom = jnp.maximum(jnp.abs(den), jnp.exp(-m_row))
    h = num / jnp.moveaxis(denom, 2, 3)[..., None]
    return h.reshape(b_, t_, h_, d)

def _token_mixer(h, norm_g, w_in, b_gates, conv_w, conv_b, ret_decay_logit,
                 ret_gn_g, mlstm_gn_g, w_out):
    b_, n_, _ = h.shape
    f32 = jnp.float32
    u = _rmsnorm(h, norm_g)
    proj = jnp.einsum('bnd,dk->bnk', u, w_in)
    rq, rk, rv, rg, mq, mk, mv, mo, gate_pre = jnp.split(proj, SPLIT_AT, axis=-1)

    pos = jnp.arange(n_, dtype=f32)
    rq = _rotary(rq.reshape(b_, n_, RET_HEADS, RET_DK).astype(f32), pos) * (RET_DK ** -0.5)
    rk = _rotary(rk.reshape(b_, n_, RET_HEADS, RET_DK).astype(f32), pos)
    rv = rv.reshape(b_, n_, RET_HEADS, RET_DV).astype(f32)
    rq, rk, rv = _pad_front(rq), _pad_front(rk), _pad_front(rv)
    log_gamma = jax.nn.log_sigmoid(ret_decay_logit.astype(f32))
    ret = (_retention_dir(rq, rk, rv, log_gamma[0])
           + _flip(_retention_dir(_flip(rq), _flip(rk), _flip(rv), log_gamma[1])))
    ret = ret[:, PAD_FRONT:]
    y_ret = _head_norm(ret, ret_gn_g) * jax.nn.silu(rg.astype(f32))

    qk = jax.nn.silu(_centred_conv(jnp.concatenate([mq, mk], axis=-1), conv_w, conv_b))
    mq, mk = jnp.split(qk, 2, axis=-1)
    mq = mq.reshape(b_, n_, MLSTM_HEADS, MLSTM_DH).astype(f32) * (MLSTM_DH ** -0.5)
    mk = mk.reshape(b_, n_, MLSTM_HEADS, MLSTM_DH).astype(f32)
    mv = mv.reshape(b_, n_, MLSTM_HEADS, MLSTM_DH).astype(f32)
    gts = gate_pre.astype(f32) + b_gates.astype(f32)
    log_i = gts[..., :2 * MLSTM_HEADS].reshape(b_, n_, 2, MLSTM_HEADS)
    log_f = jax.nn.log_sigmoid(gts[..., 2 * MLSTM_HEADS:]).reshape(b_, n_, 2, MLSTM_HEADS)
    mq, mk, mv = _pad_front(mq), _pad_front(mk), _pad_front(mv)
    log_i = _pad_front(log_i, NEG)
    log_f = _pad_front(log_f, 0.0)
    h_f = _mlstm_dir(mq, mk, mv, log_i[:, :, 0], log_f[:, :, 0])
    h_b = _flip(_mlstm_dir(_flip(mq), _flip(mk), _flip(mv),
                           _flip(log_i[:, :, 1]), _flip(log_f[:, :, 1])))
    hm = (h_f + h_b)[:, PAD_FRONT:]
    hm = jax.nn.sigmoid(mo.astype(f32)).reshape(b_, n_, MLSTM_HEADS, MLSTM_DH) * hm
    y_m = _head_norm(hm, mlstm_gn_g)

    y = jnp.concatenate([y_ret, y_m], axis=-1).astype(h.dtype)
    return jnp.einsum('bnk,kd->bnd', y, w_out)

def _expert_choice_ffn(h, norm_g, w_router, w_gate, w_up, w_down):
    b_, n_, _ = h.shape
    u = _rmsnorm(h, norm_g)
    aff = jax.nn.softmax(jnp.einsum('bnd,de->bne', u, w_router).astype(jnp.float32), axis=-1)
    cap = EC_CAPACITY * n_ // N_EXPERTS
    g, idx = lax.top_k(jnp.swapaxes(aff, 1, 2), cap)
    xs = jax.vmap(lambda ub, ib: ub[ib])(u, idx)
    hid = (jax.nn.silu(jnp.einsum('becd,edf->becf', xs, w_gate))
           * jnp.einsum('becd,edf->becf', xs, w_up))
    y = jnp.einsum('becf,efd->becd', hid, w_down) * g[..., None].astype(h.dtype)
    return jnp.zeros_like(h).at[jnp.arange(b_)[:, None, None], idx].add(y)

def first_inputs(seed: int = 0) -> dict:
    key = jax.random.key(seed)
    ks = jax.random.split(key, 17)
    f32 = jnp.float32
    nrm = jax.random.normal
    x = nrm(ks[0], (BATCH, SEQ, D_MODEL), f32)
    meta_tokens = nrm(ks[1], (N_META, D_MODEL), f32)
    mix_norm_g = 1.0 + 0.05 * nrm(ks[2], (DEPTH, D_MODEL), f32)
    w_in = nrm(ks[3], (DEPTH, D_MODEL, PROJ_COLS), f32) * (D_MODEL ** -0.5)
    f_bias = jnp.tile(jnp.linspace(3.0, 6.0, MLSTM_HEADS, dtype=f32), 2)
    base_gates = jnp.concatenate([jnp.zeros((2 * MLSTM_HEADS,), f32), f_bias])
    b_gates = base_gates[None, :] + 0.1 * nrm(ks[4], (DEPTH, N_GATES), f32)
    conv_w = nrm(ks[5], (DEPTH, CONV_K, 2 * ML_W), f32) * (CONV_K ** -0.5)
    conv_b = 0.01 * nrm(ks[6], (DEPTH, 2 * ML_W), f32)
    scales = 5.0 + jnp.arange(RET_HEADS, dtype=f32)
    gamma_logit = jnp.log(2.0 ** scales - 1.0)
    ret_decay_logit = gamma_logit[None, None, :] + 0.05 * nrm(ks[7], (DEPTH, 2, RET_HEADS), f32)
    ret_gn_g = 1.0 + 0.05 * nrm(ks[8], (DEPTH, RET_V), f32)
    mlstm_gn_g = 1.0 + 0.05 * nrm(ks[9], (DEPTH, ML_W), f32)
    w_out = nrm(ks[10], (DEPTH, D_MIX, D_MODEL), f32) * (D_MIX ** -0.5)
    ffn_norm_g = 1.0 + 0.05 * nrm(ks[11], (DEPTH, D_MODEL), f32)
    w_router = nrm(ks[12], (DEPTH, D_MODEL, N_EXPERTS), f32) * (D_MODEL ** -0.5)
    w_gate = nrm(ks[13], (DEPTH, N_EXPERTS, D_MODEL, D_FF), f32) * (D_MODEL ** -0.5)
    w_up = nrm(ks[14], (DEPTH, N_EXPERTS, D_MODEL, D_FF), f32) * (D_MODEL ** -0.5)
    w_down = nrm(ks[15], (DEPTH, N_EXPERTS, D_FF, D_MODEL), f32) * (D_FF ** -0.5)
    final_norm_g = 1.0 + 0.05 * nrm(ks[16], (D_MODEL,), f32)
    return {'x': x, 'meta_tokens': meta_tokens, 'mix_norm_g': mix_norm_g, 'w_in': w_in,
            'b_gates': b_gates, 'conv_w': conv_w, 'conv_b': conv_b,
            'ret_decay_logit': ret_decay_logit, 'ret_gn_g': ret_gn_g, 'mlstm_gn_g': mlstm_gn_g,
            'w_out': w_out, 'ffn_norm_g': ffn_norm_g, 'w_router': w_router, 'w_gate': w_gate,
            'w_up': w_up, 'w_down': w_down, 'final_norm_g': final_norm_g}

def first_block(x, meta_tokens, mix_norm_g, w_in, b_gates, conv_w, conv_b, ret_decay_logit,
              ret_gn_g, mlstm_gn_g, w_out, ffn_norm_g, w_router, w_gate, w_up, w_down,
              final_norm_g):
    b_ = x.shape[0]
    meta = jnp.broadcast_to(meta_tokens.astype(x.dtype)[None], (b_, N_META, x.shape[-1]))
    h = jnp.concatenate([meta, x], axis=1)
    for l in range(DEPTH):
        h = h + _token_mixer(h, mix_norm_g[l], w_in[l], b_gates[l], conv_w[l], conv_b[l],
                             ret_decay_logit[l], ret_gn_g[l], mlstm_gn_g[l], w_out[l])
        h = h + _expert_choice_ffn(h, ffn_norm_g[l], w_router[l], w_gate[l], w_up[l], w_down[l])
    h = _rmsnorm(h, final_norm_g)
    return h[:, N_META:]


DEPTH_2 = 2

N_EVEN = (DEPTH_2 + 1) // 2
N_ODD = DEPTH_2 // 2
NEG_INF = -1e30
Q_BLOCK = 128
FOX_WIDTH = D_MODEL // 2
FOX_HEAD_DIM = 64
FOX_HEADS = FOX_WIDTH // FOX_HEAD_DIM
SC_WIDTH = D_MODEL - FOX_WIDTH
SC_GROUPS = SC_WIDTH // 64
SC_K = 3
AB_IN = 3 * FOX_WIDTH + FOX_HEADS + 3 * SC_WIDTH
LRU_WIDTH = D_MODEL
LRU_BW = 256
LRU_BLOCKS = LRU_WIDTH // LRU_BW
RG_CONV_K = 4
RG_C = 8.0
RG_MIN_RAD = 0.9
RG_MAX_RAD = 0.999
MEM_LEN = 256
MEM_HEADS = 4
MEM_HEAD_DIM = D_MODEL // MEM_HEADS
D_FF_2 = ((8 * D_MODEL // 3 + 255) // 256) * 256


def rmsnorm(x, g):
    x32 = x.astype(jnp.float32)
    y = x32 * lax.rsqrt(jnp.mean(x32 * x32, axis=-1, keepdims=True) + EPS)
    return y.astype(x.dtype) * g

def causal_depthwise_conv(x, w):
    k_width, ch = w.shape
    return lax.conv_general_dilated(
        x, w[:, None, :], window_strides=(1,), padding=[(k_width - 1, 0)],
        dimension_numbers=("NWC", "WIO", "NWC"), feature_group_count=ch)

def forgetting_attention(q, k, v, log_f):
    seq = q.shape[1]
    scale = q.shape[-1] ** -0.5
    cum = jnp.cumsum(log_f, axis=1).transpose(0, 2, 1)
    outs = []
    for blk in range(seq // Q_BLOCK):
        lo, hi = blk * Q_BLOCK, (blk + 1) * Q_BLOCK
        s = jnp.einsum("bqhd,bkhd->bhqk", q[:, lo:hi], k[:, :hi],
                       preferred_element_type=jnp.float32) * scale
        s = s + cum[:, :, lo:hi, None] - cum[:, :, None, :hi]
        causal = (lo + jnp.arange(Q_BLOCK))[:, None] >= jnp.arange(hi)[None, :]
        s = jnp.where(causal, s, NEG_INF)
        p = jax.nn.softmax(s, axis=-1).astype(v.dtype)
        outs.append(jnp.einsum("bhqk,bkhd->bqhd", p, v[:, :hi]))
    return jnp.concatenate(outs, axis=1)

def fox_shortconv_mixer(h, w_in, b_f, conv_w, w_out):
    bsz, seq, _ = h.shape
    proj = h @ w_in
    i1 = FOX_WIDTH
    i2 = 2 * FOX_WIDTH
    i3 = 3 * FOX_WIDTH
    i4 = i3 + FOX_HEADS
    i5 = i4 + SC_WIDTH
    i6 = i5 + SC_WIDTH
    q, k, v, f_logit, b_gate, c_gate, u = jnp.split(proj, [i1, i2, i3, i4, i5, i6], axis=-1)
    heads = lambda t: t.reshape(bsz, seq, FOX_HEADS, FOX_HEAD_DIM)
    log_f = jax.nn.log_sigmoid((f_logit + b_f).astype(jnp.float32))
    y_a = forgetting_attention(heads(q), heads(k), heads(v), log_f).reshape(bsz, seq, FOX_WIDTH)
    y_b = b_gate * causal_depthwise_conv(c_gate * u, conv_w)
    return jnp.concatenate([y_a, y_b], axis=-1) @ w_out

def _lru_combine(c1, c2):
    a1, b1 = c1
    a2, b2 = c2
    return a1 * a2, a2 * b1 + b2

def rglru_mixer(h, w_in, conv_w, conv_b, w_a, b_a, w_i, b_i, lam, w_out):
    bsz, seq, _ = h.shape
    gate, u = jnp.split(h @ w_in, 2, axis=-1)
    u = causal_depthwise_conv(u, conv_w) + conv_b
    ub = u.reshape(bsz, seq, LRU_BLOCKS, LRU_BW)
    r = jax.nn.sigmoid(jnp.einsum("bsnc,ncd->bsnd", ub, w_a) + b_a).reshape(bsz, seq, LRU_WIDTH)
    i = jax.nn.sigmoid(jnp.einsum("bsnc,ncd->bsnd", ub, w_i) + b_i).reshape(bsz, seq, LRU_WIDTH)
    log_a = -RG_C * r.astype(jnp.float32) * jax.nn.softplus(-lam.astype(jnp.float32))
    a = jnp.exp(log_a)
    b = jnp.sqrt(-jnp.expm1(2.0 * log_a)) * (i * u).astype(jnp.float32)
    _, hs = lax.associative_scan(_lru_combine, (a, b), axis=1)
    y = jax.nn.gelu(gate) * hs.astype(h.dtype)
    return y @ w_out

def memory_cross_attention(h, m, w_q, w_kv, w_o):
    bsz, seq, _ = h.shape
    mlen = m.shape[1]
    q = (h @ w_q).reshape(bsz, seq, MEM_HEADS, MEM_HEAD_DIM)
    k, v = jnp.split(m @ w_kv, 2, axis=-1)
    k = k.reshape(bsz, mlen, MEM_HEADS, MEM_HEAD_DIM)
    v = v.reshape(bsz, mlen, MEM_HEADS, MEM_HEAD_DIM)
    s = jnp.einsum("bqhd,bkhd->bhqk", q, k, preferred_element_type=jnp.float32) * (MEM_HEAD_DIM ** -0.5)
    p = jax.nn.softmax(s, axis=-1).astype(v.dtype)
    o = jnp.einsum("bhqk,bkhd->bqhd", p, v).reshape(bsz, seq, D_MODEL)
    return o @ w_o

def swiglu(h, w_gu, w_down):
    g, u = jnp.split(h @ w_gu, 2, axis=-1)
    return (jax.nn.silu(g) * u) @ w_down

def second_inputs(seed: int = 0) -> dict:
    key = jax.random.key(seed)
    ks = iter(jax.random.split(key, 40))
    dense = lambda shape, fan_in: jax.random.normal(next(ks), shape, jnp.float32) * (fan_in ** -0.5)
    gain = lambda shape: 1.0 + 0.02 * jax.random.normal(next(ks), shape, jnp.float32)
    small = lambda shape: 0.01 * jax.random.normal(next(ks), shape, jnp.float32)
    x = jax.random.normal(next(ks), (BATCH, SEQ, D_MODEL), jnp.float32)
    mem = jax.random.normal(next(ks), (BATCH, MEM_LEN, D_MODEL), jnp.float32)
    rad = jax.random.uniform(next(ks), (N_ODD, LRU_WIDTH), jnp.float32, RG_MIN_RAD, RG_MAX_RAD)
    c_lam = -jnp.log(jnp.expm1(-jnp.log(rad) / RG_C))
    return {
        "x": x,
        "mem": mem,
        "g_mix_pre": gain((DEPTH_2, D_MODEL)),
        "g_mix_post": gain((DEPTH_2, D_MODEL)),
        "g_cross_pre": gain((DEPTH_2, D_MODEL)),
        "g_mem": gain((DEPTH_2, D_MODEL)),
        "g_cross_post": gain((DEPTH_2, D_MODEL)),
        "g_ffn_pre": gain((DEPTH_2, D_MODEL)),
        "g_ffn_post": gain((DEPTH_2, D_MODEL)),
        "w_xq": dense((DEPTH_2, D_MODEL, D_MODEL), D_MODEL),
        "w_xkv": dense((DEPTH_2, D_MODEL, 2 * D_MODEL), D_MODEL),
        "w_xo": dense((DEPTH_2, D_MODEL, D_MODEL), D_MODEL),
        "w_ffn_gu": dense((DEPTH_2, D_MODEL, 2 * D_FF_2), D_MODEL),
        "w_ffn_down": dense((DEPTH_2, D_FF_2, D_MODEL), D_FF_2),
        "ab_w_in": dense((N_EVEN, D_MODEL, AB_IN), D_MODEL),
        "ab_b_f": jax.random.uniform(next(ks), (N_EVEN, FOX_HEADS), jnp.float32, 2.0, 5.0),
        "ab_conv_w": dense((N_EVEN, SC_K, SC_WIDTH), SC_K),
        "ab_w_out": dense((N_EVEN, D_MODEL, D_MODEL), D_MODEL),
        "c_w_in": dense((N_ODD, D_MODEL, 2 * LRU_WIDTH), D_MODEL),
        "c_conv_w": dense((N_ODD, RG_CONV_K, LRU_WIDTH), RG_CONV_K),
        "c_conv_b": small((N_ODD, LRU_WIDTH)),
        "c_w_a": dense((N_ODD, LRU_BLOCKS, LRU_BW, LRU_BW), LRU_BW),
        "c_b_a": small((N_ODD, LRU_BLOCKS, LRU_BW)),
        "c_w_i": dense((N_ODD, LRU_BLOCKS, LRU_BW, LRU_BW), LRU_BW),
        "c_b_i": small((N_ODD, LRU_BLOCKS, LRU_BW)),
        "c_lam": c_lam,
        "c_w_out": dense((N_ODD, LRU_WIDTH, D_MODEL), LRU_WIDTH),
    }

def second_block(x, mem, g_mix_pre, g_mix_post, g_cross_pre, g_mem, g_cross_post,
              g_ffn_pre, g_ffn_post, w_xq, w_xkv, w_xo, w_ffn_gu, w_ffn_down,
              ab_w_in, ab_b_f, ab_conv_w, ab_w_out,
              c_w_in, c_conv_w, c_conv_b, c_w_a, c_b_a, c_w_i, c_b_i, c_lam, c_w_out):
    for layer in range(DEPTH_2):
        h = rmsnorm(x, g_mix_pre[layer])
        if layer % 2 == 0:
            e = layer // 2
            y = fox_shortconv_mixer(h, ab_w_in[e], ab_b_f[e], ab_conv_w[e], ab_w_out[e])
        else:
            o = layer // 2
            y = rglru_mixer(h, c_w_in[o], c_conv_w[o], c_conv_b[o], c_w_a[o], c_b_a[o],
                            c_w_i[o], c_b_i[o], c_lam[o], c_w_out[o])
        x = x + rmsnorm(y, g_mix_post[layer])
        h = rmsnorm(x, g_cross_pre[layer])
        m = rmsnorm(mem, g_mem[layer])
        y = memory_cross_attention(h, m, w_xq[layer], w_xkv[layer], w_xo[layer])
        x = x + rmsnorm(y, g_cross_post[layer])
        h = rmsnorm(x, g_ffn_pre[layer])
        y = swiglu(h, w_ffn_gu[layer], w_ffn_down[layer])
        x = x + rmsnorm(y, g_ffn_post[layer])
    return x


def setup_inputs(seed=0):
    out = dict(first_inputs(seed))
    for name, value in second_inputs(seed + 1).items():
        if name != "x":
            out[name + "_2"] = value
    return out


def reference(
    x, meta_tokens, mix_norm_g, w_in, b_gates, conv_w, conv_b, ret_decay_logit, ret_gn_g,
    mlstm_gn_g, w_out, ffn_norm_g, w_router, w_gate, w_up, w_down, final_norm_g, mem_2,
    g_mix_pre_2, g_mix_post_2, g_cross_pre_2, g_mem_2, g_cross_post_2, g_ffn_pre_2,
    g_ffn_post_2, w_xq_2, w_xkv_2, w_xo_2, w_ffn_gu_2, w_ffn_down_2, ab_w_in_2, ab_b_f_2,
    ab_conv_w_2, ab_w_out_2, c_w_in_2, c_conv_w_2, c_conv_b_2, c_w_a_2, c_b_a_2, c_w_i_2,
    c_b_i_2, c_lam_2, c_w_out_2,
):
    x = first_block(
        x, meta_tokens, mix_norm_g, w_in, b_gates, conv_w, conv_b, ret_decay_logit, ret_gn_g,
        mlstm_gn_g, w_out, ffn_norm_g, w_router, w_gate, w_up, w_down, final_norm_g,
    )
    return second_block(
        x, mem_2, g_mix_pre_2, g_mix_post_2, g_cross_pre_2, g_mem_2, g_cross_post_2,
        g_ffn_pre_2, g_ffn_post_2, w_xq_2, w_xkv_2, w_xo_2, w_ffn_gu_2, w_ffn_down_2, ab_w_in_2,
        ab_b_f_2, ab_conv_w_2, ab_w_out_2, c_w_in_2, c_conv_w_2, c_conv_b_2, c_w_a_2, c_b_a_2,
        c_w_i_2, c_b_i_2, c_lam_2, c_w_out_2,
    )


_drawn_inputs = setup_inputs


def setup_inputs(seed=0):
    import zlib

    import numpy as np

    out = dict(_drawn_inputs(seed))
    spreads = {}
    factors = {'conv_b': 4.062,
     'g_mix_post_2': 2.719,
     'g_cross_pre_2': 3.533,
     'g_cross_post_2': 3.046,
     'g_ffn_pre_2': 2.792,
     'g_ffn_post_2': 4.259,
     'c_conv_b_2': 4.679,
     'c_b_a_2': 60.135,
     'c_b_i_2': 23.503}
    for name, (base, spread) in spreads.items():
        noise = np.random.default_rng([zlib.crc32(name.encode()), seed]).standard_normal(out[name].shape)
        drawn = base * np.exp(spread * noise) if base else spread * noise
        out[name] = jnp.asarray(drawn.astype(out[name].dtype))
    for name, factor in factors.items():
        out[name] = (out[name] * factor).astype(out[name].dtype)
    return out
```

```python
from contextlib import ExitStack

import numpy as np

import concourse.bass as bass
from concourse import mybir

P = 128
F32 = mybir.dt.float32
F32R = mybir.dt.float32r
U32 = mybir.dt.uint32
ALU = mybir.AluOpType
ACT = mybir.ActivationFunctionType
AX = mybir.AxisListType

D = 1024
KT = D // P
SEQ = 256
META = 16
T = META + SEQ
TT = (T + P - 1) // P
ROWS = [min(P, T - P * i) for i in range(TT)]
H = 4
EXP = 16
CAP = 2 * T // EXP
DFF = 2816
FT = DFF // P
EPS = 1e-6
ARENA = 24960
BIG = 1e30
PAD = 2

SLOTS = 11
SLOT = KT * 256
CSLOTS = 4
PSLOTS = 3
ESLOTS = 8
DOWN_END = [-(-DFF * (g + 1) // D) for g in range(ESLOTS)]
DOWN_SLOT = [(D * (j + 1) - 1) // DFF for j in range(FT)]
HF = FT // 2
HP = 46
HCHUNKS = [(p, min(P, p + HP)) for p in range(0, P, HP)]
MPAD = 64

VEC_ROWS = [
    [("mix_norm_g", 8), ("ffn_norm_g", 8), ("final_norm_g", 8), ("conv_w", 40), ("conv_b", 8),
     ("ret_gn_g", 4), ("mlstm_gn_g", 4), ("g_mem_2", 16), ("g_mix_pre_2", 16), ("g_mix_post_2", 16)],
    [("g_cross_pre_2", 16), ("g_cross_post_2", 16), ("g_ffn_pre_2", 16), ("g_ffn_post_2", 16),
     ("ab_conv_w_2", 12), ("c_conv_w_2", 32), ("c_conv_b_2", 8), ("c_lam_2", 8)],
    [("c_b_a_2", 8), ("c_b_i_2", 8)],
]
VEC_AT = {}
for _tile, _rows in enumerate(VEC_ROWS):
    _at = 0
    for _name, _n in _rows:
        VEC_AT[_name] = (_tile, _at, _n)
        _at += _n
VEC_COUNT = [sum(n for _, n in rows) for rows in VEC_ROWS]


def constants():
    p = np.arange(P)[:, None]
    f = np.float32
    c = {}
    c["ident"] = np.eye(P, dtype=f)
    col = np.arange(256 + T)[None, :] - 256
    c["dist_fwd"] = np.maximum(col - p, 0).astype(f)
    c["dist_bwd"] = np.maximum(p - col, 0).astype(f)
    c["bar_fwd"] = np.where(np.arange(T)[None, :] >= p, 0, BIG).astype(f)
    c["bar_bwd"] = np.where(np.arange(384)[None, :] - 256 <= p, 0, BIG).astype(f)
    half = 64
    inv = 10000.0 ** (-np.arange(half, dtype=f) / half)
    ang = (np.arange(T, dtype=f)[:, None] * inv[None, :].astype(f)).astype(f)
    c["cos"] = np.concatenate([np.cos(ang).T, np.cos(ang).T], 0).astype(f)
    c["sin"] = np.concatenate([np.sin(ang).T, np.sin(ang).T], 0).astype(f)
    rot = np.zeros((P, P), f)
    rot[np.arange(64) + 64, np.arange(64)] = -1
    rot[np.arange(64), np.arange(64) + 64] = 1
    c["rot"] = rot
    pick = np.zeros((8, 8, P), f)
    for r in range(8):
        pick[r, r, :] = 1
    c["pick"] = pick.reshape(8, 8 * P)
    into = np.zeros((P, 8, 8), f)
    for r in range(8):
        into[:, r, r] = 1
    c["into"] = into.reshape(P, 64)
    c["iota_row"] = np.tile(np.arange(T, dtype=f), (P, 1))
    c["iota_col"] = np.arange(P, dtype=f)[:, None] + 128 * np.arange(TT, dtype=f)[None, :]
    own = np.zeros((EXP, EXP, CAP), f)
    for r in range(EXP):
        own[r, r] = 1
    c["own"] = own.reshape(EXP, EXP * CAP)
    c["dirs"] = np.stack([np.arange(8) < 4, np.arange(8) >= 4], 1).astype(f)
    bar = np.zeros((P, 2, 256), f)
    for i in range(2):
        bar[:, i] = np.where(np.arange(256)[None, :] <= p + 128 * i, 0, -BIG)
    c["bar_causal"] = bar.reshape(P, 512)
    return c


def build(nc, t, out):
    with ExitStack() as ctx:
        BASE = {}

        def sb(name, cols, dt=F32):
            made = ctx.enter_context(nc.sbuf_tensor(name, [P, cols], dt))
            BASE[name] = nc.sbuf_base - 4 * cols
            return made

        sems = {}

        def S(name):
            if name not in sems:
                sems[name] = ctx.enter_context(nc.semaphore(name))
            return sems[name]

        bank = [ctx.enter_context(nc.psum_tensor(f"bank{i}", [P, 512], F32)) for i in range(8)]

        W = sb("weight_ring", SLOTS * SLOT)
        ident = sb("ident", P)
        ones = sb("ones", P)
        hT = sb("hT", KT * T)
        SQ = sb("squares", KT * T)
        RSTD = sb("rstd", T)
        VC = sb("vec_cols", 384)
        GW = sb("gate_w", KT * 16)
        RW = sb("router_w", KT * 16)
        small = sb("small", 192)
        Z = sb("arena", ARENA)

        def rounded(name, over, at, cols):
            offset = BASE[over] + 4 * at
            return nc.alloc_sbuf_tensor_at(name, [P, cols], F32R, offset=offset)[:]

        def vec(name, i):
            tile, at, n = VEC_AT[name]
            return VC[:, tile * P + at + i:tile * P + at + i + 1]

        cursor = [0]

        def z(cols, at=None):
            if at is None:
                at = cursor[0]
                cursor[0] += cols
            assert at + cols <= ARENA, (at, cols)
            return Z[:, at:at + cols]

        def tiles(ap, n):
            return ap.rearrange("p (t n) -> p t n", t=n)

        lg = small[:, 0:8]
        lgt = small[:, 8:24]
        b_i, b_f = small[0:8, 24:25], small[0:8, 25:26]
        dirs = small[0:8, 26:28]
        acol = small[:, 32:56]
        iota_col = small[:, 56:59]
        idxT = small[:, 64:80]
        gT = small[:, 80:96]
        smax = small[:, 96:104]
        ssum = small[:, 104:112]
        b_fox = small[0:8, 112:113]
        half_a, half_i = small[:, 120:128], small[:, 128:136]
        n2sp = small[:, 136:144]
        lamt = small[:, 144:160]
        eps = small[:, 184:185]

        uT = z(KT * T)
        QKP = z(8 * (T + 2 * PAD))
        NUM = QKP[:, 0:8 * T]
        QK = z(8 * T)
        mvT, moT, rqT, rkT, rvT, rgT = (z(H * T) for _ in range(6))
        mv, rv = z(TT * 512), z(TT * 512)
        xtok = Z[:, cursor[0] - 2 * TT * 512:cursor[0]]
        DEC = z(H * TT * T)
        dist_fwd, dist_bwd = z(256 + T), z(256 + T)
        bar_fwd, bar_bwd = z(T), z(384)
        cosT, sinT = z(T), z(T)
        pick = z(8 * P)
        rot = z(P)
        into = z(64)
        rows = [z(T) for _ in range(7)]
        assert cursor[0] <= ARENA, cursor[0]
        vrow = QKP[:, 0:384]
        li, lf, Bf, Bb, rowt, sf, Mr = rows
        zrow = Mr
        HM = mvT
        RET = rvT

        kT2 = z(2 * KT * 256, 0)
        v2 = z(2 * 2 * D, 4096)
        mm = z(2 * KT * 256, 8192)
        mwork = z(KT * 256, 12288)
        kvw = z(KT * 256, 14336)
        utok = z(TT * D, 16384)
        ST = z(TT * (EXP + 1) * CAP, 19456)
        STe = z(TT * CAP, 21192)
        xs = z(KT * MPAD, 21296)
        th = z(P * HF, 21808)
        hidT = z(P * HF, 23216)
        iota_row = z(T, 24624)
        aff = z(TT * EXP, 24896)
        u2 = uT
        memtok = z(2 * D, 4096)
        mT = z(KT * 256, 6144)
        o = 21808
        affT, affW, vals, idxs, own, spread, idx2, val2 = (
            z(n, o + at) for n, at in ((T, 0), (T, 272), (40, 544), (40, 584), (544, 624), (544, 1168), (P, 1712), (P, 1840)))
        ys = SQ[:, 0:512]
        Se = SQ[:, 512:512 + T]

        xT = z(2048, 8192)
        hN = z(2048, 10240)
        yT = z(2048, 12288)
        work = [14336]

        def cz(cols):
            at = work[0]
            work[0] += cols
            return z(cols, at)

        fq, fk, fv, fb, fc, fu = (cz(1024) for _ in range(6))
        cu = cz(4 * 258)
        fox_e = [cz(512), cz(512)]
        fox_nm = SQ[:, 0:512]
        fox_pt = [cz(512), cz(512)]
        fox_bar = SQ[:, 1280:1792]
        frow, frow2, frow3 = SQ[:, 512:768], SQ[:, 768:1024], SQ[:, 1024:1280]
        fpick = cz(8 * P)
        work[0] = 14336
        lgate, lu, ta, ti = cz(2048), cz(2048), cz(2048), cz(2048)
        lup = cz(8 * 259)
        lr = hN
        work[0] = 14336
        xq, xo = cz(2048), cz(2048)
        att_e = [cz(512), cz(512)]
        att_pt = [cz(512), cz(512)]
        work[0] = 14336
        work[0] = 12288
        cz(2 * FT * 256)
        fhid_high = rounded("hidden_high", "arena", 12288, FT * 256)
        fhid_low = rounded("hidden_low", "arena", 12288 + FT * 256, FT * 256)
        fth = [cz(512), cz(512)]

        A_CHUNKS = [("w_in", c) for c in (8, 9, 10, 11, 12, 13, 0, 1, 2, 3, 4, 5, 14, 15, 6, 7)]
        A_CHUNKS += [("w_out", c) for c in range(4)]
        NA = len(A_CHUNKS)

        C_CHUNKS = []
        for L in range(2):
            if L == 0:
                C_CHUNKS += [("ab", c) for c in range(12)]
                C_CHUNKS += [("ab_out", c) for c in range(4)]
            else:
                C_CHUNKS += [("c_in", c) for c in (4, 5, 6, 7, 0, 1, 2, 3)] + [("c_a", 0), ("c_i", 0)]
                C_CHUNKS += [("c_out", c) for c in range(4)]
            C_CHUNKS += [(f"xq{L}", c) for c in range(4)] + [(f"xo{L}", c) for c in range(4)]
            for c in range(FT // 2):
                C_CHUNKS += [(f"gate{L}", c), (f"up{L}", c)]
            C_CHUNKS += [(f"down{L}", c) for c in range(FT // 2)]
        A_USES = [len([k for k in range(NA) if k % SLOTS == s]) for s in range(SLOTS)]
        B_USES = [3 * EXP if s < ESLOTS else 0 for s in range(SLOTS)]

        def landed(s):
            return S(f"ring_landed{s}")

        class Projections:

            def __init__(self):
                self.entries = []
                self.taken = {"act": 0, "dve": 0}
                self.last = {}

            def add(self, bank_no, taker):
                before = self.last.get(bank_no)
                self.entries.append((bank_no, taker, before))
                self.taken[taker] += 1
                self.last[bank_no] = (taker, self.taken[taker])
                return len(self.entries) - 1

        pj = Projections()
        A_FIRST = [pj.add(k % 2, "act") for k in range(32)]
        A_OUT = [pj.add(k % 2, "dve") for k in range(8)]

        if True:
            C = {}
            for L in range(2):
                if L == 0:
                    for k in range(12):
                        C["ab", k] = pj.add(k % 4, "act")
                    for k in range(4):
                        C["mix_out", 0, k] = pj.add(k % 4, "act")
                else:
                    for k in range(8):
                        C["c_in", k] = pj.add(k % 4, "act")
                    for k in range(8):
                        C["c_gates", k] = pj.add(k % 4, "act")
                    for k in range(4):
                        C["mix_out", 1, k] = pj.add(k % 4, "act")
                for k in range(4):
                    C["xq", L, k] = pj.add(k % 4, "act")
                for k in range(4):
                    C["xo", L, k] = pj.add(k % 4, "act")
                for k in range(FT // 2):
                    C["gate", L, k] = pj.add((2 * k) % 4, "dve")
                    C["up", L, k] = pj.add((2 * k + 1) % 4, "dve")
                for k in range(4):
                    C["down", L, k] = pj.add(k, "act")

        chunk_used = []
        for name, c in C_CHUNKS:
            L = int(name[-1]) if name[-1].isdigit() else None
            if name == "ab":
                entry = C["ab", c]
            elif name in ("ab_out", "c_out"):
                entry = C["mix_out", 0 if name == "ab_out" else 1, c]
            elif name == "c_in":
                entry = C["c_in", (c + 4) % 8]
            elif name in ("c_a", "c_i"):
                entry = C["c_gates", 3 if name == "c_a" else 7]
            elif name[:-1] == "down" and c < FT // 2 - 1:
                chunk_used.append((S("ffn_down_used"), L * (FT // 2 - 1) + c + 1))
                continue
            elif name[:-1] == "down":
                entry = C["down", L, 3]
            else:
                entry = C[name[:-1], L, c]
            chunk_used.append((S("proj_ready"), entry + 1))
        c_index = {key: k for k, key in enumerate(C_CHUNKS)}

        split_chunks = [k for k, (name, c) in enumerate(C_CHUNKS)
                        if name[:-1] in ("up", "down") or (name[:-1] == "gate" and c > 0)]
        split_index = {k: n for n, k in enumerate(split_chunks)}
        POOL_TILES = 5

        def raw_slot(k):
            return W[:, (k % CSLOTS) * SLOT:(k % CSLOTS + 1) * SLOT]

        highs = rounded("weights_high_ring", "weight_ring", CSLOTS * SLOT, PSLOTS * SLOT)
        lows = rounded("weights_low_ring", "weight_ring", (CSLOTS + PSLOTS) * SLOT, PSLOTS * SLOT)
        x_high = rounded("input_high", "weight_ring", (CSLOTS + 2 * PSLOTS) * SLOT, SLOT)
        x_low = rounded("input_low", "squares", 0, SLOT)

        def part(ring, n):
            return ring[:, (n % PSLOTS) * SLOT:(n % PSLOTS + 1) * SLOT]

        def chunk_landed(eng, key):
            k = c_index[key]
            s = k % CSLOTS
            eng.wait_ge(landed(s), 16 * (A_USES[s] + B_USES[s] + k // CSLOTS + 1))
            return s

        def taken_after(who, k):
            return sum(1 for e in pj.entries[:k + 1] if e[1] == who)

        def pe_bank_free(pe, k):
            before = pj.entries[k][2]
            if before:
                pe.wait_ge(S(f"proj_taken_{before[0]}"), before[1])

        def proj_ready(eng, k):
            eng.wait_ge(S("proj_ready"), k + 1)

        def norm_n(n):
            return n

        MLSTM_C = 0.25 * float(P) ** -0.5

        block = ctx.enter_context(nc.Block())

        @block.sync
        def _(sp):
            x, meta = t["x"][0], t["meta_tokens"]
            xt = tiles(xtok, TT)
            sp.dma_start(xt[0:META, 0, :], meta).then_inc(S("x_landed"), 16)
            sp.dma_start(xt[META:P, 0, :], x[0:P - META, :]).then_inc(S("x_landed"), 16)
            sp.dma_start(xt[:, 1, :], x[P - META:2 * P - META, :]).then_inc(S("x_landed"), 16)
            sp.dma_start(xt[0:META, 2, :], x[2 * P - META:SEQ, :]).then_inc(S("x_landed"), 16)
            w_in = t["w_in"][0].rearrange("(t p) n -> p t n", p=P)
            w_out = t["w_out"][0].rearrange("(t p) n -> p t n", p=P)
            sp.dma_start(tiles(GW[:], KT), w_in[:, :, 4096:4112]).then_inc(S("gate_w_landed"), 16)
            for tile, group in enumerate(VEC_ROWS):
                for name, n in group:
                    at = VEC_AT[name][1]
                    src = t[name]
                    flat = src.rearrange(" ".join("abc"[:len(src.shape)]) + " -> (" + " ".join("abc"[:len(src.shape)]) + ")") \
                        if len(src.shape) > 1 else src
                    sp.dma_start(vrow[at:at + n, tile * P:(tile + 1) * P],
                                   flat.rearrange("(r f) -> r f", f=P)).then_inc(S("vec_landed"), 16)
            sp.wait_ge(S("vec_landed"), 16 * sum(len(g) for g in VEC_ROWS))
            for k, (name, c) in enumerate(A_CHUNKS):
                if k >= SLOTS:
                    sp.wait_ge(S("proj_ready"), 2 * (k - SLOTS + 1))
                src = w_in if name == "w_in" else w_out
                sp.dma_start(tiles(W[:, (k % SLOTS) * SLOT:(k % SLOTS + 1) * SLOT], KT),
                             src[:, :, 256 * c:256 * c + 256]).then_inc(landed(k % SLOTS), 16)
            sp.dma_start(tiles(RW[:], KT), t["w_router"][0].rearrange("(t p) n -> p t n", p=P))\
              .then_inc(S("router_w_landed"), 16)

            sp.wait_ge(S("gates_ready"), 2)
            sp.dma_start(tiles(GW[:, 0:64], KT), t["ab_w_in_2"][0].rearrange("(t p) n -> p t n", p=P)[:, :, 1536:1544])\
              .then_inc(S("fox_w_landed"), 16)

            def expert_slot(s):
                return W[:, s * DFF:(s + 1) * DFF]

            mem = t["mem_2"][0].rearrange("(i p) n -> p i n", p=P)
            def last_a_use(s):
                lo, hi = s * DFF // SLOT, ((s + 1) * DFF - 1) // SLOT
                return max(max(k for k in range(NA) if k % SLOTS == a) for a in range(lo, min(hi, SLOTS - 1) + 1)) + 1

            def gate_load(e, s):
                src = t["w_gate"][0][bass.ds(e, 1)].rearrange("a (t p) n -> t p (a n)", p=P)
                sp.dma_start(expert_slot(s), src[s]).then_inc(landed(s), 16)

            def up_load(e, s):
                src = t["w_up"][0][bass.ds(e, 1)].rearrange("a (t p) n -> t p (a n)", p=P)
                sp.dma_start(expert_slot(s), src[s]).then_inc(landed(s), 16)

            def down_load(e, s):
                src = t["w_down"][0][bass.ds(e, 1)].rearrange("a (p j) n -> p (a j n)", p=P)
                sp.dma_start(expert_slot(s), src[:, s * DFF:(s + 1) * DFF]).then_inc(landed(s), 16)

            def kv_load(e):
                L, c = e // 8, e % 8
                for half in range(2):
                    src = t["w_xkv_2"].rearrange("l (t p) (h c n) -> p l h c t n", p=P, h=2, n=P)
                    src = src[:, bass.ds(L, 1), half, bass.ds(c, 1)]
                    sp.dma_start(tiles(kvw[:], KT)[:, :, half * P:(half + 1) * P],
                                 src.rearrange("p l c t n -> p (l c t) n")).then_inc(S("kv_landed"), 16)

            def rest_of_expert(e):
                for s in range(ESLOTS):
                    sp.wait_ge(S("gate_used"), 8 * e + s + 1)
                    up_load(e, s)
                for s in range(ESLOTS):
                    sp.wait_ge(S("up_used"), 8 * e + s + 1)
                    down_load(e, s)

            for s in range(ESLOTS):
                sp.wait_ge(S("proj_ready"), 2 * last_a_use(s))
                gate_load(0, s)
            sp.wait_ge(S("proj_ready"), 2 * NA)
            sp.dma_start(tiles(memtok, 2), mem).then_inc(S("mem_landed"), 16)
            kv_load(0)
            rest_of_expert(0)
            with sp.Fori(1, EXP) as e:
                for s in range(ESLOTS):
                    sp.wait_ge(S("down_used"), 8 * e - 8 + s + 1)
                    gate_load(e, s)
                sp.wait_ge(S("kv_used"), e)
                kv_load(e)
                rest_of_expert(e)

            def chunk_source(name, c):
                col = slice(256 * c, 256 * c + 256)
                if name == "ab":
                    at = 256 * c if c < 6 else 8 + 256 * c
                    return t["ab_w_in_2"][0].rearrange("(t p) n -> p t n", p=P)[:, :, at:at + 256]
                if name in ("ab_out", "c_in", "c_out"):
                    src = {"ab_out": "ab_w_out_2", "c_in": "c_w_in_2", "c_out": "c_w_out_2"}[name]
                    return t[src][0].rearrange("(t p) n -> p t n", p=P)[:, :, col]
                if name in ("c_a", "c_i"):
                    src = {"c_a": "c_w_a_2", "c_i": "c_w_i_2"}[name]
                    return t[src][0].rearrange("b (k p) n -> p (b k) n", p=P)
                L, name = int(name[-1]), name[:-1]
                if name in ("xq", "xo"):
                    return t[f"w_{name}_2"][L].rearrange("(t p) n -> p t n", p=P)[:, :, col]
                gu_w = t["w_ffn_gu_2"][L].rearrange("(t p) n -> p t n", p=P)
                if name == "gate":
                    return gu_w[:, :, col]
                if name == "up":
                    return gu_w[:, :, DFF + 256 * c:DFF + 256 * c + 256]
                return t["w_ffn_down_2"][L].rearrange("(j p) n -> p j n", p=P)[:, 2 * c:2 * c + 2, :]

            for k, (name, c) in enumerate(C_CHUNKS):
                s = k % CSLOTS
                if k < CSLOTS:
                    g = min(g for g in range(ESLOTS) if DOWN_END[g] * D >= (s + 1) * SLOT)
                    sp.wait_ge(S("down_used"), 8 * EXP - 8 + max(g, min(s, ESLOTS - 1)) + 1)
                else:
                    last = k - CSLOTS
                    if last in split_index:
                        sp.wait_ge(S("weights_low_dve"), split_index[last] + 1)
                        sp.wait_ge(S("weights_low_pool"), split_index[last] + 1)
                    else:
                        sp.wait_ge(*chunk_used[last])
                src = chunk_source(name, c)
                sp.dma_start(tiles(raw_slot(k), src.shape[1]), src).then_inc(landed(s), 16)

            y = out[0].rearrange("(i p) n -> p i n", p=P)
            for i in range(2):
                sp.wait_ge(S("out_rows"), 2 * (i + 1))
                sp.dma_start(y[:, i, :], tiles(yT, 2)[:, i, :]).then_inc(S("stored"), 16)
            sp.wait_ge(S("stored"), 32)

        @block.gpsimd
        def _(pool):
            pool.memset(ones[:], 1.0).then_inc(S("ones_ready"), 1)
            for name, dst in (("dist_fwd", dist_fwd), ("dist_bwd", dist_bwd), ("pick", pick[0:8]), ("dirs", dirs),
                              ("into", into), ("bar_fwd", bar_fwd), ("bar_bwd", bar_bwd)):
                pool.dma_start(dst, t[name]).then_inc(S("tables_landed"), 16)
            for name, dst in (("cos", cosT), ("sin", sinT), ("rot", rot)):
                pool.dma_start(dst, t[name]).then_inc(S("rotary_landed"), 16)
            gates = t["b_gates"].rearrange("a (r c) -> (a r) c", c=1)
            pool.dma_start(b_i, gates[0:8]).then_inc(S("bias_landed"), 16)
            pool.dma_start(b_f, gates[8:16]).then_inc(S("bias_landed"), 16)
            pool.dma_start(b_fox, t["ab_b_f_2"].rearrange("a (r c) -> (a r) c", c=1)).then_inc(S("bias_landed"), 16)
            pool.dma_start(iota_col, t["iota_col"]).then_inc(S("bias_landed"), 16)
            dec = DEC.rearrange("p (h i l) -> p h i l", h=H, i=TT)
            for n in range(H * TT):
                h, i = n // TT, n % TT
                pool.wait_ge(S("decay_exps"), 2 * (n + 1))
                pool.tensor_tensor(dec[:, h, i, :], dec[:, h, i, :], moT[:, (n % 2) * T:(n % 2 + 1) * T], ALU.mult)\
                    .then_inc(S("decay_product"), 1)
                pool.wait_ge(S("decay_product"), n + 1)
                blk = dec[0:ROWS[i], h, i, P * i:P * i + ROWS[i]]
                pool.tensor_tensor(blk, blk, ident[0:ROWS[i], 0:ROWS[i]], ALU.add).then_inc(S("decay_ready"), 1)
            pool.wait_ge(S("proj_ready"), 2 * NA)
            pool.dma_start(own[0:EXP], t["own"]).then_inc(S("own_landed"), 16)
            pool.dma_start(iota_row, t["iota_row"]).then_inc(S("iota_landed"), 16)
            mm_l = tiles(mm, 2)
            st3 = ST.rearrange("p (i s) -> p i s", i=TT)
            ste3 = STe.rearrange("p (i s) -> p i s", i=TT)
            pool.wait_ge(S("gather_ready"), TT)
            pool.tensor_copy(ste3, st3[:, :, 0:CAP]).then_inc(S("ste_ready"), 1)
            pool.wait_ge(S("norm_out"), 8 * 4)
            pool.tensor_copy(mwork, mm_l[:, 0, :]).then_inc(S("mwork_ready"), 1)
            with pool.Fori(1, EXP) as e:
                pool.wait_ge(S("xs_ready"), e)
                pool.tensor_copy(ste3, st3[:, :, bass.ds(e * CAP, CAP)]).then_inc(S("ste_ready"), 1)
                pool.wait_ge(S("kv_used"), e)
                pool.tensor_copy(mwork, mm[:, bass.ds((e // 8) * 2048, 2048)]).then_inc(S("mwork_ready"), 1)
            pool.wait_ge(S("xs_ready"), EXP)
            pool.tensor_copy(ste3, st3[:, :, EXP * CAP:(EXP + 1) * CAP]).then_inc(S("ste_ready"), 1)
            pool.wait_ge(S("norm_out"), 8 * 6)
            pool.dma_start(fox_bar, t["bar_causal"]).then_inc(S("fox_tables"), 16)
            pool.dma_start(fpick[0:8], t["pick"]).then_inc(S("fox_tables"), 16)
            cols = slice(0, 256 * POOL_TILES)
            for n, k in enumerate(split_chunks):
                pool.wait_ge(S("weights_high"), n + 1)
                pool.tensor_tensor(part(lows, n)[:, cols], raw_slot(k)[:, cols], part(highs, n)[:, cols], ALU.subtract)\
                    .then_inc(S("weights_low_pool"), 1)

        @block.tensor
        def _(pe):
            norms = [0]

            def norm_part(q, width):
                pe.wait_ge(S("norm_squares"), 4 * norms[0] + q + 1)
                sq = tiles(SQ[:, 0:KT * width], KT)
                for i in (2 * q, 2 * q + 1):
                    last = pe.matmul(bank[7][:, 0:width], ones[:], sq[:, i, :], start=(i == 0), stop=(i == KT - 1))
                if q == 3:
                    last.then_inc(S("norm_sum"), 1)
                    norms[0] += 1

            def norm_sum(width):
                for q in range(4):
                    norm_part(q, width)

            def column_tile(k, slot, off, moving, width, at=0, kt=KT, wait=True, done=True, fresh=None):
                if wait:
                    pe_bank_free(pe, k)
                w = tiles(W[:, slot * SLOT:(slot + 1) * SLOT], kt)
                for i in range(kt):
                    if fresh is not None:
                        pe.wait_ge(S("norm_out"), fresh + i + 1)
                    last = pe.matmul(bank[pj.entries[k][0]][:, at:at + width], w[:, i, off:off + P], moving[:, i, :],
                                     start=(i == 0), stop=(i == kt - 1))
                if done:
                    last.then_inc(S("proj_ready"), 1)
                return last

            def chunk_a(k):
                pe.wait_ge(landed(k % SLOTS), 16 * (k // SLOTS + 1))

            pe.wait_ge(S("ident_landed"), 16)
            pe.wait_ge(S("x_landed"), 64)
            xt = tiles(xtok, TT)
            for i in range(KT):
                if i >= 4:
                    pe.wait_ge(S("xt_taken_act" if i % 2 == 0 else "xt_taken_dve"), i // 2 - 1)
                for j in range(TT):
                    last = pe.transpose(bank[i % 4][:, P * j:P * j + ROWS[j]], xt[0:ROWS[j], j, P * i:P * i + P],
                                        ident[0:ROWS[j], 0:ROWS[j]])
                last.then_inc(S("xt_ready"), 1)
            pe.wait_ge(S("vec_landed"), 16 * sum(len(g) for g in VEC_ROWS))
            for j, n in enumerate(VEC_COUNT):
                last = pe.transpose(bank[4][:, P * j:P * j + n], vrow[0:n, P * j:P * j + P], ident[0:n, 0:n])
            last.then_inc(S("vec_ready"), 1)
            pe.wait_ge(S("ones_ready"), 1)
            norm_sum(T)

            u3 = tiles(uT, KT)
            gw = tiles(GW[:], KT)
            pe.wait_ge(S("norm_out"), 8)
            pe.wait_ge(S("gate_w_landed"), 16)
            for g in range(2):
                for i in range(KT):
                    last = pe.matmul(bank[4 + g][0:8, 0:T], gw[:, i, 8 * g:8 * g + 8], u3[:, i, :],
                                     start=(i == 0), stop=(i == KT - 1))
                last.then_inc(S("gates_ready"), 1)

            for b in (0, 1):
                pe.wait_ge(S("xt_taken_act"), 4)
                pe.wait_ge(S("xt_taken_dve"), 4)

            def project_a(first, last_chunk):
                for k in range(first, last_chunk):
                    chunk_a(k)
                    column_tile(A_FIRST[2 * k], k % SLOTS, 0, u3, T)
                    column_tile(A_FIRST[2 * k + 1], k % SLOTS, P, u3, T)

            project_a(0, 6)

            def values_to_tokens(src, dst_bank):
                s3 = tiles(src, H)
                for j in range(TT):
                    for h in range(H):
                        last = pe.transpose(bank[dst_bank + j][0:ROWS[j], P * h:P * h + P],
                                            s3[:, h, P * j:P * j + ROWS[j]], ident[:])
                    last.then_inc(S("values_ready"), 1)

            pe.wait_ge(S("proj_taken_act"), 12)
            pe.wait_ge(S("gates_taken"), 2)
            values_to_tokens(mvT, 4)
            project_a(6, 12)
            pe.wait_ge(S("values_taken"), TT)
            pe.wait_ge(S("proj_taken_act"), 24)
            values_to_tokens(rvT, 4)

            pe.wait_ge(S("rotary_landed"), 48)
            for n in range(2 * H):
                if n == 0:
                    pe.wait_ge(S("values_taken"), 2 * TT)
                else:
                    pe.wait_ge(S("rotary_taken"), n)
                src = tiles(rqT if n < H else rkT, H)[:, n % H, :]
                pe.matmul(bank[7][:, 0:T], rot, src, start=True, stop=True).then_inc(S("rotary_ready"), 1)

            pe.wait_ge(S("gate_rows_ready"), 1)
            for j in range(TT):
                last = pe.transpose(bank[3][0:ROWS[j], 8 * j:8 * j + 8], Bb[0:8, P * j:P * j + ROWS[j]], ident[0:8, 0:8])
            last.then_inc(S("acol_ready"), 1)

            qk = tiles(QK, 8)
            mv3 = tiles(mv, TT)

            def scores(q, k, gate, sem):
                pe.wait_ge(*gate)
                for j in range(TT):
                    last = pe.matmul(bank[4 + j][0:ROWS[j], 0:T], k[:, P * j:P * j + ROWS[j]], q, start=True, stop=True)
                last.then_inc(S(sem), 1)

            def stab(n):
                h, d = n // 2, n % 2
                r = 4 * d + h
                if n == 0:
                    pe.wait_ge(S("rotary_taken"), 2 * H)
                    pe.wait_ge(S("stab_ready"), 1)
                else:
                    pe.wait_ge(S("args_ready"), n)
                pe.matmul(bank[7][:, 0:T], pick[0:8, P * r:P * r + P], sf[0:8, :], start=True, stop=True)\
                    .then_inc(S("stab_bcast"), 1)

            def span(d, j):
                return (P * j, T) if d == 0 else (0, min(T, P * (j + 1)))

            pe.wait_ge(S("acol_taken"), 1)
            pe.wait_ge(S("tables_landed"), 7 * 16)
            stab(0)
            scores(qk[:, 0, :], qk[:, H, :], (S("qk_ready"), 8), "m_scores")
            for n in range(8):
                h, d = n // 2, n % 2
                r = 4 * d + h
                if n + 1 < 8:
                    stab(n + 1)
                pt = tiles(SQ[:, (n % 2) * 816:(n % 2 + 1) * 816], TT)
                pe.wait_ge(S("m_probs"), n + 1)
                if n:
                    pe.wait_ge(S("num_taken"), n)
                order = list(range(TT)) if d == 0 else list(range(TT))[::-1]
                for j in order:
                    lo, hi = span(d, j)
                    pe.matmul(bank[2][:, lo:hi], mv3[0:ROWS[j], j, P * h:P * h + P], pt[0:ROWS[j], j, lo:hi],
                              start=(j == order[0]), stop=(j == order[-1]))
                for j in order:
                    lo, hi = span(d, j)
                    last = pe.matmul(bank[3][0:8, lo:hi], into[0:ROWS[j], 8 * r:8 * r + 8], pt[0:ROWS[j], j, lo:hi],
                                     start=(n == 0 and j == order[0]), stop=(n == 7 and j == order[-1]))
                last.then_inc(S("num_ready"), 1)
                if d == 1 and n < 7:
                    scores(qk[:, h + 1, :], qk[:, H + h + 1, :], (S("m_probs"), n + 1), "m_scores")
                if n % 2 == 1:
                    project_a(12 + n // 2, 13 + n // 2)

            pe.wait_ge(S("recip_ready"), 1)
            for r in range(8):
                if r >= 2:
                    pe.wait_ge(S("recip_taken"), r - 1)
                else:
                    pe.wait_ge(S("num_taken"), 8)
                pe.matmul(bank[2 + r % 2][:, 0:T], pick[0:8, P * r:P * r + P], rowt[0:8, :], start=True, stop=True)\
                    .then_inc(S("recip_bcast"), 1)

            rq3, rk3, rv3 = tiles(rqT, H), tiles(rkT, H), tiles(rv, TT)
            pe.wait_ge(S("rot_out"), 8)
            pe.wait_ge(S("args_ready"), 8)
            for h in range(H):
                scores(rq3[:, h, :], rk3[:, h, :], (S("m_probs"), 8) if h == 0 else (S("r_probs"), h), "r_scores")
                pt = tiles(SQ[:, (h % 2) * 816:(h % 2 + 1) * 816], TT)
                pe.wait_ge(S("r_probs"), h + 1)
                if h:
                    pe.wait_ge(S("ret_taken"), h)
                for j in range(TT):
                    last = pe.matmul(bank[7][:, 0:T], rv3[0:ROWS[j], j, P * h:P * h + P], pt[0:ROWS[j], j, :],
                                     start=(j == 0), stop=(j == TT - 1))
                last.then_inc(S("ret_ready"), 1)

            def head_norm(src, n):
                s3 = tiles(src, H)
                sq = tiles(SQ[:, 0:H * T], H)
                for h in range(H):
                    last = pe.matmul(bank[4 + h][:, 0:T], ones[:], s3[:, h, :], start=True, stop=True)
                last.then_inc(S("hn_mean"), 1)
                pe.wait_ge(S("hn_squares"), n + 1)
                for h in range(H):
                    last = pe.matmul(bank[4 + h][:, 0:T], ones[:], sq[:, h, :], start=True, stop=True)
                last.then_inc(S("hn_var"), 1)

            pe.wait_ge(S("ret_taken"), H)
            head_norm(RET, 0)
            pe.wait_ge(S("hm_ready"), 1)
            pe.wait_ge(S("hn_rstd"), 1)
            head_norm(HM, 1)

            pe.wait_ge(S("y_ready"), 2)
            for k in range(16, NA):
                chunk_a(k)
                for half in range(2):
                    column_tile(A_OUT[2 * (k - 16) + half], k % SLOTS, P * half, u3, T)

            norm_sum(T)
            pe.wait_ge(S("norm_out"), 16)
            pe.wait_ge(S("router_w_landed"), 16)
            rw = tiles(RW[:], KT)
            u23 = tiles(u2, KT)
            for j in range(TT):
                for i in range(KT):
                    last = pe.matmul(bank[4][0:ROWS[j], 16 * j:16 * j + 16], u23[:, i, P * j:P * j + ROWS[j]], rw[:, i, :],
                                     start=(i == 0), stop=(i == KT - 1))
            last.then_inc(S("router_ready"), 1)
            pe.wait_ge(S("proj_taken_dve"), KT)
            for n in range(2 * TT):
                j, half = n // 2, n % 2
                b = [0, 1, 2, 3, 5, 6][n]
                for i in range(4):
                    last = pe.transpose(bank[b][0:ROWS[j], P * i:P * i + P], u23[:, 4 * half + i, P * j:P * j + ROWS[j]], ident[:])
                last.then_inc(S("utok_ready"), 1)
            pe.wait_ge(S("mem_landed"), 16)
            m3 = tiles(memtok, 2)
            for b in range(4):
                pe.wait_ge(S("utok_taken"), b + 1)
                for i in range(2):
                    for j in range(2):
                        last = pe.transpose(bank[b][:, 256 * i + P * j:256 * i + P * j + P],
                                            m3[:, j, P * (2 * b + i):P * (2 * b + i) + P], ident[:])
                last.then_inc(S("mem_ready"), 1)
            pe.wait_ge(S("aff_ready"), 1)
            pe.wait_ge(S("utok_taken"), 6)
            a3 = tiles(aff, TT)
            for j in range(TT):
                last = pe.transpose(bank[5][0:EXP, P * j:P * j + ROWS[j]], a3[0:ROWS[j], j, :], ident[0:ROWS[j], 0:ROWS[j]])
            last.then_inc(S("affT_ready"), 1)
            norm_sum(256)
            pe.wait_ge(S("spread_ready"), 1)
            for b in range(2):
                last = pe.matmul(bank[5 + b][:, 0:272], ones[0:EXP, :], spread[0:EXP, 272 * b:272 * b + 272], start=True, stop=True)
            pe.transpose(bank[4][:, 0:EXP], idx2[0:EXP], ident[0:EXP, 0:EXP])
            pe.transpose(bank[4][:, EXP:2 * EXP], val2[0:EXP], ident[0:EXP, 0:EXP]).then_inc(S("choice_ready"), 1)

            ut3, ste3 = tiles(utok, TT), tiles(STe, TT)
            xs3 = tiles(xs, KT)
            mw3, kw3 = tiles(mwork, KT), tiles(kvw, KT)

            def gather():
                for i in range(KT):
                    for j in range(TT):
                        last = pe.matmul(bank[6][:, CAP * i:CAP * i + CAP], ut3[0:ROWS[j], j, P * i:P * i + P],
                                         ste3[0:ROWS[j], j, :], start=(j == 0), stop=(j == TT - 1))
                last.then_inc(S("xs_ready"), 1)

            def hidden(e, first_bank, sem, use):
                for s in range(ESLOTS):
                    if use == 2:
                        scatter(e, s)
                    pe.wait_ge(landed(s), 48 * e + 16 * (A_USES[s] + use))
                    w = W[:, s * DFF:(s + 1) * DFF].rearrange("p (f j) -> p f j", j=FT)
                    for c, (lo, hi) in enumerate(HCHUNKS):
                        for half in range(2):
                            last = pe.matmul(bank[first_bank + c][MPAD * half:MPAD * half + MPAD, 0:(hi - lo) * HF],
                                             xs3[:, s, :], w[:, lo:hi, HF * half:HF * half + HF],
                                             start=(s == 0), stop=(s == ESLOTS - 1), skip_group_check=True)
                    last.then_inc(S(sem), 1)

            def scatter(e, i):
                if i == 0:
                    pe.wait_ge(S("y_taken"), e + 1)
                    pe.wait_ge(S("se_ready"), e + 1)
                    pe.wait_ge(S("kv_taken"), e + 1)
                else:
                    pe.wait_ge(S("scatter_taken"), 8 * e + i)
                r, c = MPAD * (i // 4), P * (i % 4)
                pe.matmul(bank[7][:, 0:T], ys[r:r + MPAD, c:c + P], Se[r:r + MPAD, :], start=True, stop=True)\
                    .then_inc(S("scatter_ready"), 1)

            pe.wait_ge(S("xs_pads"), 1)
            pe.wait_ge(S("gather_ready"), TT)
            pe.wait_ge(S("ste_ready"), 1)
            gather()
            hid3 = th.rearrange("p (f j) -> p f j", j=HF)
            with pe.Fori(0, EXP) as e:
                pe.wait_ge(S("xs_taken"), e + 1)
                hidden(e, 0, "gate_used", 1)
                hidden(e, 3, "up_used", 2)
                pe.wait_ge(S("scatter_taken"), 8 * e + 8)
                pe.wait_ge(S("kv_landed"), 32 * e + 32)
                pe.wait_ge(S("mwork_ready"), e + 1)
                for i in range(KT):
                    pe.matmul(bank[7][:, 0:256], kw3[:, i, 0:P], mw3[:, i, :], start=(i == 0), stop=(i == KT - 1))
                for m in range(2):
                    for i in range(KT):
                        last = pe.matmul(bank[7][:, 256 + P * m:256 + P * m + P], mw3[:, i, P * m:P * m + P], kw3[:, i, P:2 * P],
                                         start=(i == 0), stop=(i == KT - 1))
                last.then_inc(S("kv_used"), 1)
                pe.wait_ge(S("ste_ready"), e + 2)
                gather()
                pe.wait_ge(S("hid_ready"), 3 * e + 3)
                for j in range(HF):
                    last = pe.transpose(bank[j // 4][:, P * (j % 4):P * (j % 4) + P], hid3[:, :, j], ident[:])
                    if j % 4 == 3 or j == HF - 1:
                        last.then_inc(S("hidT_ready"), 1)
                pe.wait_ge(S("xs_taken"), e + 2)
                slots = 0
                for j in range(FT):
                    if j < HF and j % 4 == 0:
                        pe.wait_ge(S("hidT_taken"), 3 * e + j // 4 + 1)
                    while slots <= DOWN_SLOT[j]:
                        pe.wait_ge(landed(slots), 48 * e + 16 * (A_USES[slots] + 3))
                        slots += 1
                    at = P * (j % HF) + MPAD * (j // HF)
                    for half in range(2):
                        last = pe.matmul(bank[6][MPAD * half:MPAD * half + MPAD, :], hidT[:, at:at + MPAD],
                                         W[:, j * D + 512 * half:j * D + 512 * half + 512],
                                         start=(j == 0), stop=(j == FT - 1), skip_group_check=True)
                    if j + 1 in DOWN_END:
                        last.then_inc(S("down_used"), 1)
            for i in range(KT):
                scatter(EXP, i)

            pe.wait_ge(S("scatter_taken"), 8 * (EXP + 1))
            norm_sum(256)
            hn3 = tiles(hN, KT)
            outs = [8 * 5]

            def norm_done():
                outs[0] += 8
                pe.wait_ge(S("norm_out"), outs[0])

            def pair(key, entry, moving, fresh=False):
                s = chunk_landed(pe, key)
                pe_bank_free(pe, entry)
                for half in range(2):
                    last = column_tile(entry, s, P * half, moving, 256, at=256 * half, wait=False, done=False,
                                       fresh=outs[0] - 8 if fresh and half == 0 else None)
                last.then_inc(S("proj_ready"), 1)

            def pre_normed():
                norm_sum(256)
                outs[0] += 8

            def post_normed(pairs):
                for k, one in enumerate(pairs):
                    one()
                    if k:
                        norm_part(k - 1, 256)
                norm_part(3, 256)
                outs[0] += 8

            def transpose_probs(n, e2, src, pairs):
                pe.wait_ge(S("att_probs"), n + 1)
                if n:
                    pe.wait_ge(S("pt_taken"), n)
                for qi in range(2):
                    for m in range(2):
                        last = pe.transpose(bank[7][:, 256 * m + P * qi:256 * m + P * qi + P],
                                            src[:, 256 * qi + P * m:256 * qi + P * m + P], ident[:])
                last.then_inc(S("pt_ready"), 1)

            def split_landed(key):
                k = c_index[key]
                n = split_index[k]
                pe.wait_ge(S("weights_high"), n + 1)
                pe.wait_ge(S("weights_low_dve"), n + 1)
                pe.wait_ge(S("weights_low_pool"), n + 1)
                return part(highs, n), part(lows, n)

            def three_passes(dst, parts, start, stop, check=False):
                todo = [(wh, xh) for (wh, wl), (xh, xl) in parts] + [(wh, xl) for (wh, wl), (xh, xl) in parts] \
                    + [(wl, xh) for (wh, wl), (xh, xl) in parts]
                for n, (w, x) in enumerate(todo):
                    last = pe.matmul(dst, w, x, start=start and n == 0, stop=stop and n == len(todo) - 1,
                                     skip_group_check=check)
                return last

            def pair3(key, entry):
                high, low = (tiles(w, KT) for w in split_landed(key))
                xh, xl = tiles(x_high, KT), tiles(x_low, KT)
                pe_bank_free(pe, entry)
                for half in range(2):
                    c = slice(P * half, P * half + P)
                    last = three_passes(bank[pj.entries[entry][0]][:, 256 * half:256 * half + 256],
                                        [((high[:, i, c], low[:, i, c]), (xh[:, i, :], xl[:, i, :])) for i in range(KT)],
                                        True, True)
                last.then_inc(S("proj_ready"), 1)

            att = [0]
            for L in range(2):
                pre_normed()
                if L == 0:
                    pe.wait_ge(S("norm_out"), outs[0])
                    pe.wait_ge(S("fox_w_landed"), 16)
                    fw = tiles(GW[:, 0:64], KT)
                    for i in range(KT):
                        last = pe.matmul(bank[6][0:8, 0:256], fw[:, i, :], hn3[:, i, :], start=(i == 0), stop=(i == KT - 1))
                    last.then_inc(S("fox_logits"), 1)
                    for k in range(4):
                        pair(("ab", k), C["ab", k], hn3)
                    for k in (4, 5):
                        s = chunk_landed(pe, ("ab", k))
                        pe_bank_free(pe, C["ab", k])
                        w = tiles(W[:, s * SLOT:(s + 1) * SLOT], KT)
                        for m in range(2):
                            for i in range(KT):
                                last = pe.matmul(bank[k % 4][:, 256 * m:256 * m + 256], hn3[:, i, P * m:P * m + P], w[:, i, :],
                                                 start=(i == 0), stop=(i == KT - 1))
                        last.then_inc(S("proj_ready"), 1)
                    q3, k3, v3 = tiles(fq, 4), tiles(fk, 4), fv

                    def fox_scores(n):
                        r = 64 * (n % 2)
                        if n:
                            pe.wait_ge(S("att_scores_taken"), n)
                        for qi in range(2):
                            pe.matmul(bank[5][:, 256 * qi:256 * qi + 256], q3[r:r + 64, n // 2, P * qi:P * qi + P],
                                      k3[r:r + 64, n // 2, :], start=True, stop=True)
                        pe.matmul(bank[6][:, 0:256], fpick[0:8, P * n:P * n + P], frow[0:8, :], start=True, stop=True)\
                            .then_inc(S("att_scores"), 1)

                    pe.wait_ge(S("proj_taken_act"), taken_after("act", C["ab", 5]))
                    pe.wait_ge(S("fox_row_ready"), 1)
                    pe.wait_ge(S("fox_tables"), 32)
                    fox_scores(0)
                    for n in range(8):
                        if n < 7:
                            fox_scores(n + 1)
                        if n < 6:
                            pair(("ab", 6 + n), C["ab", 6 + n], hn3)
                        transpose_probs(n, None, fox_e[n % 2], None)
                        pe.wait_ge(S("pt_taken"), n + 1)
                        if n and n % 2 == 0:
                            pe.wait_ge(S("att_out_taken"), n // 2)
                        r = 64 * (n % 2)
                        for m in range(2):
                            at = 512 * (n // 4) + 256 * m + 64 * (n % 4)
                            last = pe.matmul(bank[4][r:r + 64, 0:256], v3[:, at:at + 64], fox_pt[n % 2][:, 256 * m:256 * m + 256],
                                             start=(m == 0), stop=(m == 1))
                        last.then_inc(S("att_out"), 1)
                    att[0] = 8
                    pe.wait_ge(S("mixed"), 2)
                else:
                    for k in range(8):
                        pair(("c_in", (k + 4) % 8), C["c_in", k], hn3, k == 0)
                    lu3 = tiles(lu, KT)
                    pe.wait_ge(S("lru_conv"), KT)
                    for k in range(8):
                        w = None
                        if k % 4 == 0:
                            s = chunk_landed(pe, ("c_a" if k < 4 else "c_i", 0))
                        w = tiles(W[:, s * SLOT:(s + 1) * SLOT], KT)
                        b = k % 4
                        pe_bank_free(pe, C["c_gates", k])
                        for half in range(2):
                            for i in range(2):
                                last = pe.matmul(bank[k % 4][:, 256 * half:256 * half + 256], w[:, 2 * b + i, P * half:P * half + P],
                                                 lu3[:, 2 * b + i, :], start=(i == 0), stop=(i == 1))
                        last.then_inc(S("proj_ready"), 1)
                    pe.wait_ge(S("mixed"), 3)
                y3 = tiles(yT, KT)
                post_normed([lambda k=k: pair(("ab_out" if L == 0 else "c_out", k), C["mix_out", L, k], y3)
                             for k in range(4)])
                pre_normed()
                for k in range(4):
                    pair((f"xq{L}", k), C["xq", L, k], hn3, k == 0)
                xq3 = tiles(xq, KT)
                kk = kT2[:, 2048 * L:2048 * L + 2048]

                def cross_scores(n):
                    h = n % 4
                    pe.wait_ge(S("att_exps"), 2 * n)
                    for qi in range(2):
                        for i in range(2):
                            last = pe.matmul(bank[5][:, 256 * qi:256 * qi + 256], xq3[:, 2 * h + i, P * qi:P * qi + P],
                                             kk[:, 256 * (2 * h + i):256 * (2 * h + i) + 256], start=(i == 0), stop=(i == 1))
                    last.then_inc(S("att_scores"), 1)

                pe.wait_ge(S("proj_taken_act"), taken_after("act", C["xq", L, 3]))
                n0 = 8 + 4 * L
                cross_scores(n0)
                for n in range(n0, n0 + 4):
                    h = n % 4
                    if n < n0 + 3:
                        cross_scores(n + 1)
                    transpose_probs(n, None, att_e[n % 2], None)
                    pe.wait_ge(S("pt_taken"), n + 1)
                    if n == n0:
                        pe.wait_ge(S("att_out_taken"), 4 + 4 * L)
                    else:
                        pe.wait_ge(S("att_out_taken"), n - 4)
                    for dv in range(2):
                        for m in range(2):
                            at = 2048 * L + 256 * (2 * h + dv) + P * m
                            last = pe.matmul(bank[6][:, 256 * dv:256 * dv + 256], v2[:, at:at + P],
                                             att_pt[n % 2][:, 256 * m:256 * m + 256], start=(m == 0), stop=(m == 1))
                    last.then_inc(S("att_out"), 1)
                pe.wait_ge(S("att_out_taken"), 4 + 4 * L + 4)
                xo3 = tiles(xo, KT)
                post_normed([lambda k=k: pair((f"xo{L}", k), C["xo", L, k], xo3) for k in range(4)])
                pre_normed()
                pair((f"gate{L}", 0), C["gate", L, 0], hn3, True)
                pe.wait_ge(S("input_split"), L + 1)
                for k in range(FT // 2):
                    if k:
                        pair3((f"gate{L}", k), C["gate", L, k])
                    pair3((f"up{L}", k), C["up", L, k])
                fh_low, fh_high = tiles(fhid_low, FT), tiles(fhid_high, FT)
                for b in range(4):
                    pe_bank_free(pe, C["down", L, b])
                for c in range(FT // 2):
                    high, low = (tiles(w, 2) for w in split_landed((f"down{L}", c)))
                    pe.wait_ge(S("hidden_split"), L * (FT // 2) + c + 1)
                    for i in range(KT):
                        f = slice(P * i, P * i + P)
                        last = three_passes(bank[i // 2][:, 256 * (i % 2):256 * (i % 2) + 256],
                                            [((high[:, jj, f], low[:, jj, f]), (fh_high[:, 2 * c + jj, :], fh_low[:, 2 * c + jj, :]))
                                             for jj in range(2)], c == 0 and i % 2 == 0, c == FT // 2 - 1, True)
                        if c == FT // 2 - 1 and i % 2 == 1:
                            last.then_inc(S("proj_ready"), 1)
                    if c < FT // 2 - 1:
                        last.then_inc(S("ffn_down_used"), 1)
                norm_sum(256)
                outs[0] += 8

            pe.wait_ge(S("norm_out"), outs[0])
            x3 = tiles(xT, KT)
            for n in range(4):
                j, half = n // 2, n % 2
                for i in range(4):
                    last = pe.transpose(bank[n][:, P * i:P * i + P], x3[:, 4 * half + i, P * j:P * j + P], ident[:])
                last.then_inc(S("out_ready"), 1)

        @block.scalar
        def _(act):
            steps = [0]

            def after(ins):
                steps[0] += 1
                ins.then_inc(S("act_step"), 1)
                act.wait_ge(S("act_step"), steps[0])

            norms = [0]

            def log_exp_set():
                act.preload_act_table_set("natural_log_exp_and_others")

            def squares_pair(q, src, width):
                act.activation(tiles(SQ[:, 0:KT * width], KT)[:, 2 * q:2 * q + 2, :], src, ACT.Square)\
                   .then_inc(S("norm_squares"), 1)

            def squares(src3, width, ready=None):
                for q in range(4):
                    if ready:
                        act.wait_ge(S(ready[0]), ready[1] + 2 * q + 2)
                    squares_pair(q, src3[:, 2 * q:2 * q + 2, :], width)

            def rstd(width):
                n = norms[0]
                norms[0] += 1
                act.wait_ge(S("norm_sum"), n + 1)
                if n:
                    act.wait_ge(S("norm_out"), [0, 8, 16, 32][n] if n < 4 else 8 * (n + 1))
                after(act.activation(RSTD[:, 0:width], bank[7][:, 0:width], ACT.Ln, bias=eps, scale=1.0 / D))
                act.activation(RSTD[:, 0:width], RSTD[:, 0:width], ACT.Exp, scale=-0.5).then_inc(S("norm_rstd"), 1)

            act.dma_start(ident[:], t["ident"]).then_inc(S("ident_landed"), 16)
            act.dma_start(lgt[:, 8:16], t["ret_decay_logit"].rearrange("a d h -> a (d h)").to_broadcast([P, 8]))\
               .then_inc(S("logit_landed"), 16)

            log_exp_set()
            act.wait_ge(S("magnitudes"), 1)
            after(act.activation(lgt[:, 0:8], lgt[:, 0:8], ACT.Exp, scale=-1.0))
            act.activation(lgt[:, 0:8], lgt[:, 0:8], ACT.Ln, bias=1.0).then_inc(S("log_terms"), 1)

            ht3, u3 = tiles(hT[:], KT), tiles(uT, KT)
            act.wait_ge(S("eps_ready"), 1)
            for i in range(0, KT, 2):
                act.wait_ge(S("xt_ready"), i + 1)
                act.activation(ht3[:, i, :], bank[i % 4][:, 0:T], ACT.Copy).then_inc(S("xt_taken_act"), 1)
                act.wait_ge(S("xt_taken_act"), i // 2 + 1)
                act.wait_ge(S("xt_taken_dve"), i // 2 + 1)
                squares_pair(i // 2, ht3[:, i:i + 2, :], T)
            rstd(T)

            act.wait_ge(S("magnitudes"), 3)
            after(act.activation(rowt[0:8], rowt[0:8], ACT.Exp, scale=-1.0))
            act.activation(rowt[0:8], rowt[0:8], ACT.Ln, bias=1.0).then_inc(S("log_terms"), 1)

            act.wait_ge(S("magnitudes"), 2)
            after(act.activation(lamt[:, 0:8], lamt[:, 0:8], ACT.Exp, scale=-1.0))
            act.activation(lamt[:, 0:8], lamt[:, 0:8], ACT.Ln, bias=1.0).then_inc(S("log_terms"), 1)

            dec = DEC.rearrange("p (h i l) -> p h i l", h=H, i=TT)
            qkp = tiles(QKP, 8)
            qk = tiles(QK, 8)
            sq8 = tiles(SQ[:], 8)

            def decay(n):
                h, i = n // TT, n % TT
                at = 256 - P * i
                if n == 0:
                    act.wait_ge(S("tables_landed"), 7 * 16)
                    act.wait_ge(S("lg_ready"), 1)
                if n >= 2:
                    act.wait_ge(S("decay_product"), n - 1)
                act.activation(dec[:, h, i, :], dist_fwd[:, at:at + T], ACT.Exp, scale=lg[:, h:h + 1])\
                   .then_inc(S("decay_exps"), 1)
                act.activation(moT[:, (n % 2) * T:(n % 2 + 1) * T], dist_bwd[:, at:at + T], ACT.Exp,
                               scale=lg[:, 4 + h:5 + h]).then_inc(S("decay_exps"), 1)

            def take(k, dst, func=ACT.Copy, scale=1.0, src=None):
                proj_ready(act, k)
                b = bank[pj.entries[k][0]]
                act.activation(dst, b[:, 0:T] if src is None else src(b), func, scale=scale)\
                   .then_inc(S("proj_taken_act"), 1)

            def values(dst, first, count):
                d3 = tiles(dst, TT)
                for j in range(TT):
                    act.wait_ge(S("values_ready"), count + j + 1)
                    act.activation(d3[0:ROWS[j], j, :], bank[4 + j][0:ROWS[j], :], ACT.Copy).then_inc(S("values_taken"), 1)

            act.wait_ge(S("pads_ready"), 2)
            mv_T, mo_T, rq_T, rk_T, rv_T, rg_T = (tiles(x, H) for x in (mvT, moT, rqT, rkT, rvT, rgT))
            for k in range(12):
                if k < 8:
                    take(k, qkp[:, k, PAD:PAD + T])
                else:
                    take(k, mv_T[:, k - 8, :])
                decay(k)
                if 2 <= k < 10:
                    act.wait_ge(S("conv_ready"), k - 1)
                    act.activation(sq8[:, k - 2, :], qk[:, k - 2, :], ACT.Tanh, scale=0.5).then_inc(S("conv_tanh"), 1)
            act.wait_ge(S("xt_ready"), KT)
            values(mv, 4, 0)
            for k in range(12, 24):
                dst = (rq_T, rk_T, rv_T)[(k - 12) // 4][:, k % 4, :]
                take(k, dst, scale=float(P) ** -0.5 if k < 16 else 1.0)
            values(rv, 4, TT)

            act.wait_ge(S("stab_ready"), 1)
            act.activation(Mr[0:8], Mr[0:8], ACT.Exp, scale=-1.0).then_inc(S("floor_ready"), 1)
            act.wait_ge(S("decay_ready"), H * TT)
            num3 = tiles(NUM, 8)

            def unit_exps(n):
                h, d = n // 2, n % 2
                pt = tiles(SQ[:, (n % 2) * 816:(n % 2 + 1) * 816], TT)
                act.wait_ge(S("args_ready"), n + 1)
                for j in range(TT):
                    lo, hi = (P * j, T) if d == 0 else (0, min(T, P * (j + 1)))
                    last = act.activation(pt[0:ROWS[j], j, lo:hi], pt[0:ROWS[j], j, lo:hi], ACT.Exp, scale=-1.0)
                last.then_inc(S("unit_exps"), 1)

            unit_exps(0)
            for n in range(8):
                h, d = n // 2, n % 2
                if n < 7:
                    unit_exps(n + 1)
                act.wait_ge(S("num_ready"), n + 1)
                act.activation(num3[:, 4 * d + h, :], bank[2][:, 0:T], ACT.Copy).then_inc(S("num_taken"), 1)
                if d == 1:
                    for k in (24 + 2 * h, 25 + 2 * h):
                        if k < 28:
                            take(k, mo_T[:, k - 24, :], ACT.Tanh, 0.5)
                        else:
                            take(k, rg_T[:, k - 28, :])
            act.wait_ge(S("proj_taken_act"), 32)
            act.activation(QK[:, 0:H * T], rgT, ACT.Tanh, scale=0.5).then_inc(S("rg_tanh"), 1)
            log_exp_set()
            ret3 = tiles(RET, H)
            for h in range(H):
                act.wait_ge(S("ret_ready"), h + 1)
                act.activation(ret3[:, h, :], bank[7][:, 0:T], ACT.Copy).then_inc(S("ret_taken"), 1)

            def head_norm(src, n):
                act.wait_ge(S("hn_centred"), n + 1)
                act.activation(SQ[:, 0:H * T], src, ACT.Square).then_inc(S("hn_squares"), 1)
                act.wait_ge(S("hn_var"), n + 1)
                ln = tiles(QK[:, H * T:2 * H * T], H)
                if n:
                    act.wait_ge(S("y_ready"), 1)
                for h in range(H):
                    last = act.activation(ln[:, h, :], bank[4 + h][:, 0:T], ACT.Ln, bias=eps, scale=1.0 / P)
                after(last)
                act.activation(QK[:, H * T:2 * H * T], QK[:, H * T:2 * H * T], ACT.Exp, scale=-0.5).then_inc(S("hn_rstd"), 1)

            head_norm(RET, 0)
            head_norm(HM, 1)

            squares(ht3, T, ("proj_taken_dve", 0))
            rstd(T)
            a3 = tiles(aff, TT)
            act.wait_ge(S("router_max"), 2)
            for j in range(TT):
                last = act.activation(a3[0:ROWS[j], j, :], bank[4][0:ROWS[j], 16 * j:16 * j + 16], ACT.Exp,
                                      bias=smax[0:ROWS[j], j:j + 1], accum_out=ssum[0:ROWS[j], j:j + 1])
                last.then_inc(S("router_exps"), 1)
            ut3 = tiles(utok, TT)
            for n in range(2 * TT):
                j, half = n // 2, n % 2
                act.wait_ge(S("utok_ready"), n + 1)
                act.activation(ut3[0:ROWS[j], j, 512 * half:512 * half + 512], bank[[0, 1, 2, 3, 5, 6][n]][0:ROWS[j], :], ACT.Copy)\
                   .then_inc(S("utok_taken"), 1)
            for b in range(4):
                act.wait_ge(S("mem_ready"), b + 1)
                act.activation(mT[:, 512 * b:512 * b + 512], bank[b][:], ACT.Copy).then_inc(S("mem_taken"), 1)
            act.wait_ge(S("mem_taken"), 4)
            act.wait_ge(S("norm_out"), 16)
            squares(tiles(mT, KT), 256)
            rstd(256)

            act.wait_ge(S("norm_sum"), 3)
            act.memzero(ys).then_inc(S("y_taken"), 1)
            act.memzero(small[0:8, 176:177]).then_inc(S("kv_taken"), 1)

            def take_xs(count):
                act.wait_ge(S("xs_ready"), count)
                act.activation(tiles(xs, KT)[:, :, 0:CAP], tiles(bank[6][:, 0:KT * CAP], KT), ACT.Copy).then_inc(S("xs_taken"), 1)

            take_xs(1)
            with act.Fori(0, EXP) as e:
                act.wait_ge(S("gate_used"), 8 * e + 8)
                for c, (lo, hi) in enumerate(HCHUNKS):
                    act.activation(th[:, HF * lo:HF * hi], bank[c][:, 0:HF * (hi - lo)], ACT.Tanh, scale=0.5)\
                       .then_inc(S("gate_tanh"), 1)
                act.wait_ge(S("kv_used"), e + 1)
                act.activation(kT2[:, bass.ds(256 * e, 256)], bank[7][:, 0:256], ACT.Copy)
                act.activation(v2[:, bass.ds(256 * e, 256)], bank[7][:, 256:512], ACT.Copy).then_inc(S("kv_taken"), 1)
                take_xs(e + 2)
                for b in range(3):
                    act.wait_ge(S("hidT_ready"), 3 * e + b + 1)
                    n = min(4, HF - 4 * b) * P
                    act.activation(hidT[:, 512 * b:512 * b + n], bank[b][:, 0:n], ACT.Copy).then_inc(S("hidT_taken"), 1)
                act.wait_ge(S("down_used"), 8 * e + 8)
                act.activation(ys, bank[6][:], ACT.Copy).then_inc(S("y_taken"), 1)

            x3, hn3, y3 = tiles(xT, KT), tiles(hN, KT), tiles(yT, KT)
            log_exp_set()
            act.wait_ge(S("scatter_ready"), 8 * (EXP + 1))
            squares(ht3[:, :, META:T], 256, ("scatter_taken", 8 * EXP))
            rstd(256)

            outs = [8 * 5]

            def pre_norm():
                squares(x3, 256, ("norm_out", outs[0] - 8))
                rstd(256)
                outs[0] += 8

            def post_norm(entries):
                for n, k in enumerate(entries):
                    proj_ready(act, k)
                    b = bank[pj.entries[k][0]]
                    squares_pair(n, tiles(b[:], 2), 256)
                    act.activation(hN[:, 512 * n:512 * n + 512], b[:], ACT.Copy).then_inc(S("proj_taken_act"), 1)
                rstd(256)
                outs[0] += 8

            def att_softmax(n, buf, scale, from_bank):
                act.wait_ge(S("att_max"), n + 1)
                for qi in range(2):
                    src = (bank[5] if from_bank else buf)[:, 256 * qi:256 * qi + 256]
                    last = act.activation(buf[:, 256 * qi:256 * qi + 256], src, ACT.Exp,
                                          bias=smax[:, 2 * (n % 2) + qi:2 * (n % 2) + qi + 1], scale=scale,
                                          accum_out=ssum[:, 2 * (n % 2) + qi:2 * (n % 2) + qi + 1])
                    last.then_inc(S("att_exps"), 1)

            def take_probs(n, dst):
                act.wait_ge(S("pt_ready"), n + 1)
                act.activation(dst, bank[7][:], ACT.Copy).then_inc(S("pt_taken"), 1)

            for L in range(2):
                pre_norm()
                if L == 0:
                    act.wait_ge(S("magnitudes"), 4)
                    after(act.activation(frow2[0:8], frow2[0:8], ACT.Exp, scale=-1.0))
                    act.activation(frow2[0:8], frow2[0:8], ACT.Ln, bias=1.0).then_inc(S("log_terms"), 1)
                    for k in range(6):
                        dst = (fq, fk, fv)[k // 2]
                        take(C["ab", k], dst[:, 512 * (k % 2):512 * (k % 2) + 512], src=lambda b: b[:])
                    att_softmax(0, fox_e[0], 1.0, False)
                    for n in range(8):
                        if n < 6:
                            dst = (fb, fc, fu)[n // 2]
                            take(C["ab", 6 + n], dst[:, 512 * (n % 2):512 * (n % 2) + 512], src=lambda b: b[:])
                        if n < 7:
                            att_softmax(n + 1, fox_e[(n + 1) % 2], 1.0, False)
                        take_probs(n, fox_pt[n % 2])
                        if n % 2 == 1:
                            act.wait_ge(S("att_out"), n + 1)
                            ins = act.activation(y3[:, n // 2, :], bank[4][:, 0:256], ACT.Copy)
                            ins.then_inc(S("att_out_taken"), 1)
                    act.wait_ge(S("att_out_taken"), 4)
                else:
                    lup3 = tiles(lup, KT)
                    act.wait_ge(S("lru_pads"), 1)
                    for k in range(4):
                        take(C["c_in", k], lup3[:, 2 * k:2 * k + 2, 3:259], src=lambda b: b[:].rearrange("p (a n) -> p a n", a=2))
                    for k in range(4):
                        take(C["c_in", 4 + k], lgate[:, 512 * k:512 * k + 512], src=lambda b: b[:])
                    act.wait_ge(S("half_bias"), 1)
                    for k in range(8):
                        dst, hb = (ta, half_a) if k < 4 else (ti, half_i)
                        b = k % 4
                        proj_ready(act, C["c_gates", k])
                        src = bank[pj.entries[C["c_gates", k]][0]]
                        act.activation(dst[:, 512 * b:512 * b + 256], src[:, 0:256], ACT.Tanh, bias=hb[:, 2 * b:2 * b + 1], scale=0.5)
                        act.activation(dst[:, 512 * b + 256:512 * b + 512], src[:, 256:512], ACT.Tanh,
                                       bias=hb[:, 2 * b + 1:2 * b + 2], scale=0.5).then_inc(S("proj_taken_act"), 1)
                    act.wait_ge(S("lru_rate"), 1)
                    act.wait_ge(S("proj_taken_act"), taken_after("act", C["c_gates", 7]))
                    for i in range(KT):
                        act.activation(tiles(ta, KT)[:, i, :], tiles(ta, KT)[:, i, :], ACT.Tanh, bias=n2sp[:, i:i + 1],
                                       scale=n2sp[:, i:i + 1]).then_inc(S("lru_tanh"), 1)
                    act.activation(SQ[:, 0:2048], lgate, ACT.Square).then_inc(S("gelu_square"), 1)
                    act.wait_ge(S("gelu_cubic"), 1)
                    act.activation(SQ[:, 0:2048], SQ[:, 0:2048], ACT.Tanh, scale=float(np.sqrt(2 / np.pi))).then_inc(S("gelu_tanh"), 1)
                    act.wait_ge(S("lru_denom"), 1)
                    log_exp_set()
                    after(act.activation(ta, ta, ACT.Ln, scale=-1.0))
                    act.activation(ta, ta, ACT.Exp, scale=0.5).then_inc(S("lru_sqrt"), 1)
                post_norm([C["mix_out", L, k] for k in range(4)])
                pre_norm()
                for k in range(4):
                    take(C["xq", L, k], xq[:, 512 * k:512 * k + 512], src=lambda b: b[:])
                n0 = 8 + 4 * L
                att_softmax(n0, att_e[0], 1.0 / 16, True)
                for n in range(n0, n0 + 4):
                    if n < n0 + 3:
                        att_softmax(n + 1, att_e[(n + 1) % 2], 1.0 / 16, True)
                    take_probs(n, att_pt[n % 2])
                    act.wait_ge(S("att_out"), n + 1)
                    act.activation(xo[:, 512 * (n % 4):512 * (n % 4) + 512], bank[6][:], ACT.Copy).then_inc(S("att_out_taken"), 1)
                post_norm([C["xo", L, k] for k in range(4)])
                pre_norm()
                for k in range(FT // 2):
                    n = L * (FT // 2) + k
                    proj_ready(act, C["gate", L, k])
                    if k >= 2:
                        act.wait_ge(S("hidden_split"), n - 1)
                    act.activation(fth[k % 2], bank[pj.entries[C["gate", L, k]][0]][:], ACT.Tanh, scale=0.5)\
                       .then_inc(S("ffn_tanh"), 1)
                log_exp_set()
                post_norm([C["down", L, k] for k in range(4)])

            for n in range(4):
                j, half = n // 2, n % 2
                act.wait_ge(S("out_ready"), n + 1)
                act.activation(tiles(yT, 2)[:, j, 512 * half:512 * half + 512], bank[n][:], ACT.Copy).then_inc(S("out_rows"), 1)

        @block.vector
        def _(dve):
            steps = [0]

            def after(ins):
                steps[0] += 1
                ins.then_inc(S("dve_step"), 1)
                dve.wait_ge(S("dve_step"), steps[0])

            norms = [0]

            def norm_apply(src3, gain, layer_at, dst3, width):
                n = norms[0]
                for i in range(KT):
                    last = dve.scalar_tensor_tensor(out=dst3[:, i, :], in0=src3[:, i, :], scalar=vec(gain, layer_at + i),
                                                    in1=RSTD[:, 0:width], op0=ALU.mult, op1=ALU.mult)
                    last.then_inc(S("norm_out"), 1)
                return last

            def magnitude(dst, src):
                return dve.scalar_tensor_tensor(out=dst, in0=src, scalar=-1.0, in1=src, op0=ALU.mult, op1=ALU.max)

            def wait_rstd():
                norms[0] += 1
                dve.wait_ge(S("norm_rstd"), norms[0])

            ht3, u3 = tiles(hT[:], KT), tiles(uT, KT)
            dve.memset(eps, EPS).then_inc(S("eps_ready"), 1)
            dve.memset(zrow[0:8], 0.0).then_inc(S("zeros_ready"), 1)
            dve.wait_ge(S("logit_landed"), 16)
            magnitude(lgt[:, 0:8], lgt[:, 8:16]).then_inc(S("magnitudes"), 1)
            dve.wait_ge(S("log_terms"), 1)
            dve.scalar_tensor_tensor(out=lg, in0=lgt[:, 8:16], scalar=0.0, in1=lgt[:, 0:8], op0=ALU.min,
                                     op1=ALU.subtract).then_inc(S("lg_ready"), 1)
            for i in range(1, KT, 2):
                dve.wait_ge(S("xt_ready"), i + 1)
                dve.tensor_copy(ht3[:, i, :], bank[i % 4][:, 0:T]).then_inc(S("xt_taken_dve"), 1)
            dve.wait_ge(S("vec_ready"), 1)
            for j, n in enumerate(VEC_COUNT):
                last = dve.tensor_copy(VC[:, P * j:P * j + n], bank[4][:, P * j:P * j + n])
            after(last)
            qkp, qk = tiles(QKP, 8), tiles(QK, 8)
            dve.memset(qkp[:, :, 0:PAD], 0.0).then_inc(S("pads_ready"), 1)
            dve.memset(qkp[:, :, PAD + T:2 * PAD + T], 0.0).then_inc(S("pads_ready"), 1)
            dve.tensor_scalar(half_a, VC[:, 256:264], 0.5, None, ALU.mult)
            dve.tensor_scalar(half_i, VC[:, 264:272], 0.5, None, ALU.mult).then_inc(S("half_bias"), 1)
            lam = VC[:, P + VEC_AT["c_lam_2"][1]:P + VEC_AT["c_lam_2"][1] + 8]
            magnitude(lamt[:, 0:8], lam).then_inc(S("magnitudes"), 1)
            wait_rstd()
            norm_apply(ht3, "mix_norm_g", 0, u3, T)

            dve.wait_ge(S("gates_ready"), 2)
            dve.wait_ge(S("bias_landed"), 64)
            dve.tensor_scalar(li[0:8], bank[4][0:8, 0:T], b_i, None, ALU.add).then_inc(S("gates_taken"), 1)
            dve.tensor_scalar(lf[0:8], bank[5][0:8, 0:T], b_f, None, ALU.add).then_inc(S("gates_taken"), 1)
            dve.wait_ge(S("gates_taken"), 2)
            magnitude(rowt[0:8], lf[0:8]).then_inc(S("magnitudes"), 1)
            dve.wait_ge(S("log_terms"), 2)
            dve.wait_ge(S("zeros_ready"), 1)
            after(dve.scalar_tensor_tensor(out=lf[0:8], in0=lf[0:8], scalar=0.0, in1=rowt[0:8], op0=ALU.min, op1=ALU.subtract))
            dve.tensor_tensor_scan(Bf[0:8], lf[0:8], zrow[0:8], 0.0, ALU.add, ALU.add)
            after(dve.tensor_tensor_scan(Bb[0:8, ::-1], lf[0:8, ::-1], zrow[0:8], 0.0, ALU.add, ALU.add))
            dve.wait_ge(S("tables_landed"), 7 * 16)
            after(dve.tensor_scalar(Bf[0:8], Bf[0:8], dirs[:, 0:1], None, ALU.mult))
            after(dve.scalar_tensor_tensor(out=Bf[0:8], in0=Bb[0:8], scalar=dirs[:, 1:2], in1=Bf[0:8], op0=ALU.mult, op1=ALU.add))
            dve.tensor_tensor(Bb[0:8], li[0:8], Bf[0:8], ALU.subtract).then_inc(S("gate_rows_ready"), 1)
            dve.wait_ge(S("gate_rows_ready"), 1)
            dve.tensor_tensor_scan(sf[0:8], Bb[0:8], Bb[0:8], 0.0, ALU.max, ALU.max)
            after(dve.tensor_tensor_scan(li[0:8, ::-1], Bb[0:8, ::-1], Bb[0:8, ::-1], 0.0, ALU.max, ALU.max))
            after(dve.tensor_scalar(sf[0:8], sf[0:8], dirs[:, 0:1], None, ALU.mult))
            after(dve.scalar_tensor_tensor(out=sf[0:8], in0=li[0:8], scalar=dirs[:, 1:2], in1=sf[0:8], op0=ALU.mult, op1=ALU.add))
            dve.tensor_tensor(Mr[0:8], Bf[0:8], sf[0:8], ALU.add).then_inc(S("stab_ready"), 1)

            sq8 = tiles(SQ[:], 8)

            def silu(i):
                dve.wait_ge(S("conv_tanh"), i + 1)
                dve.scalar_tensor_tensor(out=qk[:, i, :], in0=sq8[:, i, :], scalar=1.0, in1=qk[:, i, :], op0=ALU.add,
                                         op1=ALU.mult).then_inc(S("qk_ready"), 1)

            for i in range(8):
                dve.wait_ge(S("proj_taken_act"), i + 1)
                after(dve.tensor_scalar(qk[:, i, :], qkp[:, i, 0:T], vec("conv_w", i), vec("conv_b", i), ALU.mult, ALU.add))
                for tap in range(1, 5):
                    ins = dve.scalar_tensor_tensor(out=qk[:, i, :], in0=qkp[:, i, tap:tap + T], scalar=vec("conv_w", 8 * tap + i),
                                                   in1=qk[:, i, :], op0=ALU.mult, op1=ALU.add)
                    if tap < 4:
                        after(ins)
                ins.then_inc(S("conv_ready"), 1)
                if i:
                    silu(i - 1)
            silu(7)

            dve.wait_ge(S("log_terms"), 3)
            after(dve.scalar_tensor_tensor(out=n2sp, in0=lam, scalar=0.0, in1=lamt[:, 0:8], op0=ALU.min, op1=ALU.subtract))
            dve.tensor_scalar(n2sp, n2sp, 2.0, None, ALU.mult).then_inc(S("lru_rate"), 1)

            def unit_args(n):
                h, d = n // 2, n % 2
                r = 4 * d + h
                pt = tiles(SQ[:, (n % 2) * 816:(n % 2 + 1) * 816], TT)
                dve.wait_ge(S("stab_bcast"), n + 1)
                if n >= 2:
                    dve.wait_ge(S("num_ready"), n - 1)
                for j in range(TT):
                    if d == 0:
                        lo, hi = P * j, T
                        bar = bar_fwd[0:ROWS[j], 0:T - P * j]
                    else:
                        lo, hi = 0, min(T, P * (j + 1))
                        bar = bar_bwd[0:ROWS[j], 256 - P * j:256 - P * j + hi]
                    last = dve.scalar_tensor_tensor(out=pt[0:ROWS[j], j, lo:hi], in0=bank[7][0:ROWS[j], lo:hi],
                                                    scalar=acol[0:ROWS[j], 8 * j + r:8 * j + r + 1], in1=bar,
                                                    op0=ALU.subtract, op1=ALU.max)
                last.then_inc(S("args_ready"), 1)

            def unit_probs(n):
                h, d = n // 2, n % 2
                pt = tiles(SQ[:, (n % 2) * 816:(n % 2 + 1) * 816], TT)
                dve.wait_ge(S("unit_exps"), n + 1)
                dve.wait_ge(S("m_scores"), h + 1)
                for j in range(TT):
                    lo, hi = (P * j, T) if d == 0 else (0, min(T, P * (j + 1)))
                    v = pt[0:ROWS[j], j, lo:hi]
                    last = dve.scalar_tensor_tensor(out=v, in0=v, scalar=MLSTM_C, in1=bank[4 + j][0:ROWS[j], lo:hi],
                                                    op0=ALU.mult, op1=ALU.mult)
                last.then_inc(S("m_probs"), 1)

            dve.wait_ge(S("rotary_landed"), 48)
            dve.wait_ge(S("qk_ready"), 8)
            for n in range(8):
                src = tiles(rqT if n < H else rkT, H)[:, n % H, :]
                tmp = SQ[:, (n % 2) * T:(n % 2 + 1) * T]
                dve.wait_ge(S("rotary_ready"), n + 1)
                dve.tensor_tensor(tmp, bank[7][:, 0:T], sinT, ALU.mult).then_inc(S("rotary_taken"), 1)
                after(dve.tensor_tensor(src, src, cosT, ALU.mult))
                dve.wait_ge(S("rotary_taken"), n + 1)
                dve.tensor_tensor(src, src, tmp, ALU.add).then_inc(S("rot_out"), 1)

            dve.wait_ge(S("acol_ready"), 1)
            for j in range(TT):
                last = dve.tensor_copy(acol[0:ROWS[j], 8 * j:8 * j + 8], bank[3][0:ROWS[j], 8 * j:8 * j + 8])
            last.then_inc(S("acol_taken"), 1)
            dve.wait_ge(S("acol_taken"), 1)

            dve.wait_ge(S("rot_out"), 8)
            unit_args(0)
            for n in range(8):
                if n < 7:
                    unit_args(n + 1)
                unit_probs(n)
            dve.wait_ge(S("floor_ready"), 1)
            dve.wait_ge(S("num_ready"), 8)
            after(dve.tensor_copy(li[0:8], bank[3][0:8, 0:T]))
            after(magnitude(rowt[0:8], li[0:8]))
            after(dve.tensor_tensor(rowt[0:8], rowt[0:8], Mr[0:8], ALU.max))
            after(dve.reciprocal(rowt[0:8], rowt[0:8]))
            dve.tensor_scalar(rowt[0:8], rowt[0:8], 0.5, None, ALU.mult).then_inc(S("recip_ready"), 1)
            num3 = tiles(NUM, 8)
            dve.wait_ge(S("num_taken"), 8)
            for r in range(8):
                dve.wait_ge(S("recip_bcast"), r + 1)
                dve.tensor_tensor(num3[:, r, :], num3[:, r, :], bank[2 + r % 2][:, 0:T], ALU.mult).then_inc(S("recip_taken"), 1)
            dve.wait_ge(S("recip_taken"), 8)
            after(dve.tensor_tensor(HM, NUM[:, 0:H * T], NUM[:, H * T:], ALU.add))
            dve.wait_ge(S("proj_taken_act"), 28)
            dve.scalar_tensor_tensor(out=HM, in0=moT, scalar=1.0, in1=HM, op0=ALU.add, op1=ALU.mult).then_inc(S("hm_ready"), 1)

            dec = DEC.rearrange("p (h i l) -> p h i l", h=H, i=TT)
            dve.wait_ge(S("decay_ready"), H * TT)
            for h in range(H):
                dve.wait_ge(S("r_scores"), h + 1)
                if h >= 2:
                    dve.wait_ge(S("ret_ready"), h - 1)
                pt = tiles(SQ[:, (h % 2) * 816:(h % 2 + 1) * 816], TT)
                for j in range(TT):
                    last = dve.tensor_tensor(pt[0:ROWS[j], j, :], dec[0:ROWS[j], h, j, :], bank[4 + j][0:ROWS[j], 0:T], ALU.mult)
                last.then_inc(S("r_probs"), 1)
            dve.wait_ge(S("rg_tanh"), 1)
            after(dve.scalar_tensor_tensor(out=rgT, in0=QK[:, 0:H * T], scalar=1.0, in1=rgT, op0=ALU.add, op1=ALU.mult))

            def head_norm(src, n, gain, out_tile):
                s3 = tiles(src, H)
                dve.wait_ge(S("hn_mean"), n + 1)
                for h in range(H):
                    last = dve.scalar_tensor_tensor(out=s3[:, h, :], in0=bank[4 + h][:, 0:T], scalar=-1.0 / P, in1=s3[:, h, :],
                                                    op0=ALU.mult, op1=ALU.add)
                last.then_inc(S("hn_centred"), 1)
                dve.wait_ge(S("hn_rstd"), n + 1)
                rs = tiles(QK[:, H * T:2 * H * T], H)
                for h in range(H):
                    last = dve.scalar_tensor_tensor(out=u3[:, out_tile + h, :], in0=s3[:, h, :], scalar=vec(gain, h), in1=rs[:, h, :],
                                                    op0=ALU.mult, op1=ALU.mult)
                return last

            after(head_norm(RET, 0, "ret_gn_g", 0))
            dve.scalar_tensor_tensor(out=uT[:, 0:H * T], in0=uT[:, 0:H * T], scalar=0.5, in1=rgT, op0=ALU.mult,
                                     op1=ALU.mult).then_inc(S("y_ready"), 1)
            head_norm(HM, 1, "mlstm_gn_g", H).then_inc(S("y_ready"), 1)

            for i in range(KT):
                k = A_OUT[i]
                proj_ready(dve, k)
                dve.tensor_tensor(ht3[:, i, :], ht3[:, i, :], bank[pj.entries[k][0]][:, 0:T], ALU.add)\
                   .then_inc(S("proj_taken_dve"), 1)

            wait_rstd()
            norm_apply(ht3, "ffn_norm_g", 0, tiles(u2, KT), T)
            dve.wait_ge(S("router_ready"), 1)
            b3 = bank[4][:, 0:TT * EXP].rearrange("p (j e) -> p j e", j=TT)
            dve.tensor_reduce(smax[:, 0:2], b3[:, 0:2, :], AX.X, ALU.max, negate=True).then_inc(S("router_max"), 1)
            dve.tensor_reduce(smax[0:ROWS[2], 2:3], b3[0:ROWS[2], 2:3, :], AX.X, ALU.max, negate=True).then_inc(S("router_max"), 1)
            dve.wait_ge(S("router_exps"), TT)
            dve.reciprocal(ssum[:, 0:2], ssum[:, 0:2])
            after(dve.reciprocal(ssum[0:ROWS[2], 2:3], ssum[0:ROWS[2], 2:3]))
            a3 = tiles(aff, TT)
            for j in range(TT):
                last = dve.tensor_scalar(a3[0:ROWS[j], j, :], a3[0:ROWS[j], j, :], ssum[0:ROWS[j], j:j + 1], None, ALU.mult)
            last.then_inc(S("aff_ready"), 1)
            dve.wait_ge(S("affT_ready"), 1)
            after(dve.tensor_copy(affW[0:EXP], bank[5][0:EXP, 0:T]))
            ids = idxs.bitcast(U32)
            for r in range(5):
                c8 = slice(8 * r, 8 * r + 8)
                after(dve.max(vals[0:EXP, c8], affW[0:EXP]))
                after(dve.max_index(ids[0:EXP, c8], vals[0:EXP, c8], affW[0:EXP]))
                after(dve.match_replace(affW[0:EXP], vals[0:EXP, c8], affW[0:EXP], -1.0))
            dve.memset(idx2[0:EXP], 0.0)
            after(dve.memset(val2[0:EXP], 0.0))
            for at in (0, MPAD):
                dve.tensor_copy(idx2[0:EXP, at:at + CAP], ids[0:EXP, 0:CAP])
                last = dve.tensor_copy(val2[0:EXP, at:at + CAP], vals[0:EXP, 0:CAP])
            after(last)
            dve.wait_ge(S("own_landed"), 16)
            dve.memset(xs, 0.0).then_inc(S("xs_pads"), 1)
            own3, sp3 = tiles(own, EXP), tiles(spread, EXP)
            dve.tensor_tensor(sp3[0:EXP], own3[0:EXP], idx2[0:EXP, 0:CAP].rearrange("p (a c) -> p a c", a=1).to_broadcast([EXP, EXP, CAP]),
                              ALU.mult).then_inc(S("spread_ready"), 1)
            wait_rstd()
            m3 = tiles(mT, KT)
            for L in range(2):
                norm_apply(m3, "g_mem_2", 8 * L, tiles(mm[:, 2048 * L:2048 * L + 2048], KT), 256)
            dve.wait_ge(S("choice_ready"), 1)
            dve.tensor_copy(idxT, bank[4][:, 0:EXP])
            after(dve.tensor_copy(gT, bank[4][:, EXP:2 * EXP]))
            st3 = ST.rearrange("p (j s) -> p j s", j=TT)
            dve.memset(st3[:, :, EXP * CAP:], 0.0)
            for j in range(TT):
                dve.tensor_scalar(st3[:, j, 0:272], bank[5][:, 0:272], iota_col[:, j:j + 1], None, ALU.is_equal)
                dve.tensor_scalar(st3[:, j, 272:544], bank[6][:, 0:272], iota_col[:, j:j + 1], None, ALU.is_equal)\
                   .then_inc(S("gather_ready"), 1)

            dve.wait_ge(S("norm_sum"), 3)
            dve.wait_ge(S("iota_landed"), 16)
            dve.memset(Se, 0.0).then_inc(S("se_ready"), 1)

            def scatter_add(e):
                for i in range(KT):
                    dve.wait_ge(S("scatter_ready"), 8 * e + i + 1)
                    dve.tensor_tensor(ht3[:, i, :], ht3[:, i, :], bank[7][:, 0:T], ALU.add)\
                       .then_inc(S("scatter_taken"), 1)

            with dve.Fori(0, EXP) as e:
                for c, (lo, hi) in enumerate(HCHUNKS):
                    v = th[:, HF * lo:HF * hi]
                    dve.wait_ge(S("gate_tanh"), 3 * e + c + 1)
                    dve.scalar_tensor_tensor(out=v, in0=v, scalar=1.0, in1=bank[c][:, 0:HF * (hi - lo)], op0=ALU.add, op1=ALU.mult)\
                       .then_inc(S("gu_ready"), 1)
                scatter_add(e)
                dve.tensor_scalar(Se, iota_row, idxT[:, bass.ds(e, 1)], gT[:, bass.ds(e, 1)], ALU.is_equal, ALU.mult)\
                   .then_inc(S("se_ready"), 1)
                dve.wait_ge(S("up_used"), 8 * e + 8)
                dve.wait_ge(S("gu_ready"), 3 * e + 3)
                for c, (lo, hi) in enumerate(HCHUNKS):
                    v = th[:, HF * lo:HF * hi]
                    dve.scalar_tensor_tensor(out=v, in0=v, scalar=0.5, in1=bank[3 + c][:, 0:HF * (hi - lo)], op0=ALU.mult, op1=ALU.mult)\
                       .then_inc(S("hid_ready"), 1)
            scatter_add(EXP)

            x3, hn3, y3 = tiles(xT, KT), tiles(hN, KT), tiles(yT, KT)
            wait_rstd()
            norm_apply(ht3[:, :, META:T], "final_norm_g", 0, x3, 256)

            def pre_norm(gain, L):
                wait_rstd()
                norm_apply(x3, gain, 8 * L, hn3, 256)

            scaled = [0]

            def post_norm(gain, L):
                wait_rstd()
                for i in range(KT + 1):
                    if i < KT:
                        scaled[0] += 1
                        dve.scalar_tensor_tensor(out=hn3[:, i, :], in0=hn3[:, i, :], scalar=vec(gain, 8 * L + i),
                                                 in1=RSTD[:, 0:256], op0=ALU.mult, op1=ALU.mult).then_inc(S("post_scaled"), 1)
                    if i:
                        dve.wait_ge(S("post_scaled"), scaled[0] - (i < KT))
                        dve.tensor_tensor(x3[:, i - 1, :], x3[:, i - 1, :], hn3[:, i - 1, :], ALU.add).then_inc(S("norm_out"), 1)

            def att_normalise(n, buf):
                s = slice(2 * (n % 2), 2 * (n % 2) + 2)
                dve.wait_ge(S("att_exps"), 2 * n + 2)
                after(dve.reciprocal(ssum[:, s], ssum[:, s]))
                for qi in range(2):
                    v = buf[:, 256 * qi:256 * qi + 256]
                    last = dve.tensor_scalar(v, v, ssum[:, 2 * (n % 2) + qi:2 * (n % 2) + qi + 1], None, ALU.mult)
                last.then_inc(S("att_probs"), 1)

            splits = [0]

            def split_weights_to(end):
                while splits[0] < len(split_chunks) and split_chunks[splits[0]] < end:
                    n = splits[0]
                    k = split_chunks[n]
                    chunk_landed(dve, C_CHUNKS[k])
                    if n >= PSLOTS:
                        dve.wait_ge(*chunk_used[split_chunks[n - PSLOTS]])
                    dve.tensor_copy(part(highs, n), raw_slot(k)).then_inc(S("weights_high"), 1)
                    dve.wait_ge(S("weights_high"), n + 1)
                    cols = slice(256 * POOL_TILES, SLOT)
                    dve.tensor_tensor(part(lows, n)[:, cols], raw_slot(k)[:, cols], part(highs, n)[:, cols], ALU.subtract)\
                       .then_inc(S("weights_low_dve"), 1)
                    splits[0] += 1

            for L in range(2):
                pre_norm("g_mix_pre_2", L)
                if L == 0:
                    dve.wait_ge(S("fox_logits"), 1)
                    after(dve.tensor_scalar(frow[0:8], bank[6][0:8, 0:256], b_fox, None, ALU.add))
                    magnitude(frow2[0:8], frow[0:8]).then_inc(S("magnitudes"), 1)
                    dve.memset(frow3[0:8], 0.0)
                    dve.wait_ge(S("log_terms"), 4)
                    after(dve.scalar_tensor_tensor(out=frow2[0:8], in0=frow[0:8], scalar=0.0, in1=frow2[0:8], op0=ALU.min,
                                                   op1=ALU.subtract))
                    dve.tensor_tensor_scan(frow[0:8], frow2[0:8], frow3[0:8], 0.0, ALU.add, ALU.add).then_inc(S("fox_row_ready"), 1)
                    bar3 = tiles(fox_bar, 2)
                    nm3 = tiles(fox_nm, 2)
                    dve.wait_ge(S("fox_tables"), 32)

                    def fox_args(n):
                        dve.wait_ge(S("att_scores"), n + 1)
                        if n >= 2:
                            dve.wait_ge(S("pt_ready"), n - 1)
                        cum = bank[6][:, 0:256].rearrange("p (a c) -> p a c", a=1).to_broadcast([P, 2, 256])
                        after(dve.tensor_tensor(nm3, bar3, cum, ALU.subtract))
                        ins = dve.scalar_tensor_tensor(out=fox_e[n % 2], in0=bank[5][:], scalar=0.125, in1=fox_nm, op0=ALU.mult, op1=ALU.add)
                        ins.then_inc(S("att_scores_taken"), 1)
                        dve.wait_ge(S("att_scores_taken"), n + 1)
                        dve.tensor_reduce(smax[:, 2 * (n % 2):2 * (n % 2) + 2], tiles(fox_e[n % 2], 2), AX.X, ALU.max, negate=True)\
                           .then_inc(S("att_max"), 1)

                    fox_args(0)
                    for n in range(8):
                        if n < 7:
                            fox_args(n + 1)
                        att_normalise(n, fox_e[n % 2])
                        if n == 7:
                            cu3, fu3, fb3 = tiles(cu, 4), tiles(fu, 4), tiles(fb, 4)
                            dve.memset(cu3[:, :, 0:2], 0.0)
                            dve.wait_ge(S("proj_taken_act"), taken_after("act", C["ab", 11]))
                            after(dve.tensor_tensor(cu3[:, :, 2:258], tiles(fc, 4), fu3, ALU.mult))
                            for i in range(4):
                                ins = dve.tensor_scalar(fu3[:, i, :], cu3[:, i, 0:256], vec("ab_conv_w_2", i), None, ALU.mult)
                            after(ins)
                            for tap in (1, 2):
                                for i in range(4):
                                    ins = dve.scalar_tensor_tensor(out=fu3[:, i, :], in0=cu3[:, i, tap:tap + 256],
                                                                   scalar=vec("ab_conv_w_2", 4 * tap + i), in1=fu3[:, i, :],
                                                                   op0=ALU.mult, op1=ALU.add)
                                after(ins)
                            dve.tensor_tensor(yT[:, 1024:2048], fu, fb, ALU.mult).then_inc(S("mixed"), 1)
                    dve.wait_ge(S("att_out_taken"), 4)
                    dve.memset(small[0:8, 180:181], 0.0).then_inc(S("mixed"), 1)
                else:
                    lup3, lu3, lg3 = tiles(lup, KT), tiles(lu, KT), tiles(lgate, KT)
                    ta3, ti3, lr3, sq3 = tiles(ta, KT), tiles(ti, KT), tiles(lr, KT), tiles(SQ[:, 0:2048], KT)
                    dve.memset(lup3[:, :, 0:3], 0.0).then_inc(S("lru_pads"), 1)
                    for k in range(4):
                        dve.wait_ge(S("proj_taken_act"), taken_after("act", C["c_in", k]))
                        for i in (2 * k, 2 * k + 1):
                            after(dve.tensor_scalar(lu3[:, i, :], lup3[:, i, 0:256], vec("c_conv_w_2", i), vec("c_conv_b_2", i),
                                                    ALU.mult, ALU.add))
                            for tap in (1, 2, 3):
                                ins = dve.scalar_tensor_tensor(out=lu3[:, i, :], in0=lup3[:, i, tap:tap + 256],
                                                               scalar=vec("c_conv_w_2", 8 * tap + i), in1=lu3[:, i, :],
                                                               op0=ALU.mult, op1=ALU.add)
                                if tap < 3:
                                    after(ins)
                            ins.then_inc(S("lru_conv"), 1)
                    dve.wait_ge(S("lru_tanh"), 8)
                    dve.wait_ge(S("proj_taken_act"), taken_after("act", C["c_gates", 7]))
                    after(dve.tensor_scalar(lr, ta, -1.0, 1.0, ALU.mult, ALU.add))
                    after(dve.reciprocal(lr, lr))
                    after(dve.scalar_tensor_tensor(out=ti, in0=ti, scalar=1.0, in1=lu, op0=ALU.add, op1=ALU.mult))
                    after(dve.tensor_tensor(ti, ti, lr, ALU.mult))
                    after(dve.scalar_tensor_tensor(out=lr, in0=ta, scalar=1.0, in1=lr, op0=ALU.add, op1=ALU.mult))
                    dve.tensor_scalar(ta, ta, -1e-30, None, ALU.min).then_inc(S("lru_denom"), 1)
                    dve.wait_ge(S("gelu_square"), 1)
                    after(dve.tensor_scalar(SQ[:, 0:2048], SQ[:, 0:2048], 0.044715, 1.0, ALU.mult, ALU.add))
                    dve.tensor_tensor(SQ[:, 0:2048], SQ[:, 0:2048], lgate, ALU.mult).then_inc(S("gelu_cubic"), 1)
                    dve.wait_ge(S("gelu_tanh"), 1)
                    after(dve.scalar_tensor_tensor(out=SQ[:, 0:2048], in0=SQ[:, 0:2048], scalar=1.0, in1=lgate, op0=ALU.add, op1=ALU.mult))
                    dve.wait_ge(S("lru_sqrt"), 1)
                    after(dve.tensor_tensor(ti, ti, ta, ALU.mult))
                    for i in range(KT):
                        last = dve.tensor_tensor_scan(y3[:, i, :], lr3[:, i, :], ti3[:, i, :], 0.0, ALU.mult, ALU.add)
                    after(last)
                    dve.scalar_tensor_tensor(out=yT, in0=SQ[:, 0:2048], scalar=0.5, in1=yT, op0=ALU.mult, op1=ALU.mult)\
                       .then_inc(S("mixed"), 1)
                post_norm("g_mix_post_2", L)
                pre_norm("g_cross_pre_2", L)
                n0 = 8 + 4 * L

                def cross_max(n):
                    dve.wait_ge(S("att_scores"), n + 1)
                    s = slice(2 * (n % 2), 2 * (n % 2) + 2)
                    if n > n0:
                        dve.wait_ge(S("att_exps"), 2 * n)
                    after(dve.tensor_reduce(smax[:, s], tiles(bank[5][:], 2), AX.X, ALU.max, negate=True))
                    dve.tensor_scalar(smax[:, s], smax[:, s], 1.0 / 16, None, ALU.mult).then_inc(S("att_max"), 1)

                for n in range(n0, n0 + 4):
                    cross_max(n)
                    att_normalise(n, att_e[n % 2])
                ffn_at = c_index[f"gate{L}", 0]
                split_weights_to(ffn_at + 4)
                post_norm("g_cross_post_2", L)
                pre_norm("g_ffn_pre_2", L)
                dve.wait_ge(S("norm_out"), 40 + 8 * 6 * L + 8 * 6 - 8)
                after(dve.tensor_copy(x_high, hN))
                dve.tensor_tensor(x_low, hN, x_high, ALU.subtract).then_inc(S("input_split"), 1)
                for k in range(FT // 2):
                    n = L * (FT // 2) + k
                    dve.wait_ge(S("ffn_tanh"), n + 1)
                    kg, ku = C["gate", L, k], C["up", L, k]
                    dve.scalar_tensor_tensor(out=fth[k % 2], in0=fth[k % 2], scalar=1.0, in1=bank[pj.entries[kg][0]][:],
                                             op0=ALU.add, op1=ALU.mult).then_inc(S("proj_taken_dve"), 1)
                    dve.wait_ge(S("proj_taken_dve"), taken_after("dve", kg))
                    proj_ready(dve, ku)
                    hid_k = fth[k % 2]
                    dve.scalar_tensor_tensor(out=hid_k, in0=hid_k, scalar=0.5, in1=bank[pj.entries[ku][0]][:],
                                             op0=ALU.mult, op1=ALU.mult).then_inc(S("proj_taken_dve"), 1)
                    dve.wait_ge(S("proj_taken_dve"), taken_after("dve", ku))
                    low, high = (x[:, 512 * k:512 * k + 512] for x in (fhid_low, fhid_high))
                    after(dve.tensor_copy(high, hid_k))
                    dve.tensor_tensor(low, hid_k, high, ALU.subtract).then_inc(S("hidden_split"), 1)
                    split_weights_to(ffn_at + 6 + 2 * k)
                split_weights_to(ffn_at + FT + FT // 2)
                post_norm("g_ffn_post_2", L)


_INS = ["x", "meta_tokens", "mix_norm_g", "w_in", "b_gates", "conv_w", "conv_b", "ret_decay_logit", "ret_gn_g",
        "mlstm_gn_g", "w_out", "ffn_norm_g", "w_router", "w_gate", "w_up", "w_down", "final_norm_g", "mem_2",
        "g_mix_pre_2", "g_mix_post_2", "g_cross_pre_2", "g_mem_2", "g_cross_post_2", "g_ffn_pre_2",
        "g_ffn_post_2", "w_xq_2", "w_xkv_2", "w_xo_2", "w_ffn_gu_2", "w_ffn_down_2", "ab_w_in_2", "ab_b_f_2",
        "ab_conv_w_2", "ab_w_out_2", "c_w_in_2", "c_conv_w_2", "c_conv_b_2", "c_w_a_2", "c_b_a_2", "c_w_i_2",
        "c_b_i_2", "c_lam_2", "c_w_out_2"]


def kernel(**inputs):
    import concourse.bacc as _bacc
    from concourse.bass_utils import run_bass_kernel_spmd as _run

    nc = _bacc.Bacc("TRN2", target_bir_lowering=False, num_devices=1)
    arrays, tensors = {}, {}
    for name, a in [(n, inputs[n]) for n in _INS] + list(constants().items()):
        a = np.ascontiguousarray(a)
        arrays[f"in_{name}_dram"] = a
        tensors[name] = nc.dram_tensor(f"in_{name}_dram", a.shape, mybir.dt.from_np(a.dtype), kind="ExternalInput").ap()
    out = nc.dram_tensor("out_0_dram", (1, SEQ, D), F32, kind="ExternalOutput").ap()
    build(nc, tensors, out)
    r = _run(nc, [arrays], core_ids=[0])
    return r.results[0]["out_0_dram"]
```

```python
from contextlib import ExitStack

import numpy as np

import concourse.bass as bass
from concourse import mybir

P = 128
F32 = mybir.dt.float32
F32R = mybir.dt.float32r
U32 = mybir.dt.uint32
ALU = mybir.AluOpType
ACT = mybir.ActivationFunctionType
AX = mybir.AxisListType

D = 1024
KT = D // P
SEQ = 256
META = 16
T = META + SEQ
TT = (T + P - 1) // P
ROWS = [min(P, T - P * i) for i in range(TT)]
H = 4
EXP = 16
CAP = 2 * T // EXP
DFF = 2816
FT = DFF // P
EPS = 1e-6
ARENA = 24960
BIG = 1e30
PAD = 2

SLOTS = 11
SLOT = KT * 256
CSLOTS = 4
PSLOTS = 3
ESLOTS = 8
DOWN_END = [-(-DFF * (g + 1) // D) for g in range(ESLOTS)]
DOWN_SLOT = [(D * (j + 1) - 1) // DFF for j in range(FT)]
HF = FT // 2
HP = 46
HCHUNKS = [(p, min(P, p + HP)) for p in range(0, P, HP)]
MPAD = 64

VEC_ROWS = [
    [("mix_norm_g", 8), ("ffn_norm_g", 8), ("final_norm_g", 8), ("conv_w", 40), ("conv_b", 8),
     ("ret_gn_g", 4), ("mlstm_gn_g", 4), ("g_mem_2", 16), ("g_mix_pre_2", 16), ("g_mix_post_2", 16)],
    [("g_cross_pre_2", 16), ("g_cross_post_2", 16), ("g_ffn_pre_2", 16), ("g_ffn_post_2", 16),
     ("ab_conv_w_2", 12), ("c_conv_w_2", 32), ("c_conv_b_2", 8), ("c_lam_2", 8)],
    [("c_b_a_2", 8), ("c_b_i_2", 8)],
]
VEC_AT = {}
for _tile, _rows in enumerate(VEC_ROWS):
    _at = 0
    for _name, _n in _rows:
        VEC_AT[_name] = (_tile, _at, _n)
        _at += _n
VEC_COUNT = [sum(n for _, n in rows) for rows in VEC_ROWS]


def constants():
    p = np.arange(P)[:, None]
    f = np.float32
    c = {}
    c["ident"] = np.eye(P, dtype=f)
    col = np.arange(256 + T)[None, :] - 256
    c["dist_fwd"] = np.maximum(col - p, 0).astype(f)
    c["dist_bwd"] = np.maximum(p - col, 0).astype(f)
    c["bar_fwd"] = np.where(np.arange(T)[None, :] >= p, 0, BIG).astype(f)
    c["bar_bwd"] = np.where(np.arange(384)[None, :] - 256 <= p, 0, BIG).astype(f)
    half = 64
    inv = 10000.0 ** (-np.arange(half, dtype=f) / half)
    ang = (np.arange(T, dtype=f)[:, None] * inv[None, :].astype(f)).astype(f)
    c["cos"] = np.concatenate([np.cos(ang).T, np.cos(ang).T], 0).astype(f)
    c["sin"] = np.concatenate([np.sin(ang).T, np.sin(ang).T], 0).astype(f)
    rot = np.zeros((P, P), f)
    rot[np.arange(64) + 64, np.arange(64)] = -1
    rot[np.arange(64), np.arange(64) + 64] = 1
    c["rot"] = rot
    pick = np.zeros((8, 8, P), f)
    for r in range(8):
        pick[r, r, :] = 1
    c["pick"] = pick.reshape(8, 8 * P)
    into = np.zeros((P, 8, 8), f)
    for r in range(8):
        into[:, r, r] = 1
    c["into"] = into.reshape(P, 64)
    c["iota_row"] = np.tile(np.arange(T, dtype=f), (P, 1))
    c["iota_col"] = np.arange(P, dtype=f)[:, None] + 128 * np.arange(TT, dtype=f)[None, :]
    own = np.zeros((EXP, EXP, CAP), f)
    for r in range(EXP):
        own[r, r] = 1
    c["own"] = own.reshape(EXP, EXP * CAP)
    c["dirs"] = np.stack([np.arange(8) < 4, np.arange(8) >= 4], 1).astype(f)
    bar = np.zeros((P, 2, 256), f)
    for i in range(2):
        bar[:, i] = np.where(np.arange(256)[None, :] <= p + 128 * i, 0, -BIG)
    c["bar_causal"] = bar.reshape(P, 512)
    return c


def build(nc, t, out):
    with ExitStack() as ctx:
        BASE = {}

        def sb(name, cols, dt=F32):
            made = ctx.enter_context(nc.sbuf_tensor(name, [P, cols], dt))
            BASE[name] = nc.sbuf_base - 4 * cols
            return made

        sems = {}

        def S(name):
            if name not in sems:
                sems[name] = ctx.enter_context(nc.semaphore(name))
            return sems[name]

        bank = [ctx.enter_context(nc.psum_tensor(f"bank{i}", [P, 512], F32)) for i in range(8)]

        W = sb("weight_ring", SLOTS * SLOT)
        ident = sb("ident", P)
        ones = sb("ones", P)
        hT = sb("hT", KT * T)
        SQ = sb("squares", KT * T)
        RSTD = sb("rstd", T)
        VC = sb("vec_cols", 384)
        GW = sb("gate_w", KT * 16)
        RW = sb("router_w", KT * 16)
        small = sb("small", 192)
        Z = sb("arena", ARENA)

        def rounded(name, over, at, cols):
            offset = BASE[over] + 4 * at
            return nc.alloc_sbuf_tensor_at(name, [P, cols], F32R, offset=offset)[:]

        def vec(name, i):
            tile, at, n = VEC_AT[name]
            return VC[:, tile * P + at + i:tile * P + at + i + 1]

        cursor = [0]

        def z(cols, at=None):
            if at is None:
                at = cursor[0]
                cursor[0] += cols
            assert at + cols <= ARENA, (at, cols)
            return Z[:, at:at + cols]

        def tiles(ap, n):
            return ap.rearrange("p (t n) -> p t n", t=n)

        lg = small[:, 0:8]
        lgt = small[:, 8:24]
        b_i, b_f = small[0:8, 24:25], small[0:8, 25:26]
        dirs = small[0:8, 26:28]
        acol = small[:, 32:56]
        iota_col = small[:, 56:59]
        idxT = small[:, 64:80]
        gT = small[:, 80:96]
        smax = small[:, 96:104]
        ssum = small[:, 104:112]
        b_fox = small[0:8, 112:113]
        half_a, half_i = small[:, 120:128], small[:, 128:136]
        n2sp = small[:, 136:144]
        lamt = small[:, 144:152]
        n4sp = small[:, 152:160]
        eps = small[:, 184:185]

        uT = z(KT * T)
        QKP = z(8 * (T + 2 * PAD))
        NUM = QKP[:, 0:8 * T]
        QK = z(8 * T)
        mvT, moT, rqT, rkT, rvT, rgT = (z(H * T) for _ in range(6))
        mv, rv = z(TT * 512), z(TT * 512)
        xtok = Z[:, cursor[0] - 2 * TT * 512:cursor[0]]
        DEC = z(H * TT * T)
        dist_fwd, dist_bwd = z(256 + T), z(256 + T)
        bar_fwd, bar_bwd = z(T), z(384)
        cosT, sinT = z(T), z(T)
        pick = z(8 * P)
        rot = z(P)
        into = z(64)
        rows = [z(T) for _ in range(7)]
        assert cursor[0] <= ARENA, cursor[0]
        vrow = QKP[:, 0:384]
        li, lf, Bf, Bb, rowt, sf, Mr = rows
        zrow = Mr
        hm_rstd, hm_squares = NUM[:, 0:H * T], NUM[:, H * T:]
        ret_rstd = QK[:, H * T:2 * H * T]
        HM = mvT
        RET = rvT

        kT2 = z(2 * KT * 256, 0)
        v2 = z(2 * 2 * D, 4096)
        mm = z(2 * KT * 256, 8192)
        mwork = z(KT * 256, 12288)
        kvw = z(KT * 256, 14336)
        utok = z(TT * D, 16384)
        ST = z(TT * (EXP + 1) * CAP, 19456)
        STe = z(TT * CAP, 21192)
        xs = z(KT * MPAD, 21296)
        th = z(P * HF, 21808)
        hidT = z(P * HF, 23216)
        iota_row = z(T, 24624)
        aff = z(TT * EXP, 24896)
        u2 = uT
        memtok = z(2 * D, 4096)
        mT = z(KT * 256, 6144)
        o = 21808
        logitsT, affW, vals, idxs, own, spread, idx2, val2 = (
            z(n, o + at) for n, at in ((T, 0), (T, 272), (40, 544), (40, 584), (544, 624), (544, 1168), (P, 1712), (P, 1840)))
        ys = SQ[:, 0:512]
        Se = SQ[:, 512:512 + T]

        xT = z(2048, 8192)
        hN = z(2048, 10240)
        yT = z(2048, 12288)
        work = [14336]

        def cz(cols):
            at = work[0]
            work[0] += cols
            return z(cols, at)

        fq, fk, fv, fb, fc, fu = (cz(1024) for _ in range(6))
        cu = cz(4 * 258)
        fox_e = [cz(512), cz(512)]
        fox_nm = SQ[:, 0:512]
        fox_pt = [cz(512), cz(512)]
        fox_bar = SQ[:, 1280:1792]
        frow, frow2, frow3 = SQ[:, 512:768], SQ[:, 768:1024], SQ[:, 1024:1280]
        fpick = cz(8 * P)
        work[0] = 14336
        lgate, lu, ta, ti = cz(2048), cz(2048), cz(2048), cz(2048)
        lup = cz(8 * 259)
        lr = yT
        work[0] = 14336
        xq, xo = cz(2048), cz(2048)
        att_e = [cz(512), cz(512)]
        att_pt = [cz(512), cz(512)]
        work[0] = 14336
        work[0] = 12288
        cz(2 * FT * 256)
        fhid_high = rounded("hidden_high", "arena", 12288, FT * 256)
        fhid_low = rounded("hidden_low", "arena", 12288 + FT * 256, FT * 256)
        fth = [cz(512), cz(512)]

        A_CHUNKS = [("w_in", c) for c in (8, 9, 10, 11, 12, 13, 0, 1, 2, 3, 4, 5, 14, 15, 6, 7)]
        A_CHUNKS += [("w_out", c) for c in range(4)]
        NA = len(A_CHUNKS)

        C_CHUNKS = []
        for L in range(2):
            if L == 0:
                C_CHUNKS += [("ab", c) for c in range(12)]
                C_CHUNKS += [("ab_out", c) for c in range(4)]
            else:
                C_CHUNKS += [("c_in", c) for c in (4, 5, 6, 7, 0)] + [("c_a", 0), ("c_i", 0)] + [("c_in", c) for c in (1, 2, 3)]
                C_CHUNKS += [("c_out", c) for c in range(4)]
            C_CHUNKS += [(f"xq{L}", c) for c in range(4)] + [(f"xo{L}", c) for c in range(4)]
            for c in range(FT // 2):
                C_CHUNKS += [(f"gate{L}", c), (f"up{L}", c)]
            C_CHUNKS += [(f"down{L}", c) for c in range(FT // 2)]
        A_USES = [len([k for k in range(NA) if k % SLOTS == s]) for s in range(SLOTS)]
        B_USES = [3 * EXP if s < ESLOTS else 0 for s in range(SLOTS)]

        def landed(s):
            return S(f"ring_landed{s}")

        class Projections:

            def __init__(self):
                self.entries = []
                self.taken = {"act": 0, "dve": 0}
                self.last = {}

            def add(self, bank_no, taker):
                before = self.last.get(bank_no)
                self.entries.append((bank_no, taker, before))
                self.taken[taker] += 1
                self.last[bank_no] = (taker, self.taken[taker])
                return len(self.entries) - 1

        pj = Projections()
        A_FIRST = [pj.add(k % 2, "act") for k in range(32)]
        A_OUT = [pj.add(k % 4, "dve") for k in range(8)]

        C = {}
        for L in range(2):
            if L == 0:
                for k in range(12):
                    C["ab", k] = pj.add(k % 4, "act")
                for k in range(4):
                    C["mix_out", 0, k] = pj.add(k % 4, "act")
            else:
                for k in range(5):
                    C["c_in", k] = pj.add(k % 4, "act")
                for k in range(8):
                    C["c_gates", k] = pj.add(k % 4, "act")
                for k in range(5, 8):
                    C["c_in", k] = pj.add(k % 4, "act")
                for k in range(4):
                    C["mix_out", 1, k] = pj.add(k % 4, "act")
            for k in range(4):
                C["xq", L, k] = pj.add(k % 4, "act")
            for k in range(4):
                C["xo", L, k] = pj.add(k % 4, "act")
            for k in range(FT // 2):
                C["gate", L, k] = pj.add((2 * k) % 4, "dve")
                C["up", L, k] = pj.add((2 * k + 1) % 4, "dve")
            for k in range(4):
                C["down", L, k] = pj.add(k, "act")

        chunk_used = []
        for name, c in C_CHUNKS:
            L = int(name[-1]) if name[-1].isdigit() else None
            if name == "ab":
                entry = C["ab", c]
            elif name in ("ab_out", "c_out"):
                entry = C["mix_out", 0 if name == "ab_out" else 1, c]
            elif name == "c_in":
                entry = C["c_in", (c + 4) % 8]
            elif name in ("c_a", "c_i"):
                entry = C["c_gates", 3 if name == "c_a" else 7]
            elif name[:-1] == "down" and c < FT // 2 - 1:
                chunk_used.append((S("ffn_down_used"), L * (FT // 2 - 1) + c + 1))
                continue
            elif name[:-1] == "down":
                entry = C["down", L, 3]
            else:
                entry = C[name[:-1], L, c]
            chunk_used.append((S("proj_ready"), entry + 1))
        c_index = {key: k for k, key in enumerate(C_CHUNKS)}

        def is_split(k):
            name, c = C_CHUNKS[k]
            if name == "c_in":
                return c in (5, 6, 7, 0)
            return {"ab": 1 <= c <= 5, "ab_out": True, "c_out": True, "xq": c > 0, "xo": True, "gate": c > 0,
                    "up": True, "down": True}.get(name.rstrip("01"), False)

        split_chunks = [k for k in range(len(C_CHUNKS)) if is_split(k)]
        split_index = {k: n for n, k in enumerate(split_chunks)}
        POOL_TILES = 5

        def raw_slot(k):
            return W[:, (k % CSLOTS) * SLOT:(k % CSLOTS + 1) * SLOT]

        highs = rounded("weights_high_ring", "weight_ring", CSLOTS * SLOT, PSLOTS * SLOT)
        lows = rounded("weights_low_ring", "weight_ring", (CSLOTS + PSLOTS) * SLOT, PSLOTS * SLOT)
        x_high = rounded("input_high", "weight_ring", (CSLOTS + 2 * PSLOTS) * SLOT, SLOT)
        x_low_ffn = rounded("input_low_ffn", "squares", 0, SLOT)
        x_low_pre = rounded("input_low_pre", "arena", 12288, SLOT)
        x_low_out = rounded("input_low_out", "arena", 14336, SLOT)

        def part(ring, n):
            return ring[:, (n % PSLOTS) * SLOT:(n % PSLOTS + 1) * SLOT]

        def chunk_landed(eng, key):
            k = c_index[key]
            s = k % CSLOTS
            eng.wait_ge(landed(s), 16 * (A_USES[s] + B_USES[s] + k // CSLOTS + 1))
            return s

        def taken_after(who, k):
            return sum(1 for e in pj.entries[:k + 1] if e[1] == who)

        def pe_bank_free(pe, k):
            before = pj.entries[k][2]
            if before:
                pe.wait_ge(S(f"proj_taken_{before[0]}"), before[1])

        def proj_ready(eng, k):
            eng.wait_ge(S("proj_ready"), k + 1)

        UTOK_BANKS = [0, 1, 2, 3, 6, 4]
        MLSTM_C = 0.25 * float(P) ** -0.5

        block = ctx.enter_context(nc.Block())

        @block.sync
        def _(sp):
            x, meta = t["x"][0], t["meta_tokens"]
            xt = tiles(xtok, TT)
            sp.dma_start(xt[0:META, 0, :], meta).then_inc(S("x_landed"), 16)
            sp.dma_start(xt[META:P, 0, :], x[0:P - META, :]).then_inc(S("x_landed"), 16)
            sp.dma_start(xt[:, 1, :], x[P - META:2 * P - META, :]).then_inc(S("x_landed"), 16)
            sp.dma_start(xt[0:META, 2, :], x[2 * P - META:SEQ, :]).then_inc(S("x_landed"), 16)
            w_in = t["w_in"][0].rearrange("(t p) n -> p t n", p=P)
            w_out = t["w_out"][0].rearrange("(t p) n -> p t n", p=P)
            sp.dma_start(tiles(GW[:], KT), w_in[:, :, 4096:4112]).then_inc(S("gate_w_landed"), 16)
            for tile, group in enumerate(VEC_ROWS):
                for name, n in group:
                    at = VEC_AT[name][1]
                    src = t[name]
                    flat = src.rearrange(" ".join("abc"[:len(src.shape)]) + " -> (" + " ".join("abc"[:len(src.shape)]) + ")") \
                        if len(src.shape) > 1 else src
                    sp.dma_start(vrow[at:at + n, tile * P:(tile + 1) * P],
                                   flat.rearrange("(r f) -> r f", f=P)).then_inc(S("vec_landed"), 16)
            sp.wait_ge(S("vec_landed"), 16 * sum(len(g) for g in VEC_ROWS))
            for k, (name, c) in enumerate(A_CHUNKS):
                if k >= SLOTS:
                    sp.wait_ge(S("proj_ready"), 2 * (k - SLOTS + 1))
                src = w_in if name == "w_in" else w_out
                sp.dma_start(tiles(W[:, (k % SLOTS) * SLOT:(k % SLOTS + 1) * SLOT], KT),
                             src[:, :, 256 * c:256 * c + 256]).then_inc(landed(k % SLOTS), 16)
            sp.dma_start(tiles(RW[:], KT), t["w_router"][0].rearrange("(t p) n -> p t n", p=P))\
              .then_inc(S("router_w_landed"), 16)

            sp.wait_ge(S("gates_ready"), 2)
            sp.dma_start(tiles(GW[:, 0:64], KT), t["ab_w_in_2"][0].rearrange("(t p) n -> p t n", p=P)[:, :, 1536:1544])\
              .then_inc(S("fox_w_landed"), 16)

            def expert_slot(s):
                return W[:, s * DFF:(s + 1) * DFF]

            mem = t["mem_2"][0].rearrange("(i p) n -> p i n", p=P)
            def last_a_use(s):
                lo, hi = s * DFF // SLOT, ((s + 1) * DFF - 1) // SLOT
                return max(max(k for k in range(NA) if k % SLOTS == a) for a in range(lo, min(hi, SLOTS - 1) + 1)) + 1

            def gate_load(e, s):
                src = t["w_gate"][0][bass.ds(e, 1)].rearrange("a (t p) n -> t p (a n)", p=P)
                sp.dma_start(expert_slot(s), src[s]).then_inc(landed(s), 16)

            def up_load(e, s):
                src = t["w_up"][0][bass.ds(e, 1)].rearrange("a (t p) n -> t p (a n)", p=P)
                sp.dma_start(expert_slot(s), src[s]).then_inc(landed(s), 16)

            def down_load(e, s):
                src = t["w_down"][0][bass.ds(e, 1)].rearrange("a (p j) n -> p (a j n)", p=P)
                sp.dma_start(expert_slot(s), src[:, s * DFF:(s + 1) * DFF]).then_inc(landed(s), 16)

            def kv_load(e):
                L, c = e // 8, e % 8
                for half in range(2):
                    src = t["w_xkv_2"].rearrange("l (t p) (h c n) -> p l h c t n", p=P, h=2, n=P)
                    src = src[:, bass.ds(L, 1), half, bass.ds(c, 1)]
                    sp.dma_start(tiles(kvw[:], KT)[:, :, half * P:(half + 1) * P],
                                 src.rearrange("p l c t n -> p (l c t) n")).then_inc(S("kv_landed"), 16)

            def rest_of_expert(e):
                for s in range(ESLOTS):
                    sp.wait_ge(S("gate_used"), 8 * e + s + 1)
                    up_load(e, s)
                for s in range(ESLOTS):
                    sp.wait_ge(S("up_used"), 8 * e + s + 1)
                    down_load(e, s)

            for s in range(ESLOTS):
                sp.wait_ge(S("proj_ready"), 2 * last_a_use(s))
                gate_load(0, s)
            sp.wait_ge(S("proj_ready"), 2 * NA)
            sp.dma_start(tiles(memtok, 2), mem).then_inc(S("mem_landed"), 16)
            kv_load(0)
            rest_of_expert(0)
            with sp.Fori(1, EXP) as e:
                for s in range(ESLOTS):
                    sp.wait_ge(S("down_used"), 8 * e - 8 + s + 1)
                    gate_load(e, s)
                sp.wait_ge(S("kv_used"), e)
                kv_load(e)
                rest_of_expert(e)

            def chunk_source(name, c):
                col = slice(256 * c, 256 * c + 256)
                if name == "ab":
                    at = 256 * c if c < 6 else 8 + 256 * c
                    return t["ab_w_in_2"][0].rearrange("(t p) n -> p t n", p=P)[:, :, at:at + 256]
                if name in ("ab_out", "c_in", "c_out"):
                    src = {"ab_out": "ab_w_out_2", "c_in": "c_w_in_2", "c_out": "c_w_out_2"}[name]
                    return t[src][0].rearrange("(t p) n -> p t n", p=P)[:, :, col]
                if name in ("c_a", "c_i"):
                    src = {"c_a": "c_w_a_2", "c_i": "c_w_i_2"}[name]
                    return t[src][0].rearrange("b (k p) n -> p (b k) n", p=P)
                L, name = int(name[-1]), name[:-1]
                if name in ("xq", "xo"):
                    return t[f"w_{name}_2"][L].rearrange("(t p) n -> p t n", p=P)[:, :, col]
                gu_w = t["w_ffn_gu_2"][L].rearrange("(t p) n -> p t n", p=P)
                if name == "gate":
                    return gu_w[:, :, col]
                if name == "up":
                    return gu_w[:, :, DFF + 256 * c:DFF + 256 * c + 256]
                return t["w_ffn_down_2"][L].rearrange("(j p) n -> p j n", p=P)[:, 2 * c:2 * c + 2, :]

            for k, (name, c) in enumerate(C_CHUNKS):
                s = k % CSLOTS
                if k < CSLOTS:
                    g = min(g for g in range(ESLOTS) if DOWN_END[g] * D >= (s + 1) * SLOT)
                    sp.wait_ge(S("down_used"), 8 * EXP - 8 + max(g, min(s, ESLOTS - 1)) + 1)
                else:
                    last = k - CSLOTS
                    if last in split_index:
                        sp.wait_ge(S("weights_low_dve"), split_index[last] + 1)
                        sp.wait_ge(S("weights_low_pool"), split_index[last] + 1)
                    else:
                        sp.wait_ge(*chunk_used[last])
                src = chunk_source(name, c)
                sp.dma_start(tiles(raw_slot(k), src.shape[1]), src).then_inc(landed(s), 16)

            y = out[0].rearrange("(i p) n -> p i n", p=P)
            for i in range(2):
                sp.wait_ge(S("out_rows"), 2 * (i + 1))
                sp.dma_start(y[:, i, :], tiles(yT, 2)[:, i, :]).then_inc(S("stored"), 16)
            sp.wait_ge(S("stored"), 32)

        @block.gpsimd
        def _(pool):
            pool.memset(ones[:], 1.0).then_inc(S("ones_ready"), 1)
            for name, dst in (("dist_fwd", dist_fwd), ("dist_bwd", dist_bwd), ("pick", pick[0:8]), ("dirs", dirs),
                              ("into", into), ("bar_fwd", bar_fwd), ("bar_bwd", bar_bwd)):
                pool.dma_start(dst, t[name]).then_inc(S("tables_landed"), 16)
            for name, dst in (("cos", cosT), ("sin", sinT), ("rot", rot)):
                pool.dma_start(dst, t[name]).then_inc(S("rotary_landed"), 16)
            gates = t["b_gates"].rearrange("a (r c) -> (a r) c", c=1)
            pool.dma_start(b_i, gates[0:8]).then_inc(S("bias_landed"), 16)
            pool.dma_start(b_f, gates[8:16]).then_inc(S("bias_landed"), 16)
            pool.dma_start(b_fox, t["ab_b_f_2"].rearrange("a (r c) -> (a r) c", c=1)).then_inc(S("bias_landed"), 16)
            pool.dma_start(iota_col, t["iota_col"]).then_inc(S("bias_landed"), 16)
            dec = DEC.rearrange("p (h i l) -> p h i l", h=H, i=TT)
            for n in range(H * TT):
                h, i = n // TT, n % TT
                pool.wait_ge(S("decay_exps"), 2 * (n + 1))
                pool.tensor_tensor(dec[:, h, i, :], dec[:, h, i, :], moT[:, (n % 2) * T:(n % 2 + 1) * T], ALU.mult)\
                    .then_inc(S("decay_product"), 1)
                pool.wait_ge(S("decay_product"), n + 1)
                blk = dec[0:ROWS[i], h, i, P * i:P * i + ROWS[i]]
                pool.tensor_tensor(blk, blk, ident[0:ROWS[i], 0:ROWS[i]], ALU.add).then_inc(S("decay_ready"), 1)
            pool.wait_ge(S("proj_ready"), 2 * NA)
            pool.dma_start(own[0:EXP], t["own"]).then_inc(S("own_landed"), 16)
            pool.dma_start(iota_row, t["iota_row"]).then_inc(S("iota_landed"), 16)
            mm_l = tiles(mm, 2)
            st3 = ST.rearrange("p (i s) -> p i s", i=TT)
            ste3 = STe.rearrange("p (i s) -> p i s", i=TT)
            pool.wait_ge(S("gather_ready"), 2 * TT + 1)
            pool.wait_ge(S("norm_out"), 8 * 4)
            pool.tensor_copy(mwork, mm_l[:, 0, :]).then_inc(S("mwork_ready"), 1)
            with pool.Fori(1, EXP) as e:
                pool.wait_ge(S("xs_ready"), e)
                pool.tensor_copy(ste3, st3[:, :, bass.ds(e * CAP, CAP)]).then_inc(S("ste_ready"), 1)
                pool.wait_ge(S("kv_used"), e)
                pool.tensor_copy(mwork, mm[:, bass.ds((e // 8) * 2048, 2048)]).then_inc(S("mwork_ready"), 1)
            pool.wait_ge(S("xs_ready"), EXP)
            pool.tensor_copy(ste3, st3[:, :, EXP * CAP:(EXP + 1) * CAP]).then_inc(S("ste_ready"), 1)
            pool.wait_ge(S("norm_out"), 8 * 6)
            pool.dma_start(fox_bar, t["bar_causal"]).then_inc(S("fox_tables"), 16)
            pool.dma_start(fpick[0:8], t["pick"]).then_inc(S("fox_tables"), 16)
            cols = slice(0, 256 * POOL_TILES)
            for n, k in enumerate(split_chunks):
                pool.wait_ge(S("weights_high"), n + 1)
                pool.tensor_tensor(part(lows, n)[:, cols], raw_slot(k)[:, cols], part(highs, n)[:, cols], ALU.subtract)\
                    .then_inc(S("weights_low_pool"), 1)

        @block.tensor
        def _(pe):
            norms = [0]

            def norm_part(q, width):
                pe.wait_ge(S("norm_squares"), 4 * norms[0] + q + 1)
                sq = tiles(SQ[:, 0:KT * width], KT)
                for i in (2 * q, 2 * q + 1):
                    last = pe.matmul(bank[7][:, 0:width], ones[:], sq[:, i, :], start=(i == 0), stop=(i == KT - 1))
                if q == 3:
                    last.then_inc(S("norm_sum"), 1)
                    norms[0] += 1

            def norm_sum(width):
                for q in range(4):
                    norm_part(q, width)

            def column_tile(k, slot, off, moving, width, at=0, kt=KT, wait=True, done=True, fresh=None):
                if wait:
                    pe_bank_free(pe, k)
                w = tiles(W[:, slot * SLOT:(slot + 1) * SLOT], kt)
                for i in range(kt):
                    if fresh is not None:
                        pe.wait_ge(S("norm_out"), fresh + i + 1)
                    last = pe.matmul(bank[pj.entries[k][0]][:, at:at + width], w[:, i, off:off + P], moving[:, i, :],
                                     start=(i == 0), stop=(i == kt - 1))
                if done:
                    last.then_inc(S("proj_ready"), 1)
                return last

            def chunk_a(k):
                pe.wait_ge(landed(k % SLOTS), 16 * (k // SLOTS + 1))

            pe.wait_ge(S("ident_landed"), 16)
            pe.wait_ge(S("x_landed"), 64)
            xt = tiles(xtok, TT)
            for i in range(KT):
                if i >= 4:
                    pe.wait_ge(S("xt_taken_act" if i % 2 == 0 else "xt_taken_dve"), i // 2 - 1)
                for j in range(TT):
                    last = pe.transpose(bank[i % 4][:, P * j:P * j + ROWS[j]], xt[0:ROWS[j], j, P * i:P * i + P],
                                        ident[0:ROWS[j], 0:ROWS[j]])
                last.then_inc(S("xt_ready"), 1)
            pe.wait_ge(S("vec_landed"), 16 * sum(len(g) for g in VEC_ROWS))
            for j, n in enumerate(VEC_COUNT):
                last = pe.transpose(bank[4][:, P * j:P * j + n], vrow[0:n, P * j:P * j + P], ident[0:n, 0:n])
            last.then_inc(S("vec_ready"), 1)
            pe.wait_ge(S("ones_ready"), 1)
            norm_sum(T)

            u3 = tiles(uT, KT)
            gw = tiles(GW[:], KT)
            pe.wait_ge(S("norm_out"), 8)
            pe.wait_ge(S("gate_w_landed"), 16)
            for g in range(2):
                for i in range(KT):
                    last = pe.matmul(bank[4 + g][0:8, 0:T], gw[:, i, 8 * g:8 * g + 8], u3[:, i, :],
                                     start=(i == 0), stop=(i == KT - 1))
                last.then_inc(S("gates_ready"), 1)

            for b in (0, 1):
                pe.wait_ge(S("xt_taken_act"), 4)
                pe.wait_ge(S("xt_taken_dve"), 4)

            def project_tile(n):
                k = n // 2
                if n % 2 == 0:
                    chunk_a(k)
                column_tile(A_FIRST[n], k % SLOTS, P * (n % 2), u3, T)

            def project_a(first, last_chunk):
                for n in range(2 * first, 2 * last_chunk):
                    project_tile(n)

            project_a(0, 6)

            def values_to_tokens(src, dst_bank):
                s3 = tiles(src, H)
                for j in range(TT):
                    for h in range(H):
                        last = pe.transpose(bank[dst_bank + j][0:ROWS[j], P * h:P * h + P],
                                            s3[:, h, P * j:P * j + ROWS[j]], ident[:])
                    last.then_inc(S("values_ready"), 1)

            pe.wait_ge(S("proj_taken_act"), 12)
            pe.wait_ge(S("gates_taken"), 2)
            values_to_tokens(mvT, 4)
            project_a(6, 8)
            pe.wait_ge(S("rotary_landed"), 48)
            for n in range(2 * H):
                project_tile(16 + n)
                pe.wait_ge(S("proj_taken_act"), 13 + n)
                if n:
                    pe.wait_ge(S("rotary_taken"), n)
                src = tiles(rqT if n < H else rkT, H)[:, n % H, :]
                pe.matmul(bank[7][:, 0:T], rot, src, start=True, stop=True).then_inc(S("rotary_ready"), 1)
            pe.wait_ge(S("values_taken"), TT)
            pe.wait_ge(S("proj_taken_act"), 24)
            values_to_tokens(rvT, 4)

            pe.wait_ge(S("gate_rows_ready"), 1)
            for j in range(TT):
                last = pe.transpose(bank[3][0:ROWS[j], 8 * j:8 * j + 8], Bb[0:8, P * j:P * j + ROWS[j]], ident[0:8, 0:8])
            last.then_inc(S("acol_ready"), 1)

            qk = tiles(QK, 8)
            mv3 = tiles(mv, TT)

            def scores(q, k, gate, sem):
                pe.wait_ge(*gate)
                for j in range(TT):
                    last = pe.matmul(bank[4 + j][0:ROWS[j], 0:T], k[:, P * j:P * j + ROWS[j]], q, start=True, stop=True)
                last.then_inc(S(sem), 1)

            def stab(n):
                h, d = n // 2, n % 2
                r = 4 * d + h
                if n == 0:
                    pe.wait_ge(S("rotary_taken"), 2 * H)
                    pe.wait_ge(S("stab_ready"), 1)
                else:
                    pe.wait_ge(S("args_ready"), n)
                pe.matmul(bank[7][:, 0:T], pick[0:8, P * r:P * r + P], sf[0:8, :], start=True, stop=True)\
                    .then_inc(S("stab_bcast"), 1)

            def span(d, j):
                return (P * j, T) if d == 0 else (0, min(T, P * (j + 1)))

            pe.wait_ge(S("acol_taken"), 1)
            pe.wait_ge(S("tables_landed"), 7 * 16)
            stab(0)
            pe.wait_ge(S("values_taken"), 2 * TT)
            scores(qk[:, 0, :], qk[:, H, :], (S("qk_ready"), 8), "m_scores")
            for n in range(8):
                h, d = n // 2, n % 2
                r = 4 * d + h
                if n + 1 < 8:
                    stab(n + 1)
                project_tile(24 + n)
                pt = tiles(SQ[:, (n % 2) * 816:(n % 2 + 1) * 816], TT)
                pe.wait_ge(S("m_probs"), n + 1)
                if n:
                    pe.wait_ge(S("num_taken"), n)
                order = list(range(TT)) if d == 0 else list(range(TT))[::-1]
                for j in order:
                    lo, hi = span(d, j)
                    pe.matmul(bank[2][:, lo:hi], mv3[0:ROWS[j], j, P * h:P * h + P], pt[0:ROWS[j], j, lo:hi],
                              start=(j == order[0]), stop=(j == order[-1]))
                for j in order:
                    lo, hi = span(d, j)
                    last = pe.matmul(bank[3][0:8, lo:hi], into[0:ROWS[j], 8 * r:8 * r + 8], pt[0:ROWS[j], j, lo:hi],
                                     start=(n == 0 and j == order[0]), stop=(n == 7 and j == order[-1]))
                last.then_inc(S("num_ready"), 1)
                if d == 1 and n < 7:
                    scores(qk[:, h + 1, :], qk[:, H + h + 1, :], (S("m_probs"), n + 1), "m_scores")

            pe.wait_ge(S("recip_ready"), 1)
            for r in range(8):
                if r >= 2:
                    pe.wait_ge(S("recip_taken"), r - 1)
                else:
                    pe.wait_ge(S("num_taken"), 8)
                pe.matmul(bank[2 + r % 2][:, 0:T], pick[0:8, P * r:P * r + P], rowt[0:8, :], start=True, stop=True)\
                    .then_inc(S("recip_bcast"), 1)

            def head_mean(src, first_bank):
                s3 = tiles(src, H)
                for h in range(H):
                    last = pe.matmul(bank[first_bank + h][:, 0:T], ones[:], s3[:, h, :], start=True, stop=True)
                last.then_inc(S("hn_mean"), 1)

            def head_variance(sq, first_bank, n):
                sq3 = tiles(sq, H)
                pe.wait_ge(S("hn_squares"), n + 1)
                for h in range(H):
                    last = pe.matmul(bank[first_bank + h][:, 0:T], ones[:], sq3[:, h, :], start=True, stop=True)
                last.then_inc(S("hn_var"), 1)

            rq3, rk3, rv3 = tiles(rqT, H), tiles(rkT, H), tiles(rv, TT)
            pe.wait_ge(S("rot_out"), 8)
            pe.wait_ge(S("args_ready"), 8)
            for h in range(H):
                scores(rq3[:, h, :], rk3[:, h, :], (S("m_probs"), 8) if h == 0 else (S("r_probs"), h), "r_scores")
                if h == 0:
                    pe.wait_ge(S("hm_ready"), 1)
                    pe.wait_ge(S("proj_taken_act"), 32)
                    head_mean(HM, 0)
                if h == 2:
                    head_variance(hm_squares, 0, 0)
                pt = tiles(SQ[:, (h % 2) * 816:(h % 2 + 1) * 816], TT)
                pe.wait_ge(S("r_probs"), h + 1)
                if h:
                    pe.wait_ge(S("ret_taken"), h)
                for j in range(TT):
                    last = pe.matmul(bank[7][:, 0:T], rv3[0:ROWS[j], j, P * h:P * h + P], pt[0:ROWS[j], j, :],
                                     start=(j == 0), stop=(j == TT - 1))
                last.then_inc(S("ret_ready"), 1)
            pe.wait_ge(S("ret_taken"), H)
            head_mean(RET, 4)

            def out_part(n, first, end):
                k = 16 + n // 2
                if n % 2 == 0 and first == H:
                    chunk_a(k)
                if first == H:
                    pe_bank_free(pe, A_OUT[n])
                w = tiles(W[:, (k % SLOTS) * SLOT:(k % SLOTS + 1) * SLOT], KT)
                for i in range(first, end):
                    if n == 0 and i < H:
                        pe.wait_ge(S("y_ready"), 2 + i)
                    last = pe.matmul(bank[pj.entries[A_OUT[n]][0]][:, 0:T], w[:, i, P * (n % 2):P * (n % 2) + P], u3[:, i, :],
                                     start=(i == H), stop=(i == H - 1))
                if first == 0:
                    last.then_inc(S("proj_ready"), 1)

            pe.wait_ge(S("y_ready"), 1)
            for n in range(4):
                if n == 2:
                    head_variance(SQ[:, 0:H * T], 4, 1)
                out_part(n, H, KT)
            for n in range(KT):
                if n >= 4:
                    out_part(n, H, KT)
                out_part(n, 0, H)
                if n >= 3 and n % 2 == 1:
                    norm_part((n - 3) // 2, T)
            norm_part(3, T)

            pe.wait_ge(S("router_w_landed"), 16)
            rw = tiles(RW[:], KT)
            u23 = tiles(u2, KT)
            for i in range(KT):
                pe.wait_ge(S("norm_out"), 8 + i + 1)
                last = pe.matmul(bank[4][0:EXP, 0:T], rw[:, i, :], u23[:, i, :], start=(i == 0), stop=(i == KT - 1))
            last.then_inc(S("router_ready"), 1)
            pe.wait_ge(S("logits_taken"), 1)
            for j in range(TT):
                last = pe.transpose(bank[4][0:ROWS[j], 16 * j:16 * j + 16], logitsT[0:EXP, P * j:P * j + ROWS[j]], ident[0:EXP, 0:EXP])
            last.then_inc(S("router_ready"), 1)
            pe.wait_ge(S("proj_taken_dve"), KT)
            for n in range(2 * TT):
                j, half = n // 2, n % 2
                b = UTOK_BANKS[n]
                if n == 5:
                    pe.wait_ge(S("aff_ready"), 1)
                    a3 = tiles(aff, TT)
                    for m in range(TT):
                        last = pe.transpose(bank[5][0:EXP, P * m:P * m + ROWS[m]], a3[0:ROWS[m], m, :], ident[0:ROWS[m], 0:ROWS[m]])
                    last.then_inc(S("affT_ready"), 1)
                for i in range(4):
                    last = pe.transpose(bank[b][0:ROWS[j], P * i:P * i + P], u23[:, 4 * half + i, P * j:P * j + ROWS[j]], ident[:])
                last.then_inc(S("utok_ready"), 1)
            pe.wait_ge(S("mem_landed"), 16)
            m3 = tiles(memtok, 2)
            for b in range(4):
                pe.wait_ge(S("utok_taken"), b + 1)
                for i in range(2):
                    for j in range(2):
                        last = pe.transpose(bank[b][:, 256 * i + P * j:256 * i + P * j + P],
                                            m3[:, j, P * (2 * b + i):P * (2 * b + i) + P], ident[:])
                last.then_inc(S("mem_ready"), 1)
            pe.wait_ge(S("utok_taken"), 6)
            norm_sum(256)
            pe.wait_ge(S("spread_ready"), 1)
            for b in range(2):
                last = pe.matmul(bank[5 + b][:, 0:272], ones[0:EXP, :], spread[0:EXP, 272 * b:272 * b + 272], start=True, stop=True)
            pe.transpose(bank[4][:, 0:EXP], idx2[0:EXP], ident[0:EXP, 0:EXP])
            pe.transpose(bank[4][:, EXP:2 * EXP], val2[0:EXP], ident[0:EXP, 0:EXP]).then_inc(S("choice_ready"), 1)

            ut3, ste3 = tiles(utok, TT), tiles(STe, TT)
            xs3 = tiles(xs, KT)
            mw3, kw3 = tiles(mwork, KT), tiles(kvw, KT)

            def gather():
                for i in range(KT):
                    for j in range(TT):
                        last = pe.matmul(bank[6][:, CAP * i:CAP * i + CAP], ut3[0:ROWS[j], j, P * i:P * i + P],
                                         ste3[0:ROWS[j], j, :], start=(j == 0), stop=(j == TT - 1))
                last.then_inc(S("xs_ready"), 1)

            def hidden(e, first_bank, sem, use):
                for s in range(ESLOTS):
                    if use == 2:
                        scatter(e, s)
                    pe.wait_ge(landed(s), 48 * e + 16 * (A_USES[s] + use))
                    w = W[:, s * DFF:(s + 1) * DFF].rearrange("p (f j) -> p f j", j=FT)
                    for c, (lo, hi) in enumerate(HCHUNKS):
                        for half in range(2):
                            last = pe.matmul(bank[first_bank + c][MPAD * half:MPAD * half + MPAD, 0:(hi - lo) * HF],
                                             xs3[:, s, :], w[:, lo:hi, HF * half:HF * half + HF],
                                             start=(s == 0), stop=(s == ESLOTS - 1), skip_group_check=True)
                    last.then_inc(S(sem), 1)

            def scatter(e, i):
                if i == 0:
                    pe.wait_ge(S("y_taken"), e + 1)
                    pe.wait_ge(S("se_ready"), e + 1)
                    pe.wait_ge(S("kv_taken"), e + 1)
                else:
                    pe.wait_ge(S("scatter_taken"), 8 * e + i)
                r, c = MPAD * (i // 4), P * (i % 4)
                pe.matmul(bank[7][:, 0:T], ys[r:r + MPAD, c:c + P], Se[r:r + MPAD, :], start=True, stop=True)\
                    .then_inc(S("scatter_ready"), 1)

            pe.wait_ge(S("xs_pads"), 1)
            pe.wait_ge(S("gather_ready"), TT)
            pe.wait_ge(S("ste_ready"), 1)
            gather()
            hid3 = th.rearrange("p (f j) -> p f j", j=HF)
            with pe.Fori(0, EXP) as e:
                pe.wait_ge(S("xs_taken"), e + 1)
                hidden(e, 0, "gate_used", 1)
                hidden(e, 3, "up_used", 2)
                pe.wait_ge(S("scatter_taken"), 8 * e + 8)
                pe.wait_ge(S("kv_landed"), 32 * e + 32)
                pe.wait_ge(S("mwork_ready"), e + 1)
                for i in range(KT):
                    pe.matmul(bank[7][:, 0:256], kw3[:, i, 0:P], mw3[:, i, :], start=(i == 0), stop=(i == KT - 1))
                for m in range(2):
                    for i in range(KT):
                        last = pe.matmul(bank[7][:, 256 + P * m:256 + P * m + P], mw3[:, i, P * m:P * m + P], kw3[:, i, P:2 * P],
                                         start=(i == 0), stop=(i == KT - 1))
                last.then_inc(S("kv_used"), 1)
                pe.wait_ge(S("ste_ready"), e + 2)
                gather()
                pe.wait_ge(S("hid_ready"), 3 * e + 3)
                for j in range(HF):
                    last = pe.transpose(bank[j // 4][:, P * (j % 4):P * (j % 4) + P], hid3[:, :, j], ident[:])
                    if j % 4 == 3 or j == HF - 1:
                        last.then_inc(S("hidT_ready"), 1)
                pe.wait_ge(S("xs_taken"), e + 2)
                slots = 0
                for j in range(FT):
                    if j < HF and j % 4 == 0:
                        pe.wait_ge(S("hidT_taken"), 3 * e + j // 4 + 1)
                    while slots <= DOWN_SLOT[j]:
                        pe.wait_ge(landed(slots), 48 * e + 16 * (A_USES[slots] + 3))
                        slots += 1
                    at = P * (j % HF) + MPAD * (j // HF)
                    for half in range(2):
                        last = pe.matmul(bank[6][MPAD * half:MPAD * half + MPAD, :], hidT[:, at:at + MPAD],
                                         W[:, j * D + 512 * half:j * D + 512 * half + 512],
                                         start=(j == 0), stop=(j == FT - 1), skip_group_check=True)
                    if j + 1 in DOWN_END:
                        last.then_inc(S("down_used"), 1)
            for i in range(KT):
                scatter(EXP, i)

            pe.wait_ge(S("scatter_taken"), 8 * (EXP + 1))
            norm_sum(256)
            hn3 = tiles(hN, KT)
            outs = [8 * 5]

            def norm_done():
                outs[0] += 8
                pe.wait_ge(S("norm_out"), outs[0])

            def pair(key, entry, moving, fresh=False, halves=(0, 1)):
                s = chunk_landed(pe, key)
                if 0 in halves:
                    pe_bank_free(pe, entry)
                for half in halves:
                    last = column_tile(entry, s, P * half, moving, 256, at=256 * half, wait=False, done=False,
                                       fresh=outs[0] - 8 if fresh and half == 0 else None)
                if 1 in halves:
                    last.then_inc(S("proj_ready"), 1)

            def pre_normed():
                norm_sum(256)
                outs[0] += 8

            def post_normed(pairs):
                for k, one in enumerate(pairs):
                    one()
                    if k:
                        norm_part(k - 1, 256)
                norm_part(3, 256)
                outs[0] += 8

            def transpose_probs(n, src):
                pe.wait_ge(S("att_probs"), n + 1)
                if n:
                    pe.wait_ge(S("pt_taken"), n)
                for qi in range(2):
                    for m in range(2):
                        last = pe.transpose(bank[7][:, 256 * m + P * qi:256 * m + P * qi + P],
                                            src[:, 256 * qi + P * m:256 * qi + P * m + P], ident[:])
                last.then_inc(S("pt_ready"), 1)

            def split_landed(key):
                k = c_index[key]
                n = split_index[k]
                pe.wait_ge(S("weights_high"), n + 1)
                pe.wait_ge(S("weights_low_dve"), n + 1)
                pe.wait_ge(S("weights_low_pool"), n + 1)
                return part(highs, n), part(lows, n)

            def three_passes(dst, parts, start, stop, check=False):
                todo = [(wh, xh) for (wh, wl), (xh, xl) in parts] + [(wh, xl) for (wh, wl), (xh, xl) in parts] \
                    + [(wl, xh) for (wh, wl), (xh, xl) in parts]
                for n, (w, x) in enumerate(todo):
                    last = pe.matmul(dst, w, x, start=start and n == 0, stop=stop and n == len(todo) - 1,
                                     skip_group_check=check)
                return last

            def pair3(key, entry, x_low):
                high, low = (tiles(w, KT) for w in split_landed(key))
                xh, xl = tiles(x_high, KT), tiles(x_low, KT)
                pe_bank_free(pe, entry)
                for half in range(2):
                    c = slice(P * half, P * half + P)
                    last = three_passes(bank[pj.entries[entry][0]][:, 256 * half:256 * half + 256],
                                        [((high[:, i, c], low[:, i, c]), (xh[:, i, :], xl[:, i, :])) for i in range(KT)],
                                        True, True)
                last.then_inc(S("proj_ready"), 1)

            inputs = [0]

            def input_split():
                inputs[0] += 1
                pe.wait_ge(S("input_split"), inputs[0])

            for L in range(2):
                pre_normed()
                if L == 0:
                    pe.wait_ge(S("norm_out"), outs[0])
                    pe.wait_ge(S("fox_w_landed"), 16)
                    fw = tiles(GW[:, 0:64], KT)
                    for i in range(KT):
                        last = pe.matmul(bank[6][0:8, 0:256], fw[:, i, :], hn3[:, i, :], start=(i == 0), stop=(i == KT - 1))
                    last.then_inc(S("fox_logits"), 1)
                    pair(("ab", 0), C["ab", 0], hn3)
                    input_split()
                    for k in range(1, 4):
                        pair3(("ab", k), C["ab", k], x_low_pre)
                    for k in (4, 5):
                        high, low = (tiles(w, KT) for w in split_landed(("ab", k)))
                        xh, xl = tiles(x_high, KT), tiles(x_low_pre, KT)
                        pe_bank_free(pe, C["ab", k])
                        for m in range(2):
                            c = slice(P * m, P * m + P)
                            last = three_passes(bank[k % 4][:, 256 * m:256 * m + 256],
                                                [((xh[:, i, c], xl[:, i, c]), (high[:, i, :], low[:, i, :])) for i in range(KT)],
                                                True, True)
                        last.then_inc(S("proj_ready"), 1)
                    q3, k3, v3 = tiles(fq, 4), tiles(fk, 4), fv

                    def fox_scores(n):
                        r = 64 * (n % 2)
                        if n:
                            pe.wait_ge(S("att_scores_taken"), n)
                        for qi in range(2):
                            pe.matmul(bank[5][:, 256 * qi:256 * qi + 256], q3[r:r + 64, n // 2, P * qi:P * qi + P],
                                      k3[r:r + 64, n // 2, :], start=True, stop=True)
                        pe.matmul(bank[6][:, 0:256], fpick[0:8, P * n:P * n + P], frow[0:8, :], start=True, stop=True)\
                            .then_inc(S("att_scores"), 1)

                    pe.wait_ge(S("proj_taken_act"), taken_after("act", C["ab", 5]))
                    pe.wait_ge(S("fox_row_ready"), 1)
                    pe.wait_ge(S("fox_tables"), 32)
                    fox_scores(0)
                    for n in range(8):
                        if n < 7:
                            fox_scores(n + 1)
                        if n < 6:
                            pair(("ab", 6 + n), C["ab", 6 + n], hn3, halves=(0,))
                        transpose_probs(n, fox_e[n % 2])
                        if n < 6:
                            pair(("ab", 6 + n), C["ab", 6 + n], hn3, halves=(1,))
                        pe.wait_ge(S("pt_taken"), n + 1)
                        if n and n % 2 == 0:
                            pe.wait_ge(S("att_out_taken"), n // 2)
                        r = 64 * (n % 2)
                        for m in range(2):
                            at = 512 * (n // 4) + 256 * m + 64 * (n % 4)
                            last = pe.matmul(bank[4][r:r + 64, 0:256], v3[:, at:at + 64], fox_pt[n % 2][:, 256 * m:256 * m + 256],
                                             start=(m == 0), stop=(m == 1))
                        last.then_inc(S("att_out"), 1)
                else:
                    pair(("c_in", 4), C["c_in", 0], hn3, True)
                    input_split()
                    for k in range(1, 5):
                        pair3(("c_in", (k + 4) % 8), C["c_in", k], x_low_pre)
                    lu3 = tiles(lu, KT)
                    pe.wait_ge(S("lru_conv"), KT)
                    for k in range(8):
                        w = None
                        if k % 4 == 0:
                            s = chunk_landed(pe, ("c_a" if k < 4 else "c_i", 0))
                        w = tiles(W[:, s * SLOT:(s + 1) * SLOT], KT)
                        b = k % 4
                        pe_bank_free(pe, C["c_gates", k])
                        for half in range(2):
                            for i in range(2):
                                last = pe.matmul(bank[k % 4][:, 256 * half:256 * half + 256], w[:, 2 * b + i, P * half:P * half + P],
                                                 lu3[:, 2 * b + i, :], start=(i == 0), stop=(i == 1))
                        last.then_inc(S("proj_ready"), 1)
                    for k in range(5, 8):
                        pair(("c_in", (k + 4) % 8), C["c_in", k], hn3)
                input_split()
                post_normed([lambda k=k: pair3(("ab_out" if L == 0 else "c_out", k), C["mix_out", L, k], x_low_out)
                             for k in range(4)])
                pre_normed()
                pair((f"xq{L}", 0), C["xq", L, 0], hn3, True)
                input_split()
                for k in range(1, 4):
                    pair3((f"xq{L}", k), C["xq", L, k], x_low_pre)
                xq3 = tiles(xq, KT)
                kk = kT2[:, 2048 * L:2048 * L + 2048]

                def cross_scores(n):
                    h = n % 4
                    pe.wait_ge(S("att_exps"), 2 * n - 2)
                    for qi in range(2):
                        for i in range(2):
                            last = pe.matmul(bank[4 + n % 2][:, 256 * qi:256 * qi + 256], xq3[:, 2 * h + i, P * qi:P * qi + P],
                                             kk[:, 256 * (2 * h + i):256 * (2 * h + i) + 256], start=(i == 0), stop=(i == 1))
                    last.then_inc(S("att_scores"), 1)

                pe.wait_ge(S("proj_taken_act"), taken_after("act", C["xq", L, 3]))
                n0 = 8 + 4 * L
                cross_scores(n0)
                for n in range(n0, n0 + 4):
                    h = n % 4
                    if n < n0 + 3:
                        cross_scores(n + 1)
                    transpose_probs(n, att_e[n % 2])
                    pe.wait_ge(S("pt_taken"), n + 1)
                    if n == n0:
                        pe.wait_ge(S("att_out_taken"), 4 + 4 * L)
                    else:
                        pe.wait_ge(S("att_out_taken"), n - 4)
                    for dv in range(2):
                        for m in range(2):
                            at = 2048 * L + 256 * (2 * h + dv) + P * m
                            last = pe.matmul(bank[6][:, 256 * dv:256 * dv + 256], v2[:, at:at + P],
                                             att_pt[n % 2][:, 256 * m:256 * m + 256], start=(m == 0), stop=(m == 1))
                    last.then_inc(S("att_out"), 1)
                pe.wait_ge(S("att_out_taken"), 4 + 4 * L + 4)
                input_split()
                post_normed([lambda k=k: pair3((f"xo{L}", k), C["xo", L, k], x_low_out) for k in range(4)])
                pre_normed()
                pair((f"gate{L}", 0), C["gate", L, 0], hn3, True)
                input_split()
                for k in range(FT // 2):
                    if k:
                        pair3((f"gate{L}", k), C["gate", L, k], x_low_ffn)
                    pair3((f"up{L}", k), C["up", L, k], x_low_ffn)
                fh_low, fh_high = tiles(fhid_low, FT), tiles(fhid_high, FT)
                for b in range(4):
                    pe_bank_free(pe, C["down", L, b])
                for c in range(FT // 2):
                    high, low = (tiles(w, 2) for w in split_landed((f"down{L}", c)))
                    pe.wait_ge(S("hidden_split"), L * (FT // 2) + c + 1)
                    for i in range(KT):
                        f = slice(P * i, P * i + P)
                        last = three_passes(bank[i // 2][:, 256 * (i % 2):256 * (i % 2) + 256],
                                            [((high[:, jj, f], low[:, jj, f]), (fh_high[:, 2 * c + jj, :], fh_low[:, 2 * c + jj, :]))
                                             for jj in range(2)], c == 0 and i % 2 == 0, c == FT // 2 - 1, True)
                        if c == FT // 2 - 1 and i % 2 == 1:
                            last.then_inc(S("proj_ready"), 1)
                    if c < FT // 2 - 1:
                        last.then_inc(S("ffn_down_used"), 1)
                norm_sum(256)
                outs[0] += 8

            pe.wait_ge(S("norm_out"), outs[0])
            x3 = tiles(xT, KT)
            for n in range(4):
                j, half = n // 2, n % 2
                for i in range(4):
                    last = pe.transpose(bank[n][:, P * i:P * i + P], x3[:, 4 * half + i, P * j:P * j + P], ident[:])
                last.then_inc(S("out_ready"), 1)

        @block.scalar
        def _(act):
            steps = [0]

            def after(ins):
                steps[0] += 1
                ins.then_inc(S("act_step"), 1)
                act.wait_ge(S("act_step"), steps[0])

            norms = [0]

            def log_exp_set():
                act.preload_act_table_set("natural_log_exp_and_others")

            def exp_tanh_set():
                act.preload_act_table_set("exp_and_others")

            def squares_pair(q, src, width):
                act.activation(tiles(SQ[:, 0:KT * width], KT)[:, 2 * q:2 * q + 2, :], src, ACT.Square)\
                   .then_inc(S("norm_squares"), 1)

            def squares(src3, width, ready=None):
                for q in range(4):
                    if ready:
                        act.wait_ge(S(ready[0]), ready[1] + 2 * q + 2)
                    squares_pair(q, src3[:, 2 * q:2 * q + 2, :], width)

            def rstd(width):
                n = norms[0]
                norms[0] += 1
                act.wait_ge(S("norm_sum"), n + 1)
                if n:
                    act.wait_ge(S("norm_out"), [0, 8, 16, 32][n] if n < 4 else 8 * (n + 1))
                after(act.activation(RSTD[:, 0:width], bank[7][:, 0:width], ACT.Ln, bias=eps, scale=1.0 / D))
                act.activation(RSTD[:, 0:width], RSTD[:, 0:width], ACT.Exp, scale=-0.5).then_inc(S("norm_rstd"), 1)

            act.dma_start(ident[:], t["ident"]).then_inc(S("ident_landed"), 16)
            act.dma_start(lgt[:, 8:16], t["ret_decay_logit"].rearrange("a d h -> a (d h)").to_broadcast([P, 8]))\
               .then_inc(S("logit_landed"), 16)

            log_exp_set()
            act.wait_ge(S("magnitudes"), 1)
            after(act.activation(lgt[:, 0:8], lgt[:, 0:8], ACT.Exp, scale=-1.0))
            act.activation(lgt[:, 0:8], lgt[:, 0:8], ACT.Ln, bias=1.0).then_inc(S("log_terms"), 1)

            ht3, u3 = tiles(hT[:], KT), tiles(uT, KT)
            act.wait_ge(S("eps_ready"), 1)
            for i in range(0, KT, 2):
                act.wait_ge(S("xt_ready"), i + 1)
                act.activation(ht3[:, i, :], bank[i % 4][:, 0:T], ACT.Copy).then_inc(S("xt_taken_act"), 1)
                act.wait_ge(S("xt_taken_act"), i // 2 + 1)
                act.wait_ge(S("xt_taken_dve"), i // 2 + 1)
                squares_pair(i // 2, ht3[:, i:i + 2, :], T)
            rstd(T)

            act.wait_ge(S("magnitudes"), 3)
            after(act.activation(rowt[0:8], rowt[0:8], ACT.Exp, scale=-1.0))
            act.activation(rowt[0:8], rowt[0:8], ACT.Ln, bias=1.0).then_inc(S("log_terms"), 1)

            act.wait_ge(S("magnitudes"), 2)
            after(act.activation(lamt[:, 0:8], lamt[:, 0:8], ACT.Exp, scale=-1.0))
            act.activation(lamt[:, 0:8], lamt[:, 0:8], ACT.Ln, bias=1.0).then_inc(S("log_terms"), 1)

            dec = DEC.rearrange("p (h i l) -> p h i l", h=H, i=TT)
            qkp = tiles(QKP, 8)
            qk = tiles(QK, 8)
            sq8 = tiles(SQ[:], 8)

            def decay(n):
                h, i = n // TT, n % TT
                at = 256 - P * i
                if n == 0:
                    act.wait_ge(S("tables_landed"), 7 * 16)
                    act.wait_ge(S("lg_ready"), 1)
                if n >= 2:
                    act.wait_ge(S("decay_product"), n - 1)
                act.activation(dec[:, h, i, :], dist_fwd[:, at:at + T], ACT.Exp, scale=lg[:, h:h + 1])\
                   .then_inc(S("decay_exps"), 1)
                act.activation(moT[:, (n % 2) * T:(n % 2 + 1) * T], dist_bwd[:, at:at + T], ACT.Exp,
                               scale=lg[:, 4 + h:5 + h]).then_inc(S("decay_exps"), 1)

            def take(k, dst, func=ACT.Copy, scale=1.0, src=None):
                proj_ready(act, k)
                b = bank[pj.entries[k][0]]
                act.activation(dst, b[:, 0:T] if src is None else src(b), func, scale=scale)\
                   .then_inc(S("proj_taken_act"), 1)

            def values(dst, first, count):
                d3 = tiles(dst, TT)
                for j in range(TT):
                    act.wait_ge(S("values_ready"), count + j + 1)
                    act.activation(d3[0:ROWS[j], j, :], bank[4 + j][0:ROWS[j], :], ACT.Copy).then_inc(S("values_taken"), 1)

            act.wait_ge(S("pads_ready"), 2)
            mv_T, mo_T, rq_T, rk_T, rv_T, rg_T = (tiles(x, H) for x in (mvT, moT, rqT, rkT, rvT, rgT))
            for k in range(12):
                if k < 8:
                    take(k, qkp[:, k, PAD:PAD + T])
                else:
                    take(k, mv_T[:, k - 8, :])
                decay(k)
                if 2 <= k < 10:
                    act.wait_ge(S("conv_ready"), k - 1)
                    act.activation(sq8[:, k - 2, :], qk[:, k - 2, :], ACT.Tanh, scale=0.5).then_inc(S("conv_tanh"), 1)
            act.wait_ge(S("xt_ready"), KT)
            values(mv, 4, 0)
            for k in range(12, 24):
                dst = (rq_T, rk_T, rv_T)[(k - 12) // 4][:, k % 4, :]
                take(k, dst, scale=float(P) ** -0.5 if k < 16 else 1.0)
            values(rv, 4, TT)

            act.wait_ge(S("stab_ready"), 1)
            act.activation(Mr[0:8], Mr[0:8], ACT.Exp, scale=-1.0).then_inc(S("floor_ready"), 1)
            act.wait_ge(S("decay_ready"), H * TT)
            num3 = tiles(NUM, 8)

            def unit_exps(n):
                h, d = n // 2, n % 2
                pt = tiles(SQ[:, (n % 2) * 816:(n % 2 + 1) * 816], TT)
                act.wait_ge(S("args_ready"), n + 1)
                for j in range(TT):
                    lo, hi = (P * j, T) if d == 0 else (0, min(T, P * (j + 1)))
                    last = act.activation(pt[0:ROWS[j], j, lo:hi], pt[0:ROWS[j], j, lo:hi], ACT.Exp, scale=-1.0)
                last.then_inc(S("unit_exps"), 1)

            unit_exps(0)
            for n in range(8):
                h, d = n // 2, n % 2
                if n < 7:
                    unit_exps(n + 1)
                k = 24 + n
                if k < 28:
                    take(k, mo_T[:, k - 24, :], ACT.Tanh, 0.5)
                else:
                    take(k, rg_T[:, k - 28, :])
                act.wait_ge(S("num_ready"), n + 1)
                act.activation(num3[:, 4 * d + h, :], bank[2][:, 0:T], ACT.Copy).then_inc(S("num_taken"), 1)
            act.wait_ge(S("proj_taken_act"), 32)
            act.activation(QK[:, 0:H * T], rgT, ACT.Tanh, scale=0.5).then_inc(S("rg_tanh"), 1)
            log_exp_set()

            def hn_squares(src, sq, n):
                act.wait_ge(S("hn_centred"), n + 1)
                act.activation(sq, src, ACT.Square).then_inc(S("hn_squares"), 1)

            def hn_rstd(dst, first_bank, n):
                act.wait_ge(S("hn_var"), n + 1)
                ln = tiles(dst, H)
                for h in range(H):
                    last = act.activation(ln[:, h, :], bank[first_bank + h][:, 0:T], ACT.Ln, bias=eps, scale=1.0 / P)
                after(last)
                act.activation(dst, dst, ACT.Exp, scale=-0.5).then_inc(S("hn_rstd"), 1)

            ret3 = tiles(RET, H)
            for h in range(H):
                if h == 1:
                    hn_squares(HM, hm_squares, 0)
                if h == 3:
                    hn_rstd(hm_rstd, 0, 0)
                act.wait_ge(S("ret_ready"), h + 1)
                act.activation(ret3[:, h, :], bank[7][:, 0:T], ACT.Copy).then_inc(S("ret_taken"), 1)
            hn_squares(RET, SQ[:, 0:H * T], 1)
            hn_rstd(ret_rstd, 4, 1)

            squares(ht3, T, ("proj_taken_dve", 0))
            rstd(T)
            a3 = tiles(aff, TT)
            act.wait_ge(S("router_max"), 2)
            for j in range(TT):
                last = act.activation(a3[0:ROWS[j], j, :], bank[4][0:ROWS[j], 16 * j:16 * j + 16], ACT.Exp,
                                      bias=smax[0:ROWS[j], j:j + 1], accum_out=ssum[0:ROWS[j], j:j + 1])
                last.then_inc(S("router_exps"), 1)
            ut3 = tiles(utok, TT)
            for n in range(2 * TT):
                j, half = n // 2, n % 2
                act.wait_ge(S("utok_ready"), n + 1)
                act.activation(ut3[0:ROWS[j], j, 512 * half:512 * half + 512], bank[UTOK_BANKS[n]][0:ROWS[j], :], ACT.Copy)\
                   .then_inc(S("utok_taken"), 1)
            for b in range(4):
                act.wait_ge(S("mem_ready"), b + 1)
                act.activation(mT[:, 512 * b:512 * b + 512], bank[b][:], ACT.Copy).then_inc(S("mem_taken"), 1)
            act.wait_ge(S("mem_taken"), 4)
            act.wait_ge(S("norm_out"), 16)
            squares(tiles(mT, KT), 256)
            rstd(256)

            act.wait_ge(S("norm_sum"), 3)
            act.memzero(ys).then_inc(S("y_taken"), 1)
            act.memzero(small[0:8, 176:177]).then_inc(S("kv_taken"), 1)

            def take_xs(count):
                act.wait_ge(S("xs_ready"), count)
                act.activation(tiles(xs, KT)[:, :, 0:CAP], tiles(bank[6][:, 0:KT * CAP], KT), ACT.Copy).then_inc(S("xs_taken"), 1)

            take_xs(1)
            with act.Fori(0, EXP) as e:
                act.wait_ge(S("gate_used"), 8 * e + 8)
                for c, (lo, hi) in enumerate(HCHUNKS):
                    act.activation(th[:, HF * lo:HF * hi], bank[c][:, 0:HF * (hi - lo)], ACT.Tanh, scale=0.5)\
                       .then_inc(S("gate_tanh"), 1)
                act.wait_ge(S("kv_used"), e + 1)
                act.activation(kT2[:, bass.ds(256 * e, 256)], bank[7][:, 0:256], ACT.Copy)
                act.activation(v2[:, bass.ds(256 * e, 256)], bank[7][:, 256:512], ACT.Copy).then_inc(S("kv_taken"), 1)
                take_xs(e + 2)
                for b in range(3):
                    act.wait_ge(S("hidT_ready"), 3 * e + b + 1)
                    n = min(4, HF - 4 * b) * P
                    act.activation(hidT[:, 512 * b:512 * b + n], bank[b][:, 0:n], ACT.Copy).then_inc(S("hidT_taken"), 1)
                act.wait_ge(S("down_used"), 8 * e + 8)
                act.activation(ys, bank[6][:], ACT.Copy).then_inc(S("y_taken"), 1)

            x3, hn3, y3 = tiles(xT, KT), tiles(hN, KT), tiles(yT, KT)
            log_exp_set()
            act.wait_ge(S("scatter_ready"), 8 * (EXP + 1))
            squares(ht3[:, :, META:T], 256, ("scatter_taken", 8 * EXP))
            rstd(256)

            outs = [8 * 5]

            def pre_norm():
                squares(x3, 256, ("norm_out", outs[0] - 8))
                rstd(256)
                outs[0] += 8

            def post_norm(entries):
                for n, k in enumerate(entries):
                    proj_ready(act, k)
                    b = bank[pj.entries[k][0]]
                    squares_pair(n, tiles(b[:], 2), 256)
                    act.activation(hN[:, 512 * n:512 * n + 512], b[:], ACT.Copy).then_inc(S("proj_taken_act"), 1)
                rstd(256)
                outs[0] += 8

            def att_softmax(n, buf, scale, from_bank):
                act.wait_ge(S("att_max"), n + 1)
                for qi in range(2):
                    src = (bank[4 + n % 2] if from_bank else buf)[:, 256 * qi:256 * qi + 256]
                    last = act.activation(buf[:, 256 * qi:256 * qi + 256], src, ACT.Exp,
                                          bias=smax[:, 2 * (n % 2) + qi:2 * (n % 2) + qi + 1], scale=scale,
                                          accum_out=ssum[:, 2 * (n % 2) + qi:2 * (n % 2) + qi + 1])
                    last.then_inc(S("att_exps"), 1)

            def take_probs(n, dst):
                act.wait_ge(S("pt_ready"), n + 1)
                act.activation(dst, bank[7][:], ACT.Copy).then_inc(S("pt_taken"), 1)

            for L in range(2):
                pre_norm()
                if L == 0:
                    act.wait_ge(S("magnitudes"), 4)
                    after(act.activation(frow2[0:8], frow2[0:8], ACT.Exp, scale=-1.0))
                    act.activation(frow2[0:8], frow2[0:8], ACT.Ln, bias=1.0).then_inc(S("log_terms"), 1)
                    for k in range(6):
                        dst = (fq, fk, fv)[k // 2]
                        take(C["ab", k], dst[:, 512 * (k % 2):512 * (k % 2) + 512], src=lambda b: b[:])
                    att_softmax(0, fox_e[0], 1.0, False)
                    for n in range(8):
                        if n < 7:
                            att_softmax(n + 1, fox_e[(n + 1) % 2], 1.0, False)
                        take_probs(n, fox_pt[n % 2])
                        if n < 6:
                            dst = (fb, fc, fu)[n // 2]
                            take(C["ab", 6 + n], dst[:, 512 * (n % 2):512 * (n % 2) + 512], src=lambda b: b[:])
                        if n % 2 == 1:
                            act.wait_ge(S("att_out"), n + 1)
                            ins = act.activation(y3[:, n // 2, :], bank[4][:, 0:256], ACT.Copy)
                            ins.then_inc(S("att_out_taken"), 1)
                    act.wait_ge(S("att_out_taken"), 4)
                else:
                    exp_tanh_set()
                    lup3 = tiles(lup, KT)
                    act.wait_ge(S("lru_pads"), 1)
                    for k in range(4):
                        take(C["c_in", k], lup3[:, 2 * k:2 * k + 2, 3:259], src=lambda b: b[:].rearrange("p (a n) -> p a n", a=2))

                    def gelu_in(k):
                        entry = C["c_in", 4 + k]
                        proj_ready(act, entry)
                        b = bank[pj.entries[entry][0]]
                        act.activation(SQ[:, 512 * k:512 * k + 512], b[:], ACT.Square).then_inc(S("gelu_square"), 1)
                        act.activation(lgate[:, 512 * k:512 * k + 512], b[:], ACT.Copy).then_inc(S("proj_taken_act"), 1)

                    def gelu_tanh(k):
                        act.wait_ge(S("gelu_cubic"), k + 1)
                        v = SQ[:, 512 * k:512 * k + 512]
                        act.activation(v, v, ACT.Tanh, scale=float(np.sqrt(2 / np.pi))).then_inc(S("gelu_tanh"), 1)

                    gelu_in(0)
                    act.wait_ge(S("half_bias"), 1)
                    act.wait_ge(S("lru_rate"), 1)
                    ta3, lr3 = tiles(ta, KT), tiles(lr, KT)
                    for k in range(8):
                        dst, hb = (ta, half_a) if k < 4 else (ti, half_i)
                        b = k % 4
                        proj_ready(act, C["c_gates", k])
                        src = bank[pj.entries[C["c_gates", k]][0]]
                        act.activation(dst[:, 512 * b:512 * b + 256], src[:, 0:256], ACT.Tanh, bias=hb[:, 2 * b:2 * b + 1], scale=0.5)
                        act.activation(dst[:, 512 * b + 256:512 * b + 512], src[:, 256:512], ACT.Tanh,
                                       bias=hb[:, 2 * b + 1:2 * b + 2], scale=0.5).then_inc(S("proj_taken_act"), 1)
                        if k < 4:
                            act.wait_ge(S("proj_taken_act"), taken_after("act", C["c_gates", k]))
                            for i in (2 * b, 2 * b + 1):
                                act.activation(lr3[:, i, :], ta3[:, i, :], ACT.Exp, bias=n4sp[:, i:i + 1], scale=n4sp[:, i:i + 1])
                                last = act.activation(ta3[:, i, :], ta3[:, i, :], ACT.Tanh, bias=n2sp[:, i:i + 1], scale=n2sp[:, i:i + 1])
                            last.then_inc(S("lru_tanh"), 1)
                    gelu_tanh(0)
                    act.wait_ge(S("lru_denom"), 1)
                    log_exp_set()
                    after(act.activation(ta, ta, ACT.Ln, scale=-1.0))
                    act.activation(ta, ta, ACT.Exp, scale=0.5).then_inc(S("lru_sqrt"), 1)
                    exp_tanh_set()
                    for k in (1, 2, 3):
                        gelu_in(k)
                        gelu_tanh(k)
                    log_exp_set()
                post_norm([C["mix_out", L, k] for k in range(4)])
                pre_norm()
                for k in range(4):
                    take(C["xq", L, k], xq[:, 512 * k:512 * k + 512], src=lambda b: b[:])
                n0 = 8 + 4 * L
                att_softmax(n0, att_e[0], 1.0 / 16, True)
                for n in range(n0, n0 + 4):
                    if n < n0 + 3:
                        att_softmax(n + 1, att_e[(n + 1) % 2], 1.0 / 16, True)
                    take_probs(n, att_pt[n % 2])
                    act.wait_ge(S("att_out"), n + 1)
                    act.activation(xo[:, 512 * (n % 4):512 * (n % 4) + 512], bank[6][:], ACT.Copy).then_inc(S("att_out_taken"), 1)
                post_norm([C["xo", L, k] for k in range(4)])
                pre_norm()
                for k in range(FT // 2):
                    n = L * (FT // 2) + k
                    proj_ready(act, C["gate", L, k])
                    if k >= 2:
                        act.wait_ge(S("hidden_split"), n - 1)
                    act.activation(fth[k % 2], bank[pj.entries[C["gate", L, k]][0]][:], ACT.Tanh, scale=0.5)\
                       .then_inc(S("ffn_tanh"), 1)
                log_exp_set()
                post_norm([C["down", L, k] for k in range(4)])

            for n in range(4):
                j, half = n // 2, n % 2
                act.wait_ge(S("out_ready"), n + 1)
                act.activation(tiles(yT, 2)[:, j, 512 * half:512 * half + 512], bank[n][:], ACT.Copy).then_inc(S("out_rows"), 1)

        @block.vector
        def _(dve):
            steps = [0]

            def after(ins):
                steps[0] += 1
                ins.then_inc(S("dve_step"), 1)
                dve.wait_ge(S("dve_step"), steps[0])

            norms = [0]

            def norm_apply(src3, gain, layer_at, dst3, width):
                n = norms[0]
                for i in range(KT):
                    last = dve.scalar_tensor_tensor(out=dst3[:, i, :], in0=src3[:, i, :], scalar=vec(gain, layer_at + i),
                                                    in1=RSTD[:, 0:width], op0=ALU.mult, op1=ALU.mult)
                    last.then_inc(S("norm_out"), 1)
                return last

            def magnitude(dst, src):
                return dve.scalar_tensor_tensor(out=dst, in0=src, scalar=-1.0, in1=src, op0=ALU.mult, op1=ALU.max)

            def wait_rstd():
                norms[0] += 1
                dve.wait_ge(S("norm_rstd"), norms[0])

            ht3, u3 = tiles(hT[:], KT), tiles(uT, KT)
            dve.memset(eps, EPS).then_inc(S("eps_ready"), 1)
            dve.memset(zrow[0:8], 0.0).then_inc(S("zeros_ready"), 1)
            dve.wait_ge(S("logit_landed"), 16)
            magnitude(lgt[:, 0:8], lgt[:, 8:16]).then_inc(S("magnitudes"), 1)
            dve.wait_ge(S("log_terms"), 1)
            dve.scalar_tensor_tensor(out=lg, in0=lgt[:, 8:16], scalar=0.0, in1=lgt[:, 0:8], op0=ALU.min,
                                     op1=ALU.subtract).then_inc(S("lg_ready"), 1)
            for i in range(1, KT, 2):
                dve.wait_ge(S("xt_ready"), i + 1)
                dve.tensor_copy(ht3[:, i, :], bank[i % 4][:, 0:T]).then_inc(S("xt_taken_dve"), 1)
            dve.wait_ge(S("vec_ready"), 1)
            for j, n in enumerate(VEC_COUNT):
                last = dve.tensor_copy(VC[:, P * j:P * j + n], bank[4][:, P * j:P * j + n])
            after(last)
            qkp, qk = tiles(QKP, 8), tiles(QK, 8)
            dve.memset(qkp[:, :, 0:PAD], 0.0).then_inc(S("pads_ready"), 1)
            dve.memset(qkp[:, :, PAD + T:2 * PAD + T], 0.0).then_inc(S("pads_ready"), 1)
            dve.tensor_scalar(half_a, VC[:, 256:264], 0.5, None, ALU.mult)
            dve.tensor_scalar(half_i, VC[:, 264:272], 0.5, None, ALU.mult).then_inc(S("half_bias"), 1)
            lam = VC[:, P + VEC_AT["c_lam_2"][1]:P + VEC_AT["c_lam_2"][1] + 8]
            magnitude(lamt[:, 0:8], lam).then_inc(S("magnitudes"), 1)
            wait_rstd()
            norm_apply(ht3, "mix_norm_g", 0, u3, T)

            dve.wait_ge(S("gates_ready"), 2)
            dve.wait_ge(S("bias_landed"), 64)
            dve.tensor_scalar(li[0:8], bank[4][0:8, 0:T], b_i, None, ALU.add).then_inc(S("gates_taken"), 1)
            dve.tensor_scalar(lf[0:8], bank[5][0:8, 0:T], b_f, None, ALU.add).then_inc(S("gates_taken"), 1)
            dve.wait_ge(S("gates_taken"), 2)
            magnitude(rowt[0:8], lf[0:8]).then_inc(S("magnitudes"), 1)
            dve.wait_ge(S("log_terms"), 2)
            dve.wait_ge(S("zeros_ready"), 1)
            after(dve.scalar_tensor_tensor(out=lf[0:8], in0=lf[0:8], scalar=0.0, in1=rowt[0:8], op0=ALU.min, op1=ALU.subtract))
            dve.tensor_tensor_scan(Bf[0:8], lf[0:8], zrow[0:8], 0.0, ALU.add, ALU.add)
            after(dve.tensor_tensor_scan(Bb[0:8, ::-1], lf[0:8, ::-1], zrow[0:8], 0.0, ALU.add, ALU.add))
            dve.wait_ge(S("tables_landed"), 7 * 16)
            after(dve.tensor_scalar(Bf[0:8], Bf[0:8], dirs[:, 0:1], None, ALU.mult))
            after(dve.scalar_tensor_tensor(out=Bf[0:8], in0=Bb[0:8], scalar=dirs[:, 1:2], in1=Bf[0:8], op0=ALU.mult, op1=ALU.add))
            dve.tensor_tensor(Bb[0:8], li[0:8], Bf[0:8], ALU.subtract).then_inc(S("gate_rows_ready"), 1)
            dve.wait_ge(S("gate_rows_ready"), 1)
            dve.tensor_tensor_scan(sf[0:8], Bb[0:8], Bb[0:8], 0.0, ALU.max, ALU.max)
            after(dve.tensor_tensor_scan(li[0:8, ::-1], Bb[0:8, ::-1], Bb[0:8, ::-1], 0.0, ALU.max, ALU.max))
            after(dve.tensor_scalar(sf[0:8], sf[0:8], dirs[:, 0:1], None, ALU.mult))
            after(dve.scalar_tensor_tensor(out=sf[0:8], in0=li[0:8], scalar=dirs[:, 1:2], in1=sf[0:8], op0=ALU.mult, op1=ALU.add))
            dve.tensor_tensor(Mr[0:8], Bf[0:8], sf[0:8], ALU.add).then_inc(S("stab_ready"), 1)

            sq8 = tiles(SQ[:], 8)

            def silu(i):
                dve.wait_ge(S("conv_tanh"), i + 1)
                dve.scalar_tensor_tensor(out=qk[:, i, :], in0=sq8[:, i, :], scalar=1.0, in1=qk[:, i, :], op0=ALU.add,
                                         op1=ALU.mult).then_inc(S("qk_ready"), 1)

            for i in range(8):
                dve.wait_ge(S("proj_taken_act"), i + 1)
                after(dve.tensor_scalar(qk[:, i, :], qkp[:, i, 0:T], vec("conv_w", i), vec("conv_b", i), ALU.mult, ALU.add))
                for tap in range(1, 5):
                    ins = dve.scalar_tensor_tensor(out=qk[:, i, :], in0=qkp[:, i, tap:tap + T], scalar=vec("conv_w", 8 * tap + i),
                                                   in1=qk[:, i, :], op0=ALU.mult, op1=ALU.add)
                    if tap < 4:
                        after(ins)
                ins.then_inc(S("conv_ready"), 1)
                if i:
                    silu(i - 1)
            silu(7)

            dve.wait_ge(S("log_terms"), 3)
            after(dve.scalar_tensor_tensor(out=n2sp, in0=lam, scalar=0.0, in1=lamt[:, 0:8], op0=ALU.min, op1=ALU.subtract))
            after(dve.tensor_scalar(n2sp, n2sp, 2.0, None, ALU.mult))
            dve.tensor_scalar(n4sp, n2sp, 2.0, None, ALU.mult).then_inc(S("lru_rate"), 1)

            def unit_args(n):
                h, d = n // 2, n % 2
                r = 4 * d + h
                pt = tiles(SQ[:, (n % 2) * 816:(n % 2 + 1) * 816], TT)
                dve.wait_ge(S("stab_bcast"), n + 1)
                if n >= 2:
                    dve.wait_ge(S("num_ready"), n - 1)
                for j in range(TT):
                    if d == 0:
                        lo, hi = P * j, T
                        bar = bar_fwd[0:ROWS[j], 0:T - P * j]
                    else:
                        lo, hi = 0, min(T, P * (j + 1))
                        bar = bar_bwd[0:ROWS[j], 256 - P * j:256 - P * j + hi]
                    last = dve.scalar_tensor_tensor(out=pt[0:ROWS[j], j, lo:hi], in0=bank[7][0:ROWS[j], lo:hi],
                                                    scalar=acol[0:ROWS[j], 8 * j + r:8 * j + r + 1], in1=bar,
                                                    op0=ALU.subtract, op1=ALU.max)
                last.then_inc(S("args_ready"), 1)

            def unit_probs(n):
                h, d = n // 2, n % 2
                pt = tiles(SQ[:, (n % 2) * 816:(n % 2 + 1) * 816], TT)
                dve.wait_ge(S("unit_exps"), n + 1)
                dve.wait_ge(S("m_scores"), h + 1)
                for j in range(TT):
                    lo, hi = (P * j, T) if d == 0 else (0, min(T, P * (j + 1)))
                    v = pt[0:ROWS[j], j, lo:hi]
                    last = dve.scalar_tensor_tensor(out=v, in0=v, scalar=MLSTM_C, in1=bank[4 + j][0:ROWS[j], lo:hi],
                                                    op0=ALU.mult, op1=ALU.mult)
                last.then_inc(S("m_probs"), 1)

            dve.wait_ge(S("rotary_landed"), 48)
            dve.wait_ge(S("qk_ready"), 8)
            for n in range(8):
                src = tiles(rqT if n < H else rkT, H)[:, n % H, :]
                tmp = SQ[:, (n % 2) * T:(n % 2 + 1) * T]
                dve.wait_ge(S("rotary_ready"), n + 1)
                dve.tensor_tensor(tmp, bank[7][:, 0:T], sinT, ALU.mult).then_inc(S("rotary_taken"), 1)
                after(dve.tensor_tensor(src, src, cosT, ALU.mult))
                dve.wait_ge(S("rotary_taken"), n + 1)
                dve.tensor_tensor(src, src, tmp, ALU.add).then_inc(S("rot_out"), 1)

            dve.wait_ge(S("acol_ready"), 1)
            for j in range(TT):
                last = dve.tensor_copy(acol[0:ROWS[j], 8 * j:8 * j + 8], bank[3][0:ROWS[j], 8 * j:8 * j + 8])
            last.then_inc(S("acol_taken"), 1)
            dve.wait_ge(S("acol_taken"), 1)

            dve.wait_ge(S("rot_out"), 8)
            unit_args(0)
            for n in range(8):
                if n < 7:
                    unit_args(n + 1)
                unit_probs(n)
            dve.wait_ge(S("floor_ready"), 1)
            dve.wait_ge(S("num_ready"), 8)
            after(dve.tensor_copy(li[0:8], bank[3][0:8, 0:T]))
            after(magnitude(rowt[0:8], li[0:8]))
            after(dve.tensor_tensor(rowt[0:8], rowt[0:8], Mr[0:8], ALU.max))
            after(dve.reciprocal(rowt[0:8], rowt[0:8]))
            dve.tensor_scalar(rowt[0:8], rowt[0:8], 0.5, None, ALU.mult).then_inc(S("recip_ready"), 1)
            num3 = tiles(NUM, 8)
            dve.wait_ge(S("num_taken"), 8)
            for r in range(8):
                dve.wait_ge(S("recip_bcast"), r + 1)
                dve.tensor_tensor(num3[:, r, :], num3[:, r, :], bank[2 + r % 2][:, 0:T], ALU.mult).then_inc(S("recip_taken"), 1)
            dve.wait_ge(S("recip_taken"), 8)
            after(dve.tensor_tensor(HM, NUM[:, 0:H * T], NUM[:, H * T:], ALU.add))
            dve.wait_ge(S("proj_taken_act"), 28)
            dve.scalar_tensor_tensor(out=HM, in0=moT, scalar=1.0, in1=HM, op0=ALU.add, op1=ALU.mult).then_inc(S("hm_ready"), 1)

            dec = DEC.rearrange("p (h i l) -> p h i l", h=H, i=TT)
            dve.wait_ge(S("decay_ready"), H * TT)

            def head_centre(src, first_bank, n):
                s3 = tiles(src, H)
                dve.wait_ge(S("hn_mean"), n + 1)
                for h in range(H):
                    last = dve.scalar_tensor_tensor(out=s3[:, h, :], in0=bank[first_bank + h][:, 0:T], scalar=-1.0 / P, in1=s3[:, h, :],
                                                    op0=ALU.mult, op1=ALU.add)
                last.then_inc(S("hn_centred"), 1)

            def head_apply(src, rstd, n, gain, out_tile):
                s3, rs = tiles(src, H), tiles(rstd, H)
                dve.wait_ge(S("hn_rstd"), n + 1)
                for h in range(H):
                    last = dve.scalar_tensor_tensor(out=u3[:, out_tile + h, :], in0=s3[:, h, :], scalar=vec(gain, h), in1=rs[:, h, :],
                                                    op0=ALU.mult, op1=ALU.mult)
                return last

            for h in range(H):
                dve.wait_ge(S("r_scores"), h + 1)
                if h >= 2:
                    dve.wait_ge(S("ret_ready"), h - 1)
                pt = tiles(SQ[:, (h % 2) * 816:(h % 2 + 1) * 816], TT)
                for j in range(TT):
                    last = dve.tensor_tensor(pt[0:ROWS[j], j, :], dec[0:ROWS[j], h, j, :], bank[4 + j][0:ROWS[j], 0:T], ALU.mult)
                last.then_inc(S("r_probs"), 1)
                if h == 0:
                    head_centre(HM, 0, 0)
            head_apply(HM, hm_rstd, 0, "mlstm_gn_g", H).then_inc(S("y_ready"), 1)
            dve.wait_ge(S("rg_tanh"), 1)
            after(dve.scalar_tensor_tensor(out=rgT, in0=QK[:, 0:H * T], scalar=1.0, in1=rgT, op0=ALU.add, op1=ALU.mult))
            head_centre(RET, 4, 1)
            rg3, ret3, rs3 = tiles(rgT, H), tiles(RET, H), tiles(ret_rstd, H)
            dve.wait_ge(S("hn_rstd"), 2)
            for h in range(H + 1):
                if h < H:
                    dve.scalar_tensor_tensor(out=u3[:, h, :], in0=ret3[:, h, :], scalar=vec("ret_gn_g", h), in1=rs3[:, h, :],
                                             op0=ALU.mult, op1=ALU.mult).then_inc(S("ret_scaled"), 1)
                if h:
                    dve.wait_ge(S("ret_scaled"), h)
                    dve.scalar_tensor_tensor(out=u3[:, h - 1, :], in0=u3[:, h - 1, :], scalar=0.5, in1=rg3[:, h - 1, :],
                                             op0=ALU.mult, op1=ALU.mult).then_inc(S("y_ready"), 1)

            for i in range(KT):
                k = A_OUT[i]
                proj_ready(dve, k)
                dve.tensor_tensor(ht3[:, i, :], ht3[:, i, :], bank[pj.entries[k][0]][:, 0:T], ALU.add)\
                   .then_inc(S("proj_taken_dve"), 1)

            wait_rstd()
            norm_apply(ht3, "ffn_norm_g", 0, tiles(u2, KT), T)
            dve.wait_ge(S("router_ready"), 1)
            dve.tensor_copy(logitsT[0:EXP], bank[4][0:EXP, 0:T]).then_inc(S("logits_taken"), 1)
            dve.wait_ge(S("router_ready"), 2)
            b3 = bank[4][:, 0:TT * EXP].rearrange("p (j e) -> p j e", j=TT)
            dve.tensor_reduce(smax[:, 0:2], b3[:, 0:2, :], AX.X, ALU.max, negate=True).then_inc(S("router_max"), 1)
            dve.tensor_reduce(smax[0:ROWS[2], 2:3], b3[0:ROWS[2], 2:3, :], AX.X, ALU.max, negate=True).then_inc(S("router_max"), 1)
            dve.wait_ge(S("router_exps"), TT)
            dve.reciprocal(ssum[:, 0:2], ssum[:, 0:2])
            after(dve.reciprocal(ssum[0:ROWS[2], 2:3], ssum[0:ROWS[2], 2:3]))
            a3 = tiles(aff, TT)
            for j in range(TT):
                last = dve.tensor_scalar(a3[0:ROWS[j], j, :], a3[0:ROWS[j], j, :], ssum[0:ROWS[j], j:j + 1], None, ALU.mult)
            last.then_inc(S("aff_ready"), 1)
            dve.wait_ge(S("affT_ready"), 1)
            after(dve.tensor_copy(affW[0:EXP], bank[5][0:EXP, 0:T]))
            ids = idxs.bitcast(U32)
            for r in range(5):
                c8 = slice(8 * r, 8 * r + 8)
                after(dve.max(vals[0:EXP, c8], affW[0:EXP]))
                after(dve.max_index(ids[0:EXP, c8], vals[0:EXP, c8], affW[0:EXP]))
                after(dve.match_replace(affW[0:EXP], vals[0:EXP, c8], affW[0:EXP], -1.0))
            dve.memset(idx2[0:EXP], 0.0)
            after(dve.memset(val2[0:EXP], 0.0))
            for at in (0, MPAD):
                dve.tensor_copy(idx2[0:EXP, at:at + CAP], ids[0:EXP, 0:CAP])
                last = dve.tensor_copy(val2[0:EXP, at:at + CAP], vals[0:EXP, 0:CAP])
            after(last)
            dve.wait_ge(S("own_landed"), 16)
            dve.memset(xs, 0.0).then_inc(S("xs_pads"), 1)
            own3, sp3 = tiles(own, EXP), tiles(spread, EXP)
            dve.tensor_tensor(sp3[0:EXP], own3[0:EXP], idx2[0:EXP, 0:CAP].rearrange("p (a c) -> p a c", a=1).to_broadcast([EXP, EXP, CAP]),
                              ALU.mult).then_inc(S("spread_ready"), 1)
            dve.wait_ge(S("choice_ready"), 1)
            dve.tensor_copy(idxT, bank[4][:, 0:EXP])
            after(dve.tensor_copy(gT, bank[4][:, EXP:2 * EXP]))
            st3 = ST.rearrange("p (j s) -> p j s", j=TT)
            ste3 = tiles(STe, TT)
            for j in range(TT):
                last = dve.tensor_scalar(ste3[:, j, :], bank[5][:, 0:CAP], iota_col[:, j:j + 1], None, ALU.is_equal)
            last.then_inc(S("ste_ready"), 1)
            for b in (1, 0):
                for j in range(TT):
                    dve.tensor_scalar(st3[:, j, 272 * b:272 * b + 272], bank[5 + b][:, 0:272], iota_col[:, j:j + 1], None, ALU.is_equal)\
                       .then_inc(S("gather_ready"), 1)
            dve.memset(st3[:, :, EXP * CAP:], 0.0).then_inc(S("gather_ready"), 1)
            wait_rstd()
            m3 = tiles(mT, KT)
            for L in range(2):
                norm_apply(m3, "g_mem_2", 8 * L, tiles(mm[:, 2048 * L:2048 * L + 2048], KT), 256)

            dve.wait_ge(S("norm_sum"), 3)
            dve.wait_ge(S("iota_landed"), 16)
            dve.memset(Se, 0.0).then_inc(S("se_ready"), 1)

            def scatter_add(e):
                for i in range(KT):
                    dve.wait_ge(S("scatter_ready"), 8 * e + i + 1)
                    dve.tensor_tensor(ht3[:, i, :], ht3[:, i, :], bank[7][:, 0:T], ALU.add)\
                       .then_inc(S("scatter_taken"), 1)

            with dve.Fori(0, EXP) as e:
                for c, (lo, hi) in enumerate(HCHUNKS):
                    v = th[:, HF * lo:HF * hi]
                    dve.wait_ge(S("gate_tanh"), 3 * e + c + 1)
                    dve.scalar_tensor_tensor(out=v, in0=v, scalar=1.0, in1=bank[c][:, 0:HF * (hi - lo)], op0=ALU.add, op1=ALU.mult)\
                       .then_inc(S("gu_ready"), 1)
                scatter_add(e)
                dve.tensor_scalar(Se, iota_row, idxT[:, bass.ds(e, 1)], gT[:, bass.ds(e, 1)], ALU.is_equal, ALU.mult)\
                   .then_inc(S("se_ready"), 1)
                dve.wait_ge(S("up_used"), 8 * e + 8)
                dve.wait_ge(S("gu_ready"), 3 * e + 3)
                for c, (lo, hi) in enumerate(HCHUNKS):
                    v = th[:, HF * lo:HF * hi]
                    dve.scalar_tensor_tensor(out=v, in0=v, scalar=0.5, in1=bank[3 + c][:, 0:HF * (hi - lo)], op0=ALU.mult, op1=ALU.mult)\
                       .then_inc(S("hid_ready"), 1)
            scatter_add(EXP)

            x3, hn3, y3 = tiles(xT, KT), tiles(hN, KT), tiles(yT, KT)
            wait_rstd()
            norm_apply(ht3[:, :, META:T], "final_norm_g", 0, x3, 256)

            def pre_norm(gain, L):
                wait_rstd()
                norm_apply(x3, gain, 8 * L, hn3, 256)

            scaled = [0]

            def post_norm(gain, L):
                wait_rstd()
                for i in range(KT + 1):
                    if i < KT:
                        scaled[0] += 1
                        dve.scalar_tensor_tensor(out=hn3[:, i, :], in0=hn3[:, i, :], scalar=vec(gain, 8 * L + i),
                                                 in1=RSTD[:, 0:256], op0=ALU.mult, op1=ALU.mult).then_inc(S("post_scaled"), 1)
                    if i:
                        dve.wait_ge(S("post_scaled"), scaled[0] - (i < KT))
                        dve.tensor_tensor(x3[:, i - 1, :], x3[:, i - 1, :], hn3[:, i - 1, :], ALU.add).then_inc(S("norm_out"), 1)

            def att_normalise(n, buf):
                s = slice(2 * (n % 2), 2 * (n % 2) + 2)
                dve.wait_ge(S("att_exps"), 2 * n + 2)
                after(dve.reciprocal(ssum[:, s], ssum[:, s]))
                for qi in range(2):
                    v = buf[:, 256 * qi:256 * qi + 256]
                    last = dve.tensor_scalar(v, v, ssum[:, 2 * (n % 2) + qi:2 * (n % 2) + qi + 1], None, ALU.mult)
                last.then_inc(S("att_probs"), 1)

            splits = [0]

            def split_weights_to(end):
                while splits[0] < len(split_chunks) and split_chunks[splits[0]] < end:
                    n = splits[0]
                    k = split_chunks[n]
                    chunk_landed(dve, C_CHUNKS[k])
                    if n >= PSLOTS:
                        dve.wait_ge(*chunk_used[split_chunks[n - PSLOTS]])
                    dve.tensor_copy(part(highs, n), raw_slot(k)).then_inc(S("weights_high"), 1)
                    dve.wait_ge(S("weights_high"), n + 1)
                    cols = slice(256 * POOL_TILES, SLOT)
                    dve.tensor_tensor(part(lows, n)[:, cols], raw_slot(k)[:, cols], part(highs, n)[:, cols], ALU.subtract)\
                       .then_inc(S("weights_low_dve"), 1)
                    splits[0] += 1

            def split_part(src, x_low, c, last=False):
                after(dve.tensor_copy(x_high[:, c], src[:, c]))
                ins = dve.tensor_tensor(x_low[:, c], src[:, c], x_high[:, c], ALU.subtract)
                if last:
                    ins.then_inc(S("input_split"), 1)

            def split_normed(x_low, norms_before):
                dve.wait_ge(S("norm_out"), 40 + 8 * (norms_before + 1))
                split_part(hN, x_low, slice(0, SLOT), True)

            for L in range(2):
                mix_at = c_index["ab_out" if L == 0 else "c_out", 0]
                pre_norm("g_mix_pre_2", L)
                split_normed(x_low_pre, 6 * L)
                split_weights_to(c_index["ab", 2] if L == 0 else c_index["c_in", 0])
                if L == 0:
                    dve.wait_ge(S("fox_logits"), 1)
                    after(dve.tensor_scalar(frow[0:8], bank[6][0:8, 0:256], b_fox, None, ALU.add))
                    magnitude(frow2[0:8], frow[0:8]).then_inc(S("magnitudes"), 1)
                    dve.memset(frow3[0:8], 0.0)
                    dve.wait_ge(S("log_terms"), 4)
                    after(dve.scalar_tensor_tensor(out=frow2[0:8], in0=frow[0:8], scalar=0.0, in1=frow2[0:8], op0=ALU.min,
                                                   op1=ALU.subtract))
                    dve.tensor_tensor_scan(frow[0:8], frow2[0:8], frow3[0:8], 0.0, ALU.add, ALU.add).then_inc(S("fox_row_ready"), 1)
                    bar3 = tiles(fox_bar, 2)
                    nm3 = tiles(fox_nm, 2)
                    dve.wait_ge(S("fox_tables"), 32)

                    def fox_args(n):
                        dve.wait_ge(S("att_scores"), n + 1)
                        if n >= 2:
                            dve.wait_ge(S("pt_ready"), n - 1)
                        cum = bank[6][:, 0:256].rearrange("p (a c) -> p a c", a=1).to_broadcast([P, 2, 256])
                        after(dve.tensor_tensor(nm3, bar3, cum, ALU.subtract))
                        ins = dve.scalar_tensor_tensor(out=fox_e[n % 2], in0=bank[5][:], scalar=0.125, in1=fox_nm, op0=ALU.mult, op1=ALU.add)
                        ins.then_inc(S("att_scores_taken"), 1)
                        dve.wait_ge(S("att_scores_taken"), n + 1)
                        dve.tensor_reduce(smax[:, 2 * (n % 2):2 * (n % 2) + 2], tiles(fox_e[n % 2], 2), AX.X, ALU.max, negate=True)\
                           .then_inc(S("att_max"), 1)

                    cu3, fu3, fb3, fc3 = (tiles(x, 4) for x in (cu, fu, fb, fc))
                    dve.memset(cu3[:, :, 0:2], 0.0)

                    def short_convolution(t):
                        dve.wait_ge(S("proj_taken_act"), taken_after("act", C["ab", 10 + t // 2]))
                        two = slice(t, t + 2)
                        after(dve.tensor_tensor(cu3[:, two, 2:258], fc3[:, two], fu3[:, two], ALU.mult))
                        for i in (t, t + 1):
                            ins = dve.tensor_scalar(fu3[:, i, :], cu3[:, i, 0:256], vec("ab_conv_w_2", i), None, ALU.mult)
                        after(ins)
                        for tap in (1, 2):
                            for i in (t, t + 1):
                                ins = dve.scalar_tensor_tensor(out=fu3[:, i, :], in0=cu3[:, i, tap:tap + 256],
                                                               scalar=vec("ab_conv_w_2", 4 * tap + i), in1=fu3[:, i, :],
                                                               op0=ALU.mult, op1=ALU.add)
                            after(ins)
                        c = slice(1024 + 256 * t, 1024 + 256 * t + 512)
                        after(dve.tensor_tensor(yT[:, c], fu[:, 256 * t:256 * t + 512], fb[:, 256 * t:256 * t + 512], ALU.mult))
                        after(dve.tensor_copy(x_high[:, c], yT[:, c]))

                    split_weights_to(c_index["ab", 6])
                    fox_args(0)
                    for n in range(8):
                        if n < 7:
                            fox_args(n + 1)
                        att_normalise(n, fox_e[n % 2])
                        if n in (4, 5, 6):
                            split_weights_to(mix_at + n - 3)
                        if n in (5, 6):
                            short_convolution(2 * (n - 5))
                    c = slice(1024, 2048)
                    dve.wait_ge(S("att_scores"), 8)
                    dve.tensor_tensor(x_low_out[:, c], yT[:, c], x_high[:, c], ALU.subtract)
                    for i in range(4):
                        dve.wait_ge(S("att_out_taken"), i + 1)
                        split_part(yT, x_low_out, slice(256 * i, 256 * i + 256), i == 3)
                else:
                    lup3, lu3, lg3 = tiles(lup, KT), tiles(lu, KT), tiles(lgate, KT)
                    ta3, ti3, lr3, sq3 = tiles(ta, KT), tiles(ti, KT), tiles(lr, KT), tiles(SQ[:, 0:2048], KT)
                    dve.memset(lup3[:, :, 0:3], 0.0).then_inc(S("lru_pads"), 1)
                    for k in range(4):
                        dve.wait_ge(S("proj_taken_act"), taken_after("act", C["c_in", k]))
                        for i in (2 * k, 2 * k + 1):
                            after(dve.tensor_scalar(lu3[:, i, :], lup3[:, i, 0:256], vec("c_conv_w_2", i), vec("c_conv_b_2", i),
                                                    ALU.mult, ALU.add))
                            for tap in (1, 2, 3):
                                ins = dve.scalar_tensor_tensor(out=lu3[:, i, :], in0=lup3[:, i, tap:tap + 256],
                                                               scalar=vec("c_conv_w_2", 8 * tap + i), in1=lu3[:, i, :],
                                                               op0=ALU.mult, op1=ALU.add)
                                if tap < 3:
                                    after(ins)
                            ins.then_inc(S("lru_conv"), 1)
                        if k == 1:
                            split_weights_to(c_index["c_in", 0] + 1)

                    def gelu_cubic(k):
                        v, x = SQ[:, 512 * k:512 * k + 512], lgate[:, 512 * k:512 * k + 512]
                        dve.wait_ge(S("gelu_square"), k + 1)
                        after(dve.tensor_scalar(v, v, 0.044715, 1.0, ALU.mult, ALU.add))
                        dve.wait_ge(S("proj_taken_act"), taken_after("act", C["c_in", 4 + k]))
                        dve.tensor_tensor(v, v, x, ALU.mult).then_inc(S("gelu_cubic"), 1)

                    def gelu_out(k):
                        c = slice(512 * k, 512 * k + 512)
                        dve.wait_ge(S("gelu_tanh"), k + 1)
                        after(dve.scalar_tensor_tensor(out=SQ[:, c], in0=SQ[:, c], scalar=1.0, in1=lgate[:, c], op0=ALU.add, op1=ALU.mult))
                        after(dve.scalar_tensor_tensor(out=yT[:, c], in0=SQ[:, c], scalar=0.5, in1=lu[:, c], op0=ALU.mult, op1=ALU.mult))
                        split_part(yT, x_low_out, c, k == 3)

                    gelu_cubic(0)
                    dve.wait_ge(S("lru_tanh"), 4)
                    dve.tensor_scalar(ta, ta, -1e-30, None, ALU.min).then_inc(S("lru_denom"), 1)
                    dve.wait_ge(S("proj_taken_act"), taken_after("act", C["c_gates", 7]))
                    after(dve.scalar_tensor_tensor(out=ti, in0=ti, scalar=1.0, in1=lu, op0=ALU.add, op1=ALU.mult))
                    after(dve.scalar_tensor_tensor(out=ti, in0=lr, scalar=1.0, in1=ti, op0=ALU.add, op1=ALU.mult))
                    split_weights_to(mix_at + 1)
                    dve.wait_ge(S("lru_sqrt"), 1)
                    after(dve.scalar_tensor_tensor(out=ti, in0=ti, scalar=0.5, in1=ta, op0=ALU.mult, op1=ALU.mult))
                    gelu_cubic(1)
                    for i in range(KT):
                        last = dve.tensor_tensor_scan(lu3[:, i, :], lr3[:, i, :], ti3[:, i, :], 0.0, ALU.mult, ALU.add)
                    after(last)
                    gelu_out(0)
                    gelu_cubic(2)
                    gelu_out(1)
                    gelu_out(2)
                    gelu_cubic(3)
                    gelu_out(3)
                split_weights_to(mix_at + 7)
                post_norm("g_mix_post_2", L)
                pre_norm("g_cross_pre_2", L)
                split_normed(x_low_pre, 6 * L + 2)
                split_weights_to(mix_at + 10)
                n0 = 8 + 4 * L

                def cross_max(n):
                    dve.wait_ge(S("att_scores"), n + 1)
                    s = slice(2 * (n % 2), 2 * (n % 2) + 2)
                    if n > n0:
                        dve.wait_ge(S("att_exps"), 2 * n - 2)
                    after(dve.tensor_reduce(smax[:, s], tiles(bank[4 + n % 2][:], 2), AX.X, ALU.max, negate=True))
                    dve.tensor_scalar(smax[:, s], smax[:, s], 1.0 / 16, None, ALU.mult).then_inc(S("att_max"), 1)

                def split_head(n):
                    dve.wait_ge(S("att_out_taken"), 4 + 4 * L + n - n0 + 1)
                    split_part(xo, x_low_out, slice(512 * (n - n0), 512 * (n - n0) + 512), n == n0 + 3)

                cross_max(n0)
                for n in range(n0, n0 + 4):
                    if n < n0 + 3:
                        cross_max(n + 1)
                    att_normalise(n, att_e[n % 2])
                    if n == n0:
                        split_weights_to(mix_at + 11)
                    else:
                        split_head(n - 1)
                split_head(n0 + 3)
                ffn_at = c_index[f"gate{L}", 0]
                split_weights_to(ffn_at + 3)
                post_norm("g_cross_post_2", L)
                pre_norm("g_ffn_pre_2", L)
                split_normed(x_low_ffn, 6 * L + 4)
                split_weights_to(ffn_at + 4)
                for k in range(FT // 2):
                    n = L * (FT // 2) + k
                    dve.wait_ge(S("ffn_tanh"), n + 1)
                    kg, ku = C["gate", L, k], C["up", L, k]
                    dve.scalar_tensor_tensor(out=fth[k % 2], in0=fth[k % 2], scalar=1.0, in1=bank[pj.entries[kg][0]][:],
                                             op0=ALU.add, op1=ALU.mult).then_inc(S("proj_taken_dve"), 1)
                    dve.wait_ge(S("proj_taken_dve"), taken_after("dve", kg))
                    proj_ready(dve, ku)
                    hid_k = fth[k % 2]
                    dve.scalar_tensor_tensor(out=hid_k, in0=hid_k, scalar=0.5, in1=bank[pj.entries[ku][0]][:],
                                             op0=ALU.mult, op1=ALU.mult).then_inc(S("proj_taken_dve"), 1)
                    dve.wait_ge(S("proj_taken_dve"), taken_after("dve", ku))
                    low, high = (x[:, 512 * k:512 * k + 512] for x in (fhid_low, fhid_high))
                    after(dve.tensor_copy(high, hid_k))
                    dve.tensor_tensor(low, hid_k, high, ALU.subtract).then_inc(S("hidden_split"), 1)
                    split_weights_to(ffn_at + 6 + 2 * k)
                split_weights_to(ffn_at + FT + FT // 2 + 3)
                post_norm("g_ffn_post_2", L)


_INS = ["x", "meta_tokens", "mix_norm_g", "w_in", "b_gates", "conv_w", "conv_b", "ret_decay_logit", "ret_gn_g",
        "mlstm_gn_g", "w_out", "ffn_norm_g", "w_router", "w_gate", "w_up", "w_down", "final_norm_g", "mem_2",
        "g_mix_pre_2", "g_mix_post_2", "g_cross_pre_2", "g_mem_2", "g_cross_post_2", "g_ffn_pre_2",
        "g_ffn_post_2", "w_xq_2", "w_xkv_2", "w_xo_2", "w_ffn_gu_2", "w_ffn_down_2", "ab_w_in_2", "ab_b_f_2",
        "ab_conv_w_2", "ab_w_out_2", "c_w_in_2", "c_conv_w_2", "c_conv_b_2", "c_w_a_2", "c_b_a_2", "c_w_i_2",
        "c_b_i_2", "c_lam_2", "c_w_out_2"]


def kernel(**inputs):
    import concourse.bacc as _bacc
    from concourse.bass_utils import run_bass_kernel_spmd as _run

    nc = _bacc.Bacc("TRN2", target_bir_lowering=False, num_devices=1)
    arrays, tensors = {}, {}
    for name, a in [(n, inputs[n]) for n in _INS] + list(constants().items()):
        a = np.ascontiguousarray(a)
        arrays[f"in_{name}_dram"] = a
        tensors[name] = nc.dram_tensor(f"in_{name}_dram", a.shape, mybir.dt.from_np(a.dtype), kind="ExternalInput").ap()
    out = nc.dram_tensor("out_0_dram", (1, SEQ, D), F32, kind="ExternalOutput").ap()
    build(nc, tensors, out)
    r = _run(nc, [arrays], core_ids=[0])
    return r.results[0]["out_0_dram"]
```
